# Optimizing a Trainium2 kernel written in Bass

```python
import math
import jax, jax.numpy as jnp
from jax import lax
import numpy as np

D_MODEL = 1024
BATCH = 1
SEQ = 256
DEPTH = 1

CHUNK = 64
Q_BLOCK = 128
EPS = 1e-6

FOX_HEADS = 8
FOX_HEAD_DIM = 64
FOX_WIDTH = FOX_HEADS * FOX_HEAD_DIM
GDN_HEADS = 4
GDN_HEAD_DIM = 128
GDN_WIDTH = GDN_HEADS * GDN_HEAD_DIM
CONV_WIDTH = 4
MIX_WIDTH = FOX_WIDTH + GDN_WIDTH

IN_SPLITS = (FOX_WIDTH, FOX_WIDTH, FOX_WIDTH, FOX_HEADS,
             GDN_WIDTH, GDN_WIDTH, GDN_WIDTH,
             GDN_HEADS, GDN_HEADS, GDN_WIDTH)
IN_WIDTH = 3 * FOX_WIDTH + FOX_HEADS + 4 * GDN_WIDTH + 2 * GDN_HEADS

MEM_LEN = 256
XA_HEADS = 4
XA_HEAD_DIM = D_MODEL // XA_HEADS

N_EXPERTS = 32
TOP_K = 4
D_EXPERT = D_MODEL
SWIGLU_LIMIT = 7.0
SWIGLU_ALPHA = 1.702

kernel_name = "hybrid_fox_gdn_xattn_moe_block"

def rms_norm(x, gain):
    xf = x.astype(jnp.float32)
    y = xf * lax.rsqrt(jnp.mean(xf * xf, axis=-1, keepdims=True) + EPS)
    return (y * gain.astype(jnp.float32)).astype(x.dtype)

def l2_norm(x):
    xf = x.astype(jnp.float32)
    return xf * lax.rsqrt(jnp.sum(xf * xf, axis=-1, keepdims=True) + EPS)

def forgetting_attention(q, k, v, log_f):
    B, H, T, Dh = q.shape
    cum = jnp.cumsum(log_f, axis=-1)
    scale = Dh ** -0.5
    nb = T // Q_BLOCK
    qb = jnp.moveaxis(q.reshape(B, H, nb, Q_BLOCK, Dh), 2, 0)
    cb = jnp.moveaxis(cum.reshape(B, H, nb, Q_BLOCK), 2, 0)
    pos_k = jnp.arange(T)

    def one_block(args):
        i, q_blk, c_blk = args
        pos_q = i * Q_BLOCK + jnp.arange(Q_BLOCK)
        s = jnp.einsum('bhqd,bhkd->bhqk', q_blk, k).astype(jnp.float32) * scale
        s = s + (c_blk[..., :, None] - cum[..., None, :])
        s = jnp.where(pos_k[None, :] <= pos_q[:, None], s, -jnp.inf)
        p = jax.nn.softmax(s, axis=-1)
        return jnp.einsum('bhqk,bhkd->bhqd', p.astype(v.dtype), v)

    out = lax.map(one_block, (jnp.arange(nb), qb, cb))
    return jnp.moveaxis(out, 0, 2).reshape(B, H, T, Dh)

def causal_depthwise_conv(x, w):
    K = w.shape[-1]
    rhs = jnp.transpose(w)[:, None, :].astype(x.dtype)
    return lax.conv_general_dilated(x, rhs, window_strides=(1,), padding=[(K - 1, 0)],
                                    dimension_numbers=('NWC', 'WIO', 'NWC'),
                                    feature_group_count=x.shape[-1])

def gated_delta_rule(q, k, v, g, beta):
    B, H, T, Dk = q.shape
    Dv = v.shape[-1]
    n = T // CHUNK
    q = q.reshape(B, H, n, CHUNK, Dk)
    k = k.reshape(B, H, n, CHUNK, Dk)
    v = v.reshape(B, H, n, CHUNK, Dv)
    g = g.reshape(B, H, n, CHUNK)
    beta = beta.reshape(B, H, n, CHUNK)
    G = jnp.cumsum(g, axis=-1)
    idx = jnp.arange(CHUNK)
    lower_incl = idx[:, None] >= idx[None, :]
    strict = idx[:, None] > idx[None, :]
    decay = jnp.exp(jnp.where(lower_incl, G[..., :, None] - G[..., None, :], -jnp.inf))
    A = jnp.where(strict, beta[..., :, None] * jnp.einsum('bhncd,bhnsd->bhncs', k, k) * decay, 0.0)
    eye = jnp.eye(CHUNK, dtype=jnp.float32)
    T_inv = lax.linalg.triangular_solve(A + eye, jnp.broadcast_to(eye, A.shape),
                                        left_side=True, lower=True)
    u = T_inv @ (v * beta[..., None])
    w = T_inv @ (k * (beta * jnp.exp(G))[..., None])
    qk = jnp.where(lower_incl, jnp.einsum('bhncd,bhnsd->bhncs', q, k) * decay, 0.0)
    q_dec = q * jnp.exp(G)[..., None]
    k_dec = k * jnp.exp(G[..., -1:] - G)[..., None]
    last = jnp.exp(G[..., -1])

    def step(S, inp):
        qk_c, u_c, w_c, qd_c, kd_c, last_c = inp
        v_new = u_c - w_c @ S
        o = qd_c @ S + qk_c @ v_new
        S = S * last_c[..., None, None] + jnp.swapaxes(kd_c, -1, -2) @ v_new
        return S, o

    xs = tuple(jnp.moveaxis(a, 2, 0) for a in (qk, u, w, q_dec, k_dec, last))
    S0 = jnp.zeros((B, H, Dk, Dv), jnp.float32)
    _, o = lax.scan(step, S0, xs)
    return jnp.moveaxis(o, 0, 2).reshape(B, H, T, Dv)

def gated_deltanet(q, k, v, a, b, z, conv_w, a_log, dt_bias, out_gain):
    B, T, _ = q.shape
    qkv = jax.nn.silu(causal_depthwise_conv(jnp.concatenate([q, k, v], axis=-1), conv_w))
    qkv = qkv.astype(jnp.float32).reshape(B, T, 3, GDN_HEADS, GDN_HEAD_DIM)
    qkv = jnp.transpose(qkv, (2, 0, 3, 1, 4))
    qh = l2_norm(qkv[0]) * (GDN_HEAD_DIM ** -0.5)
    kh = l2_norm(qkv[1])
    vh = qkv[2]
    beta = jnp.transpose(jax.nn.sigmoid(b.astype(jnp.float32)), (0, 2, 1))
    g = -jnp.exp(a_log.astype(jnp.float32)) * jax.nn.softplus(a.astype(jnp.float32) + dt_bias.astype(jnp.float32))
    g = jnp.transpose(g, (0, 2, 1))
    o = jnp.transpose(gated_delta_rule(qh, kh, vh, g, beta), (0, 2, 1, 3))
    zh = z.astype(jnp.float32).reshape(B, T, GDN_HEADS, GDN_HEAD_DIM)
    o = rms_norm(o, out_gain) * jax.nn.silu(zh)
    return o.reshape(B, T, GDN_WIDTH).astype(q.dtype)

def memory_cross_attention(h, m, w_xq, w_xkv, xq_gain, xk_gain, w_xo):
    B, T, D = h.shape
    q = (h @ w_xq).reshape(B, T, XA_HEADS, XA_HEAD_DIM)
    kv = (m @ w_xkv).reshape(B, MEM_LEN, 2, XA_HEADS, XA_HEAD_DIM)
    q = rms_norm(q, xq_gain)
    k = rms_norm(kv[:, :, 0], xk_gain)
    v = kv[:, :, 1]
    s = jnp.einsum('bthd,bmhd->bhtm', q, k).astype(jnp.float32) * (XA_HEAD_DIM ** -0.5)
    p = jax.nn.softmax(s, axis=-1).astype(v.dtype)
    o = jnp.einsum('bhtm,bmhd->bthd', p, v).reshape(B, T, D)
    return o @ w_xo

def moe_ffn(h, w_router, b_router, w_gate_up, b_gate_up, w_down, b_down):
    B, T, D = h.shape
    ht = h.reshape(B * T, D)
    logits = (ht @ w_router).astype(jnp.float32) + b_router.astype(jnp.float32)
    top_val, top_idx = lax.top_k(logits, TOP_K)
    top_w = jax.nn.softmax(top_val, axis=-1)
    combine = jnp.sum(jax.nn.one_hot(top_idx, N_EXPERTS, dtype=jnp.float32) * top_w[..., None], axis=1)
    combine = combine.astype(h.dtype)
    y = jnp.zeros_like(ht)
    for e in range(N_EXPERTS):
        gu = ht @ w_gate_up[e] + b_gate_up[e]
        gate = jnp.minimum(gu[:, :D_EXPERT], SWIGLU_LIMIT)
        up = jnp.clip(gu[:, D_EXPERT:], -SWIGLU_LIMIT, SWIGLU_LIMIT)
        act = (up + 1.0) * (gate * jax.nn.sigmoid(SWIGLU_ALPHA * gate))
        y = y + combine[:, e:e + 1] * (act @ w_down[e] + b_down[e])
    return y.reshape(B, T, D)

def setup_inputs(seed: int = 0) -> dict:
    key = jax.random.key(seed)
    ks = jax.random.split(key, 32)
    L, D, F, E = DEPTH, D_MODEL, D_EXPERT, N_EXPERTS

    def nrm(k, shape, scale):
        return jax.random.normal(k, shape, jnp.float32) * scale

    def gain(k, shape):
        return 1.0 + 0.02 * jax.random.normal(k, shape, jnp.float32)

    dt = jnp.exp(jax.random.uniform(ks[9], (L, GDN_HEADS), jnp.float32, math.log(1e-3), math.log(1e-1)))
    return {
        "x": nrm(ks[0], (BATCH, SEQ, D), 1.0),
        "mem": nrm(ks[1], (BATCH, MEM_LEN, D), 1.0),
        "mix_norm": gain(ks[2], (L, D)),
        "w_in": nrm(ks[3], (L, D, IN_WIDTH), D ** -0.5),
        "b_forget": 3.0 + nrm(ks[4], (L, FOX_HEADS), 1.0),
        "fox_q_gain": gain(ks[5], (L, FOX_HEAD_DIM)),
        "fox_k_gain": gain(ks[6], (L, FOX_HEAD_DIM)),
        "fox_out_gain": gain(ks[7], (L, FOX_HEADS, FOX_HEAD_DIM)),
        "gdn_conv_w": nrm(ks[8], (L, 3 * GDN_WIDTH, CONV_WIDTH), CONV_WIDTH ** -0.5),
        "gdn_a_log": jnp.log(jax.random.uniform(ks[10], (L, GDN_HEADS), jnp.float32, 1.0, 16.0)),
        "gdn_dt_bias": dt + jnp.log(-jnp.expm1(-dt)),
        "gdn_out_gain": gain(ks[11], (L, GDN_HEAD_DIM)),
        "w_out": nrm(ks[12], (L, MIX_WIDTH, D), MIX_WIDTH ** -0.5),
        "xattn_norm": gain(ks[13], (L, D)),
        "mem_norm": gain(ks[14], (L, D)),
        "w_xq": nrm(ks[15], (L, D, D), D ** -0.5),
        "w_xkv": nrm(ks[16], (L, D, 2 * D), D ** -0.5),
        "xq_gain": gain(ks[17], (L, XA_HEAD_DIM)),
        "xk_gain": gain(ks[18], (L, XA_HEAD_DIM)),
        "w_xo": nrm(ks[19], (L, D, D), D ** -0.5),
        "moe_norm": gain(ks[20], (L, D)),
        "w_router": nrm(ks[21], (L, D, E), D ** -0.5),
        "b_router": nrm(ks[22], (L, E), 0.01),
        "w_gate_up": nrm(ks[23], (L, E, D, 2 * F), D ** -0.5),
        "b_gate_up": nrm(ks[24], (L, E, 2 * F), 0.01),
        "w_down": nrm(ks[25], (L, E, F, D), F ** -0.5),
        "b_down": nrm(ks[26], (L, E, D), 0.01),
    }

def reference(x, mem, mix_norm, w_in, b_forget, fox_q_gain, fox_k_gain, fox_out_gain,
              gdn_conv_w, gdn_a_log, gdn_dt_bias, gdn_out_gain, w_out,
              xattn_norm, mem_norm, w_xq, w_xkv, xq_gain, xk_gain, w_xo,
              moe_norm, w_router, b_router, w_gate_up, b_gate_up, w_down, b_down):
    B, T, D = x.shape
    split_at = [int(i) for i in np.cumsum(IN_SPLITS)[:-1]]
    for l in range(DEPTH):
        h = rms_norm(x, mix_norm[l])
        proj = h @ w_in[l]
        fq, fk, fv, ff, gq, gk, gv, ga, gb, gz = jnp.split(proj, split_at, axis=-1)
        fq = rms_norm(fq.reshape(B, T, FOX_HEADS, FOX_HEAD_DIM), fox_q_gain[l])
        fk = rms_norm(fk.reshape(B, T, FOX_HEADS, FOX_HEAD_DIM), fox_k_gain[l])
        fv = fv.reshape(B, T, FOX_HEADS, FOX_HEAD_DIM)
        log_f = jax.nn.log_sigmoid(ff.astype(jnp.float32) + b_forget[l].astype(jnp.float32))
        o_fox = forgetting_attention(jnp.transpose(fq, (0, 2, 1, 3)), jnp.transpose(fk, (0, 2, 1, 3)),
                                     jnp.transpose(fv, (0, 2, 1, 3)), jnp.transpose(log_f, (0, 2, 1)))
        o_fox = rms_norm(jnp.transpose(o_fox, (0, 2, 1, 3)), fox_out_gain[l]).reshape(B, T, FOX_WIDTH)
        o_gdn = gated_deltanet(gq, gk, gv, ga, gb, gz, gdn_conv_w[l], gdn_a_log[l],
                               gdn_dt_bias[l], gdn_out_gain[l])
        x = x + jnp.concatenate([o_fox, o_gdn], axis=-1) @ w_out[l]
        x = x + memory_cross_attention(rms_norm(x, xattn_norm[l]), rms_norm(mem, mem_norm[l]),
                                       w_xq[l], w_xkv[l], xq_gain[l], xk_gain[l], w_xo[l])
        x = x + moe_ffn(rms_norm(x, moe_norm[l]), w_router[l], b_router[l],
                        w_gate_up[l], b_gate_up[l], w_down[l], b_down[l])
    return x


_drawn_inputs = setup_inputs


def setup_inputs(seed=0):
    import zlib

    import numpy as np

    out = dict(_drawn_inputs(seed))
    spreads = {}
    factors = {'gdn_out_gain': 2.936,
     'xattn_norm': 5.588,
     'mem_norm': 4.444,
     'xq_gain': 3.614,
     'xk_gain': 8.0,
     'b_gate_up': 42.085,
     'b_down': 48.46,
     'moe_norm': 5.89,
     'b_router': 8.0}
    for name, (base, spread) in spreads.items():
        noise = np.random.default_rng([zlib.crc32(name.encode()), seed]).standard_normal(out[name].shape)
        drawn = base * np.exp(spread * noise) if base else spread * noise
        out[name] = __import__('jax').numpy.asarray(drawn.astype(out[name].dtype))
    for name, factor in factors.items():
        out[name] = (out[name] * factor).astype(out[name].dtype)
    return out
```

```python
from contextlib import ExitStack

import concourse.bass as bass
from concourse import mybir

F32 = mybir.dt.float32
I32 = mybir.dt.int32
ALU = mybir.AluOpType
ACT = mybir.ActivationFunctionType
AX = mybir.AxisListType

P = 128
T = 256
TB = T // P
D = 1024
KD = D // P
EPS = 1e-6
FH, FD = 8, 64
GH, GD = 4, 128
CONV = 4
CHUNK = 64
XH, XD = 4, 256
NE, TOPK = 32, 4
F = 1024
KF = F // P
LIMIT, ALPHA = 7.0, 1.702
NEG = -1.0e30
SLOTS = 64
ROUNDS = T // SLOTS
PAIRS = NE // 2
LEVELS = [1, 2, 4, 8, 16, 32]

FQ, FK, FV, FF = 0, 512, 1024, 1536
GQ, GK, GV, GA, GB, GZ = 1544, 2056, 2568, 3080, 3084, 3088

WIDE = 512
SLOT = KD * WIDE
RING = 6
PRE = 3
PRE_FILLS = 17
JOB_FILLS = 12


def layer_kernel(nc, x, mem, mix_norm, w_in, b_forget, fox_q_gain, fox_k_gain, fox_out_gain,
                 gdn_conv_w, gdn_a_log, gdn_dt_bias, gdn_out_gain, w_out,
                 xattn_norm, mem_norm, w_xq, w_xkv, xq_gain, xk_gain, w_xo,
                 moe_norm, w_router, b_router, w_gate_up, b_gate_up, w_down, b_down, out):
    ctx = ExitStack()
    with ctx:
        def sb(name, shape, dt=F32):
            return ctx.enter_context(nc.sbuf_tensor(name, shape, dt))

        def sem(name):
            return ctx.enter_context(nc.semaphore(name))

        ring = sb("ring", [P, RING * SLOT])
        xs = sb("xs", [P, TB, D])
        hn = sb("hn", [P, TB, D])
        hT = sb("hT", [P, KD, T])
        mixT = sb("mixT", [P, KD, T])
        kvx = sb("kvx", [P, 4096])
        early = sb("early", [P, 4096])
        work = sb("work", [P, 7936])
        ident = sb("ident", [P, P])
        prefix = sb("prefix", [P, P])
        ones = sb("ones", [P, P])
        cprefix = sb("cprefix", [P, P])
        cones = sb("cones", [P, P])
        fmask = sb("fmask", [P, 2, P])
        dmask = sb("dmask", [P, P])
        lmask = sb("lmask", [P, len(LEVELS), P])
        slot_no = sb("slot_no", [P, SLOTS])
        pairsel = sb("pairsel", [2, P])
        gains = sb("gains", [P, 4, KD])
        fqk_gain = sb("fqk_gain", [P, 2])
        fout_gain = sb("fout_gain", [P, 4])
        gout_gain = sb("gout_gain", [P, 1])
        conv_w = sb("conv_w", [P, 12, CONV])
        gate_b = sb("gate_b", [P, 12])
        alog = sb("alog", [P, GH])
        brt = sb("brt", [P, NE])
        x_gain = sb("x_gain", [P, 2, 2])
        wsm = sb("wsm", [P, KD, 16])
        wr = sb("wr", [P, KD, NE])
        ss = sb("ss", [P, 8])
        rs = sb("rs", [P, 8])
        gv = sb("gv", [P, TB, 16])
        gabs = sb("gabs", [P, TB, 12])
        gln = sb("gln", [P, TB, 12])
        nlf = sb("nlf", [P, TB, FH])
        ncum = sb("ncum", [P, TB, FH])
        ea = sb("ea", [P, GH])
        gg = sb("gg", [P, TB, GH])
        beta = sb("beta", [P, TB, GH])
        gcum = sb("gcum", [P, TB, 2, GH])
        sc4 = sb("sc4", [P, TB, 3, GH])
        fmx = sb("fmx", [P, FH, 2])
        fsum = sb("fsum", [P, FH, 2])
        frs = sb("frs", [P, TB, FH])
        grs = sb("grs", [P, TB, GH])
        xmx = sb("xmx", [P, XH, 2])
        xsum = sb("xsum", [P, XH, 2])
        lg = sb("lg", [P, TB, NE])
        top8 = sb("top8", [P, TB, 8])
        rt = sb("rt", [P, TB, 4, NE])
        rcol = sb("rcol", [P, TB, 4])
        sel = sb("sel", [P, TB, NE])
        comb = sb("comb", [P, TB, NE])
        combT = sb("combT", [NE, T])
        posx = sb("posx", [P, TB, (ROUNDS + 1) * NE])
        combx = sb("combx", [P, TB, (ROUNDS + 1) * NE])
        flag_f = sb("flag_f", [P, 1])
        eps = sb("eps", [P, 1])
        flag = sb("flag", [P, 1], I32)

        ps = [ctx.enter_context(nc.psum_tensor(f"ps{i}", [P, WIDE], F32)) for i in range(8)]

        def cut(buf, base, *shape):
            n = 1
            for s in shape:
                n *= s
            v = buf[:, base:base + n]
            if len(shape) == 2:
                v = v.rearrange("p (a b) -> p a b", a=shape[0])
            if len(shape) == 3:
                v = v.rearrange("p (a b c) -> p a b c", a=shape[0], b=shape[1])
            return v

        kxT = cut(kvx, 0, KD, T)
        vx = cut(kvx, 2048, TB, D)
        mn = cut(early, 0, TB, D)
        mT = cut(early, 2048, KD, T)
        kbn = cut(early, 0, TB, GH, P)
        vb = cut(early, 1024, TB, GH, P)
        fqT = cut(work, 0, 4, T)
        fqz = mixT[:, :, :]
        fkT = cut(work, 1024, 4, T)
        fv = cut(work, 2048, TB, FH * FD)
        fS = cut(work, 3072, 2, 3 * P)
        fP = cut(work, 3840, 2, 3 * P)
        fPT = cut(work, 4608, 2, 3 * P)
        fo = cut(work, 5376, TB, FH * FD)
        sq = cut(work, 6400, 4, T)
        rn = cut(work, 7424, 2, T)
        G0 = PRE * SLOT
        raw = cut(ring, G0, 12, T + CONV - 1 + 1)
        cv = cut(ring, G0 + 3120, 12, T)
        gq, gk, gvT = (cv[:, 4 * i:4 * i + 4, :] for i in range(3))
        qd = gq
        kd = cut(ring, G0 + 3120 + 8 * T, TB, GH, P)
        zs = cut(ring, G0 + 6192, TB, GH * GD)
        expG = cut(ring, G0 + 7216, TB, GH, P)
        dec = cut(ring, G0 + 8240, TB, GH, P)
        AT = cut(ring, G0 + 9264, TB, GH, P)
        qkT = cut(ring, G0 + 10288, TB, GH, P)
        assert 11312 <= (RING - PRE) * SLOT
        ATl = [cut(work, 0, TB, GH, P), cut(work, 1024, TB, GH, P)]
        Ti = cut(work, 2048, TB, GH, P)
        TiT = cut(work, 3072, TB, GH, P)
        Xi = cut(work, 4096, TB, GH, P)
        wTn = hn[:, 0, :].rearrange("p (t h c) -> p t h c", t=TB, h=GH)
        vnew = hn[:, 1, :].rearrange("p (t n) -> p t n", t=TB)
        St = cut(ring, G0 + 0, GH, P)
        Sd = cut(ring, G0 + 512, GH, P)
        go = cut(ring, G0 + 1024, TB, GH * GD)
        gsq = cut(ring, G0 + 2048, 1, GH * GD)
        qxT = cut(work, 0, KD, T)
        xP = cut(work, 2048, 2, 2 * T)
        xPT = cut(work, 3072, 2, 2 * T)
        hgT = cut(work, 0, KD, P)
        actT = cut(work, 1024, KF, P)
        gS = cut(work, 2048, 2, WIDE)
        uS = cut(work, 3072, 2, WIDE)
        sS = cut(work, 4096, 2, WIDE)
        aS = cut(work, 5120, 2, WIDE)
        yS = cut(work, 6144, 2, WIDE)
        WT = cut(work, 7168, TB, P)
        Sel = cut(work, 7424, TB, P)
        CW = cut(work, 7680, TB, P)
        bgu = early[0:2, 0:2 * F]
        bdn = work[0:NE, 4096:4096 + D]

        landed = [sem(f"landed{i}") for i in range(RING)]
        spent = [sem(f"spent{i}") for i in range(RING)]
        full = [sem(f"full{i}") for i in range(8)]
        free = [sem(f"free{i}") for i in range(8)]
        s_mem, s_x = sem("mem_loaded"), sem("x_loaded")
        s_par, s_par2 = sem("params_loaded"), sem("gate_weights_loaded")
        s_bgu = sem("expert_bias_loaded")
        s_const = sem("constants_built")
        s_gc = sem("pool_step")
        s_lvl = sem("level_masked")
        s_dv, s_ac = sem("dve_step"), sem("act_step")
        s_ss, s_hn, s_hT = sem("squares_summed"), sem("rows_normalised"), sem("transposed")
        s_raw, s_sq, s_nrm = sem("projection_copied"), sem("squared"), sem("head_normed")
        s_tok = sem("token_values_copied")
        s_gv, s_gln, s_nlf = (sem(n) for n in (
            "gates_in", "gates_logged", "gates_done"))
        s_fs, s_fp, s_fpt, s_fo, s_mix = (sem(n) for n in (
            "fox_scores", "fox_probs", "fox_probs_turned", "fox_out", "mixed"))
        s_conv, s_silu = sem("conv_done"), sem("silu_done")
        s_garg, s_dec, s_kop, s_AT = (sem(n) for n in (
            "decay_argument", "decays_done", "gdn_operands", "gdn_matrices"))
        s_X, s_T, s_w = sem("inverse_product"), sem("inverse_level"), sem("gdn_w")
        s_vn, s_S, s_go, s_gsq = sem("gdn_vnew"), sem("gdn_state"), sem("gdn_out"), sem("gdn_squares")
        s_res = sem("residual_added")
        s_xm, s_xe, s_xp, s_xpt, s_xo = (sem(n) for n in (
            "xattn_max", "xattn_exp", "xattn_probs", "xattn_probs_turned", "xattn_out"))
        s_lg, s_re, s_sel, s_comb, s_combT, s_pos = (sem(n) for n in (
            "logits", "router_exp", "selected", "combine_weights", "combine_turned", "positions"))
        s_flag = sem("overflow_flag")
        j_sel, j_wt, j_hg, j_bias, j_gu = (sem(n) for n in (
            "job_selection", "job_weights_turned", "job_rows_gathered", "job_bias_used", "job_gate_up"))
        j_g, j_u, j_sg, j_a, j_T, j_aT = (sem(n) for n in (
            "job_gate", "job_up", "job_sigmoid", "job_act", "job_act_turn", "job_act_turned"))
        j_D, j_y, j_sc, j_add, j_ga, j_ct = (sem(n) for n in (
            "job_down", "job_rows_out", "job_scattered", "job_added", "job_gather", "job_weights_turn"))
        j_t = sem("job_product")
        s_pv, s_os, s_T0, s_bdn = (sem(n) for n in (
            "fox_values_used", "gdn_state_read", "inverse_start", "down_bias_loaded"))
        s_ident, s_gain = sem("identity_built"), sem("norm_gains_loaded")
        s_arg, s_root = sem("root_argument"), sem("root_taken")
        s_out = sem("stored")

        turn = {}
        uses = [0] * 8

        def plan(name, bank):
            turn[name] = (bank, uses[bank])
            uses[bank] += 1

        rot = [0]

        def plan_next(*names):
            for n in names:
                plan(n, rot[0] % 8)
                rot[0] += 1

        plan_next(*[f"xT{i}" for i in range(4)])
        plan_next("gate0", "gate1")
        plan_next("fq0", "fq1")
        plan_next(*[f"mT{i}" for i in range(4)])
        plan_next("fk0", "fk1", "cumT0", "cumT1", "fqs0", "fqs1", "fks0", "fks1", "fv0", "fv1")
        for h in range(FH + 2):
            if h < FH:
                if h % 2 == 0:
                    plan(f"fcum{h // 2}", 6 + h // 2 % 2)
                plan(f"fS{h}", h % 2)
            if 1 <= h <= FH:
                plan(f"fPT{h - 1}", 2 + (h - 1) % 2)
        plan("fo0", 4)
        plan("fo1", 5)
        rot[0] = 0
        plan_next("GS0", "GS1", "GB0", "GB1", "bB0", "bB1")
        plan_next(*[f"gr{i}" for i in range(6)])
        plan_next(*[f"gs{i}" for i in range(4)])
        plan_next("z0", "z1", "fT0", "fT1", "kx0", "kx1")
        plan_next("ktok0", "vtok0", "ktok1", "vtok1")
        plan_next("kk0", "kk1", "qk0", "qk1")
        plan_next("kx2", "kx3", "kxs0", "kxs1", "kxs2", "kxs3")
        for n in range(len(LEVELS)):
            plan(f"X{n}_0", 0)
            plan(f"X{n}_1", 1)
            if n > 0:
                for tb in range(TB):
                    if n < len(LEVELS) - 1:
                        plan(f"Y{n}_{tb}", 2 + tb)
                    plan(f"YT{n}_{tb}", 4 + tb)
        plan("w0", 6)
        plan("w1", 7)
        plan("vx0", 6)
        plan("vx1", 7)
        for c in range(4):
            plan(f"vn{c}", c % 2)
            if c % 2 == 0:
                plan(f"go{c // 2}", 4 + c // 2)
            if c < 3:
                plan(f"S{c}", 2 + c % 2)
        plan("gT0", 6)
        plan("gT1", 7)
        rot[0] = 0
        plan_next(*[f"wo{i}" for i in range(4)])
        plan_next(*[f"h2T{i}" for i in range(4)])
        plan_next(*[f"qx{i}" for i in range(4)])
        plan_next(*[f"qxs{i}" for i in range(4)])
        plan_next("vx2", "vx3")
        for h in range(XH + 2):
            if h < XH:
                plan(f"xS{h}", h % 2)
            if 1 <= h <= XH:
                plan(f"xPT{h - 1}", 2 + (h - 1) % 2)
            if 2 <= h:
                plan(f"xO{h - 2}", 4 + (h - 2) % 2)
        rot[0] = 0
        plan_next(*[f"xo{i}" for i in range(4)])
        plan_next(*[f"h3T{i}" for i in range(4)])
        plan_next("lg0", "lg1", "rank0", "rank1", "cnt", "cT")
        plan_next(*[f"bd{i}" for i in range(4)])

        def into(pe, name):
            bank, before = turn[name]
            if before:
                pe.wait_ge(free[bank], before)
            return ps[bank]

        def filled(ins, name):
            ins.then_inc(full[turn[name][0]], 1)

        def bank_of(eng, name):
            bank, before = turn[name]
            eng.wait_ge(full[bank], before + 1)
            return ps[bank]

        def read(ins, name):
            ins.then_inc(free[turn[name][0]], 1)

        dma_gates = [w_in[0].rearrange("(p k) n -> p k n", k=KD)]
        w_in_v = dma_gates[0]
        xkv_v = w_xkv[0].rearrange("(p k) n -> p k n", k=KD)
        xq_v = w_xq[0].rearrange("(p k) n -> p k n", k=KD)
        out_v = w_out[0].rearrange("(k p) n -> p k n", p=P)
        xo_v = w_xo[0].rearrange("(k p) n -> p k n", p=P)
        pre_fills = ([w_in_v[:, :, c:c + WIDE] for c in (FQ, FK, FV, GQ, GK, GV, GZ)]
                     + [xkv_v[:, :, WIDE * c:WIDE * c + WIDE] for c in range(3)]
                     + [out_v[:, :, WIDE * c:WIDE * c + WIDE] for c in range(2)]
                     + [xq_v[:, :, WIDE * c:WIDE * c + WIDE] for c in range(2)]
                     + [xkv_v[:, :, 3 * WIDE:4 * WIDE]]
                     + [xo_v[:, :, WIDE * c:WIDE * c + WIDE] for c in range(2)])
        assert len(pre_fills) == PRE_FILLS
        last_bank = ["fq1", "fk1", "fv1", "gr1", "gr3", "gr5", "z1", "kx1", "kx3", "vx1",
                     "wo1", "wo3", "qx1", "qx3", "vx3", "xo1", "xo3"]
        pre_count = [len(range(s, PRE_FILLS, PRE)) if s < PRE else 0 for s in range(RING)]

        def slot(s):
            return ring[:, s * SLOT:(s + 1) * SLOT]

        block = ctx.enter_context(nc.Block())

        def pre_w(pe, f):
            pe.wait_ge(landed[f % PRE], 16 * (f // PRE + 1))
            return slot(f % PRE).rearrange("p (k n) -> p k n", k=KD)

        def full_of(name):
            return full[turn[name][0]], turn[name][1] + 1

        def free_of(name):
            return free[turn[name][0]], turn[name][1] + 1

        gu_v = w_gate_up[0].rearrange("e (p k) n -> e p k n", k=KD)
        dn_v = w_down[0].rearrange("e (k p) n -> e p k n", p=P)

        job_fills = [(a, "gu", q) for q in range(4) for a in range(2)] + \
                    [(a, "dn", q) for q in range(2) for a in range(2)]
        REFILLS = JOB_FILLS // RING

        def gate_up_end(j):
            return spent[7 % RING], REFILLS * j + 7 // RING + 1

        def down_end(j):
            return spent[11 % RING], REFILLS * j + 11 // RING + 1

        @block.sync
        def _(sp):
            def pre_fill(f):
                if f >= PRE:
                    sp.wait_ge(*full_of(last_bank[f - PRE]))
                sp.dma_start(slot(f % PRE).rearrange("p (k n) -> p k n", k=KD), pre_fills[f]).then_inc(landed[f % PRE], 16)

            def expert_fill(j, i, m):
                a, kind, q = job_fills[m]
                s = m % RING
                if not isinstance(j, int) or j > 0 or m >= RING:
                    sp.wait_ge(spent[s], REFILLS * j + m // RING)
                e = 2 * i + a
                view, nk = (gu_v, 2) if kind == "gu" else (dn_v, 4)
                if isinstance(e, int):
                    src = view[e, :, nk * q:nk * q + nk, :]
                else:
                    src = view[bass.ds(e, 1), :, nk * q:nk * q + nk, :].rearrange("e p k n -> p (e k) n")
                sp.dma_start(slot(s).rearrange("p (k n) -> p k n", k=nk), src).then_inc(landed[s], 16)

            def job(j, i):
                sp.wait_ge(j_bias, j)
                sp.dma_start(bgu, b_gate_up[0, bass.ds(2 * i, 2), :]).then_inc(s_bgu, 16)
                for m in range(JOB_FILLS):
                    expert_fill(j, i, m)

            for f in range(PRE_FILLS - 3):
                if f == 1:
                    sp.wait_ge(s_x, 16 * TB)
                pre_fill(f)
            sp.wait_ge(*free_of("gT1"))
            for m in range(PRE, RING):
                expert_fill(0, 0, m)
            sp.dma_start(bdn, b_down[0]).then_inc(s_bdn, 16)
            sp.dma_start(bgu, b_gate_up[0, 0:2, :]).then_inc(s_bgu, 16)
            for f in range(PRE_FILLS - 3, PRE_FILLS):
                pre_fill(f)
            for m in list(range(PRE)) + list(range(RING, JOB_FILLS)):
                if m < PRE:
                    sp.wait_ge(*full_of(last_bank[max(f for f in range(PRE_FILLS) if f % PRE == m)]))
                expert_fill(0, 0, m)
            with sp.Fori(1, PAIRS) as j:
                job(j, j)
            sp.wait_ge(s_flag, 1)
            more = sp.value_load(flag[0:1, 0:1], min_val=0, max_val=1)
            with sp.If(more > 0):
                with sp.Fori(1, ROUNDS) as r:
                    with sp.Fori(0, PAIRS) as i:
                        job(r * PAIRS + i, i)
                sp.wait_ge(j_add, 4 * ROUNDS * PAIRS)
            with sp.Else():
                sp.wait_ge(j_add, 4 * PAIRS)
            sp.dma_start(out[0].rearrange("(t p) d -> p t d", p=P), xs[:, :, :]).then_inc(s_out, 16)
            sp.wait_ge(s_out, 16)

        @block.gpsimd
        def _(pool):
            steps = [0]

            def step(ins):
                steps[0] += 1
                ins.then_inc(s_gc, 1)
                pool.wait_ge(s_gc, steps[0])

            def keep(out_, pattern, base, mult, fill, op=ALU.is_ge):
                step(pool.affine_select(out=out_, in_=out_, compare_op=op, fill=fill, base=base,
                                        pattern=pattern, channel_multiplier=mult))

            step(pool.memset(ident[:, :], 0.0))
            step(pool.memset(eps[:, :], EPS))
            keep(ident[:, :], [[-1, P]], 0, 1, 1.0, ALU.not_equal)
            pool.memset(fqz, 0.0).then_inc(s_ident, 1)
            step(pool.memset(ones[:, :], 1.0))
            step(pool.memset(prefix[:, :], 1.0))
            keep(prefix[:, :], [[1, P]], 0, -1, 0.0)
            step(pool.memset(cones[:, :], 0.0))
            step(pool.memset(cones[0:CHUNK, 0:CHUNK], 1.0))
            step(pool.memset(cones[CHUNK:P, CHUNK:P], 1.0))
            step(pool.tensor_tensor(cprefix[:, :], cones[:, :], prefix[:, :], ALU.mult))
            step(pool.memset(fmask[:, :, :], 0.0))
            keep(fmask[:, 1, :], [[-1, P]], 0, 1, NEG)
            step(pool.tensor_scalar(dmask[:, :], cprefix[:, :], -NEG, NEG, ALU.mult, ALU.add))
            step(pool.memset(lmask[:, :, :], 0.0))
            for n, w in enumerate(LEVELS):
                nb = P // (2 * w)
                upper = lmask[:, n, :].rearrange("p (b u w) -> p b u w", b=nb, u=2)[:, :, 1, :]
                step(pool.memset(upper, 1.0))
                keep(upper, [[-2 * w, nb], [0, w]], 0, 1, 0.0)
                keep(upper, [[2 * w, nb], [0, w]], w - 1, -1, 0.0)
            step(pool.iota(slot_no[:, :], pattern=[[1, SLOTS]], base=0, channel_multiplier=0,
                           allow_small_or_imprecise_dtypes=True))
            step(pool.memset(pairsel[:, :], 1.0))
            keep(pairsel[:, :], [[-1, P]], SLOTS - 1, SLOTS, 0.0)
            keep(pairsel[:, :], [[1, P]], 0, -SLOTS, 0.0)
            pool.memset(raw[:, :, 0:CONV - 1], 0.0).then_inc(s_const, 1)

            for n in range(len(LEVELS)):
                if n == 2:
                    pool.wait_ge(s_T0, 2)
                for tb in range(TB):
                    if n == 0:
                        pool.wait_ge(s_fo, TB)
                        pool.wait_ge(*free_of(f"kk{tb}"))
                        pool.wait_ge(*free_of(f"fT{tb}"))
                    if n >= 2:
                        pool.wait_ge(*full_of(f"X{n - 2}_{tb}"))
                    pool.tensor_tensor(ATl[n % 2][:, tb, :, :], AT[:, tb, :, :],
                                       lmask[:, n:n + 1, :].to_broadcast([P, GH, P]), ALU.mult).then_inc(s_lvl, 1)

        @block.scalar
        def _(act):
            def load(dst, src, s=s_par):
                act.dma_start(dst, src, allow_slow_non_contiguous=True).then_inc(s, 16)

            for tb in range(TB):
                load(xs[:, tb, :], x[0, P * tb:P * tb + P, :], s_x)
            for i, g in enumerate((mix_norm, mem_norm, xattn_norm, moe_norm)):
                load(gains[:, i, :], g[0].rearrange("(p k) -> p k", k=KD), s_gain)
            load(wsm[:, :, 0:8], w_in_v[:, :, FF:FF + 8], s_par2)
            load(wsm[:, :, 8:16], w_in_v[:, :, GA:GA + 8], s_par2)
            load(mn, mem[0].rearrange("(t p) d -> p t d", p=P), s_mem)
            for i, g in enumerate((fox_q_gain, fox_k_gain)):
                load(fqk_gain[0:FD, i:i + 1], g[0].rearrange("(p o) -> p o", o=1))
                load(fqk_gain[FD:P, i:i + 1], g[0].rearrange("(p o) -> p o", o=1))
            load(fout_gain[:, :], fox_out_gain[0].rearrange("(j a) d -> (a d) j", a=2))
            load(gout_gain[:, :], gdn_out_gain[0].rearrange("(p o) -> p o", o=1))
            load(conv_w[:, :, :], gdn_conv_w[0].rearrange("(j p) k -> p j k", p=P))
            load(gate_b[:, 0:FH], b_forget[0:1, :].to_broadcast([P, FH]))
            load(gate_b[:, FH:12], gdn_dt_bias[0:1, :].to_broadcast([P, GH]))
            load(alog[:, :], gdn_a_log[0:1, :].to_broadcast([P, GH]))
            load(brt[:, :], b_router[0:1, :].to_broadcast([P, NE]))
            for i, g in enumerate((xq_gain, xk_gain)):
                load(x_gain[:, i, :], g[0].rearrange("(j p) -> p j", p=P))
            load(wr[:, :, :], w_router[0].rearrange("(p k) n -> p k n", k=KD))

            steps = [0]

            def link(ins):
                steps[0] += 1
                ins.then_inc(s_ac, 1)
                act.wait_ge(s_ac, steps[0])

            def square_rows(src, dst, cols):
                for tb in range(TB):
                    act.activation(dst[:, tb, :], src[:, tb, :], ACT.Square,
                                   accum_out=ss[:, cols + tb:cols + tb + 1]).then_inc(s_ss, 1)

            def root(dst, src, n):
                return act.activation(dst, src, ACT.Sqrt, scale=1.0 / n, bias=eps[:, 0:1])

            def rooted_rows(cols):
                root(rs[:, cols:cols + 2], ss[:, cols:cols + 2], D).then_inc(s_root, 1)

            def head_roots(name, i, n, before, tiles=2):
                b = bank_of(act, f"{name}{i}")
                if before:
                    act.wait_ge(s_nrm, before)
                read(root(rn[:, 0:tiles, :], b[:, 0:tiles * T].rearrange("p (a t) -> p a t", a=tiles), n), f"{name}{i}")

            act.wait_ge(s_ident, 1)
            junk = hT[:, :, :].rearrange("p (t a) n -> p t (a n)", t=TB)
            mjunk = mT.rearrange("p (t a) n -> p t (a n)", t=TB)
            act.wait_ge(s_x, 32)
            square_rows(xs, junk, 2)
            act.wait_ge(s_ss, 2)
            rooted_rows(2)
            act.wait_ge(s_mem, 16)
            square_rows(mn, mjunk, 0)
            act.wait_ge(s_ss, 4)
            rooted_rows(0)

            def project(name, dst, n, sq_read, raws):
                for i in range(n):
                    b = bank_of(act, f"{name}{i}")[:, :].rearrange("p (a t) -> p a t", a=2)
                    act.activation(dst[:, 2 * i:2 * i + 2, :], b, ACT.Copy).then_inc(s_raw, 1)
                    if sq_read[i] is not None:
                        s, v = sq_read[i]
                        act.wait_ge(s, v)
                    act.wait_ge(s_raw, raws + i + 1)
                    ins = act.activation(sq[:, 2 * (i % 2):2 * (i % 2) + 2, :], b, ACT.Square)
                    read(ins, f"{name}{i}")

            act.wait_ge(s_gv, 2)
            act.wait_ge(*free_of("gate0"))
            act.wait_ge(*free_of("gate1"))
            link(act.activation(gabs[:, :, :], gv[:, :, 0:12], ACT.Abs))
            link(act.activation(gabs[:, :, :], gabs[:, :, :], ACT.Exp, scale=-1.0))
            act.activation(gln[:, :, :], gabs[:, :, :], ACT.Ln, bias=1.0).then_inc(s_gln, 1)
            act.activation(beta[:, :, :], gv[:, :, 12:16], ACT.Exp, scale=-1.0).then_inc(s_gln, 1)
            act.wait_ge(s_par, 16 * 14)
            act.activation(ea[:, :], alog[:, :], ACT.Exp).then_inc(s_gln, 1)
            project("fq", fqT, 2, [None, None], 0)
            project("fk", fkT, 2, [full_of("fqs0"), full_of("fqs1")], 2)
            for i in range(2):
                head_roots("fqs", i, FD, i)
            for i in range(2):
                head_roots("fks", i, FD, 2 + i)
            for i in range(2):
                b = bank_of(act, f"fv{i}")
                read(act.activation(fv[:, i, :], b[:, :], ACT.Copy), f"fv{i}")

            for h in range(FH + 1):
                if h < FH:
                    act.wait_ge(s_fs, 2 * h + 2)
                    if h >= 2:
                        act.wait_ge(*full_of(f"fPT{h - 2}"))
                    act.activation(fP[:, h % 2, 0:P], fS[:, h % 2, 0:P], ACT.Exp, bias=fmx[:, h, 0:1],
                                   accum_out=fsum[:, h, 0:1]).then_inc(s_fp, 1)
                    act.activation(fP[:, h % 2, P:3 * P], fS[:, h % 2, P:3 * P], ACT.Exp, bias=fmx[:, h, 1:2],
                                   accum_out=fsum[:, h, 1:2]).then_inc(s_fp, 1)
                if h >= 1:
                    b = bank_of(act, f"fPT{h - 1}")
                    if h >= 3:
                        act.wait_ge(s_pv, h - 2)
                    ins = act.activation(fPT[:, (h - 1) % 2, :], b[:, 0:3 * P], ACT.Copy)
                    read(ins, f"fPT{h - 1}")

            for tb in range(TB):
                act.wait_ge(s_arg, tb + 1)
                root(frs[:, tb, :], frs[:, tb, :], FD).then_inc(s_root, 1)

            act.wait_ge(s_garg, 1)
            act.activation(sc4[:, :, 0, :], gcum[:, :, 0, :], ACT.Exp).then_inc(s_dec, 1)
            act.activation(sc4[:, :, 2, :], sc4[:, :, 2, :], ACT.Exp).then_inc(s_dec, 1)
            for tb in range(TB):
                act.wait_ge(s_garg, 2 + tb)
                b = bank_of(act, f"GB{tb}")
                read(act.activation(expG[:, tb, :, :], b[:, :].rearrange("p (h c) -> p h c", h=GH), ACT.Exp), f"GB{tb}")
                act.activation(dec[:, tb, :, :], dec[:, tb, :, :], ACT.Exp).then_inc(s_dec, 1)
            for i in range(6):
                b = bank_of(act, f"gr{i}")[:, :].rearrange("p (a t) -> p a t", a=2)
                read(act.activation(raw[:, 2 * i:2 * i + 2, CONV - 1:CONV - 1 + T], b, ACT.Copy), f"gr{i}")
            for i in range(2):
                act.wait_ge(s_conv, 4 * i + 4)
                act.activation(cv[:, 4 * i:4 * i + 4, :], cv[:, 4 * i:4 * i + 4, :], ACT.Silu).then_inc(s_silu, 1)
            for i in range(4):
                act.wait_ge(s_silu, i // 2 + 1)
                if i == 0:
                    act.wait_ge(s_fo, TB)
                if i >= 2:
                    act.wait_ge(*full_of(f"gs{i - 2}"))
                act.activation(sq[:, 2 * (i % 2):2 * (i % 2) + 2, :], cv[:, 2 * i:2 * i + 2, :], ACT.Square).then_inc(s_sq, 1)
            act.wait_ge(s_conv, 12)
            act.activation(cv[:, 8:12, :], cv[:, 8:12, :], ACT.Silu).then_inc(s_silu, 1)
            for i in range(4):
                head_roots("gs", i, 1.0, 4 + i)
            for i in range(2):
                b = bank_of(act, f"z{i}")
                read(act.activation(zs[:, i, :], b[:, :], ACT.Silu), f"z{i}")
            project("kx", kxT, 4, [full_of("gs2"), full_of("gs3"), full_of("kxs0"), full_of("kxs1")], 4)
            for i in range(4):
                head_roots("kxs", i, XD, 8 + i, tiles=1)
            for n in range(1, len(LEVELS)):
                for tb in range(TB):
                    b = bank_of(act, f"X{n}_{tb}")
                    if n >= 2:
                        act.wait_ge(*full_of(f"YT{n - 1}_{tb}"))
                    read(act.activation(Xi[:, tb, :, :], b[:, :].rearrange("p (h c) -> p h c", h=GH), ACT.Copy), f"X{n}_{tb}")
            for tb in range(TB):
                b = bank_of(act, f"w{tb}")
                read(act.activation(wTn[:, tb, :, :], b[:, :].rearrange("p (h c) -> p h c", h=GH), ACT.Copy), f"w{tb}")
            def memory_values(i):
                b = bank_of(act, f"vx{i}")
                read(act.activation(vx[:, i % 2, WIDE * (i // 2):WIDE * (i // 2) + WIDE], b[:, :], ACT.Copy), f"vx{i}")

            memory_values(0)
            memory_values(1)
            for tb in range(TB):
                b = bank_of(act, f"go{tb}")
                act.activation(gsq[:, 0, :], b[:, :], ACT.Square).then_inc(s_gsq, 1)
                act.wait_ge(s_gsq, 2 * tb + 2)
                root(grs[:, tb, :], grs[:, tb, :], GD).then_inc(s_root, 1)

            for i in range(4):
                act.wait_ge(*free_of(f"wo{i}"))
            act.wait_ge(s_ss, 4)
            square_rows(xs, junk, 0)
            act.wait_ge(s_ss, 6)
            rooted_rows(0)
            project("qx", qxT, 4, [full_of("kxs2"), full_of("kxs3"), full_of("qxs0"), full_of("qxs1")], 8)
            for i in range(4):
                head_roots("qxs", i, XD, 12 + i, tiles=1)
            memory_values(2)
            memory_values(3)

            for h in range(XH + 2):
                if h < XH:
                    act.wait_ge(s_xm, h + 1)
                    b = bank_of(act, f"xS{h}")[:, :].rearrange("p (a t) -> p a t", a=2)
                    if h >= 2:
                        act.wait_ge(*full_of(f"xPT{h - 2}"))
                    for qb in range(2):
                        ins = act.activation(xP[:, h % 2, T * qb:T * qb + T], b[:, qb, :], ACT.Exp, scale=XD ** -0.5,
                                             bias=xmx[:, h, qb:qb + 1], accum_out=xsum[:, h, qb:qb + 1])
                        if qb:
                            read(ins, f"xS{h}")
                        else:
                            ins.then_inc(s_xe, 1)
                if 1 <= h <= XH:
                    b = bank_of(act, f"xPT{h - 1}")
                    if h >= 3:
                        act.wait_ge(*full_of(f"xO{h - 3}"))
                    read(act.activation(xPT[:, (h - 1) % 2, :], b[:, :], ACT.Copy), f"xPT{h - 1}")
                if h >= 2:
                    b = bank_of(act, f"xO{h - 2}")[:, :].rearrange("p (a t) -> p a t", a=2)
                    read(act.activation(mixT[:, 2 * (h - 2):2 * (h - 2) + 2, :], b, ACT.Copy), f"xO{h - 2}")

            for i in range(4):
                act.wait_ge(*free_of(f"xo{i}"))
            square_rows(xs, junk, 4)
            act.wait_ge(s_ss, 8)
            rooted_rows(4)
            for tb in range(TB):
                act.wait_ge(s_lg, tb + 1)
                act.activation(rt[:, tb, 3, :], lg[:, tb, :], ACT.Exp, bias=rcol[:, tb, 3:4]).then_inc(s_re, 1)

            def job(j):
                for a in range(2):
                    act.wait_ge(j_g, 2 * j + a + 1)
                    act.activation(sS[:, a, :], gS[:, a, :], ACT.Sigmoid, scale=ALPHA).then_inc(j_sg, 1)
                for a in range(2):
                    act.wait_ge(j_T, 2 * j + a + 1)
                    act.activation(actT[:, 4 * a:4 * a + 4, :], ps[4 + a][:, :].rearrange("p (k s) -> p k s", k=4),
                                   ACT.Copy).then_inc(j_aT, 1)
                for a in range(2):
                    if a == 0:
                        act.wait_ge(j_D, j + 1)
                    else:
                        act.wait_ge(*down_end(j))
                    act.activation(yS[:, a, :], ps[4 + a][:, :], ACT.Copy).then_inc(j_y, 1)

            job(0)
            with act.Fori(1, PAIRS) as j:
                job(j)
            act.wait_ge(s_flag, 1)
            more = act.value_load(flag[0:1, 0:1], min_val=0, max_val=1)
            with act.If(more > 0):
                with act.Fori(PAIRS, ROUNDS * PAIRS) as j:
                    job(j)
                act.nop()
            with act.Else():
                act.nop()

        @block.vector
        def _(dve):
            V = nc.vector
            steps = [0]

            def link(ins):
                steps[0] += 1
                ins.then_inc(s_dv, 1)
                dve.wait_ge(s_dv, steps[0])

            rooted = [0]

            def root_wait():
                rooted[0] += 1
                dve.wait_ge(s_root, rooted[0])


            def norm_rows(src, dst, cols):
                root_wait()
                link(V.reciprocal(rs[:, cols:cols + 2], rs[:, cols:cols + 2]))
                for tb in range(TB):
                    V.tensor_scalar(dst[:, tb, :], src[:, tb, :], rs[:, cols + tb:cols + tb + 1], None,
                                    ALU.mult).then_inc(s_hn, 1)

            def turned(name, dst, gain):
                for i in range(4):
                    q, tb = i % 2, i // 2
                    b = bank_of(dve, f"{name}{i}")[:, :].rearrange("p (k t) -> p k t", k=4)
                    ins = V.tensor_tensor(dst[:, 4 * q:4 * q + 4, P * tb:P * tb + P], b,
                                          gains[:, gain, 4 * q:4 * q + 4].unsqueeze(2).to_broadcast([P, 4, P]), ALU.mult)
                    read(ins, f"{name}{i}")

            norm_rows(xs, hn, 2)
            dve.wait_ge(s_gain, 16 * 4)
            turned("xT", hT, 0)
            norm_rows(mn, mn, 0)
            dve.wait_ge(s_par, 16 * 14)

            for tb in range(TB):
                b = bank_of(dve, f"gate{tb}")
                V.tensor_tensor(gv[:, tb, 0:12], b[:, 0:12], gate_b[:, :], ALU.add).then_inc(s_gv, 1)
                read(V.tensor_copy(gv[:, tb, 12:16], b[:, 12:16]), f"gate{tb}")
            def head_norm(name, i, dst, gain, tiles, root):
                dve.wait_ge(*free_of(f"{name}{i}"))
                r = rn[:, 0:2 // tiles, :]
                link(V.reciprocal(r, r))
                for c in range(tiles):
                    n = 2 // tiles
                    d = dst[:, 2 * i + c:2 * i + c + n, :]
                    ins = V.scalar_tensor_tensor(d, d, gain[c], r, ALU.mult, ALU.mult)
                    if c == tiles - 1:
                        ins.then_inc(s_nrm, 1)
                        dve.wait_ge(s_nrm, root)
                    else:
                        link(ins)

            dve.wait_ge(s_gln, 3)
            link(V.tensor_scalar(nlf[:, :, :], gv[:, :, 0:8], -1.0, 0.0, ALU.mult, ALU.max))
            V.tensor_tensor(nlf[:, :, :], nlf[:, :, :], gln[:, :, 0:8], ALU.add).then_inc(s_nlf, 1)
            link(V.tensor_scalar(gg[:, :, :], gv[:, :, 8:12], 0.0, None, ALU.max))
            link(V.tensor_tensor(gg[:, :, :], gg[:, :, :], gln[:, :, 8:12], ALU.add))
            link(V.scalar_tensor_tensor(gg[:, :, :], gg[:, :, :], -1.0,
                                        ea[:, :].unsqueeze(1).to_broadcast([P, TB, GH]), ALU.mult, ALU.mult))
            link(V.tensor_scalar(beta[:, :, :], beta[:, :, :], 1.0, None, ALU.add))
            V.reciprocal(beta[:, :, :], beta[:, :, :]).then_inc(s_nlf, 1)
            dve.wait_ge(s_nlf, 2)
            turned("mT", mT, 1)
            for i in range(2):
                dve.wait_ge(*free_of(f"fqs{i}"))
                link(V.reciprocal(rn[:, :, :], rn[:, :, :]))
                for half in range(2):
                    r = slice(FD * half, FD * half + FD)
                    d = fqz.rearrange("p (t a) n -> p t a n", a=2)[r, 2 * i:2 * i + 2, half, :]
                    ins = V.scalar_tensor_tensor(d, fqT[r, 2 * i:2 * i + 2, :], fqk_gain[r, 0:1], rn[r, :, :],
                                                 ALU.mult, ALU.mult)
                    if half:
                        ins.then_inc(s_nrm, 1)
                        dve.wait_ge(s_nrm, i + 1)
                    else:
                        link(ins)
            for i in range(2):
                head_norm("fks", i, fkT, [fqk_gain[:, 1:2]], 1, 3 + i)
            for tb in range(TB):
                b = bank_of(dve, f"cumT{tb}")
                read(V.tensor_copy(ncum[:, tb, :], b[:, 0:FH]), f"cumT{tb}")

            dve.wait_ge(s_const, 1)
            dve.wait_ge(free[turn["cumT1"][0]], turn["cumT1"][1] + 1)
            dve.wait_ge(free[turn["cumT0"][0]], turn["cumT0"][1] + 1)
            for h in range(FH):
                S = fS[:, h % 2, :]
                if h >= 2:
                    dve.wait_ge(s_fp, 2 * (h - 1))
                b = bank_of(dve, f"fcum{h // 2}")[:, T * (h % 2):T * (h % 2) + T]
                link(V.scalar_tensor_tensor(S[:, 0:P], b[:, 0:P], ncum[:, 0, h:h + 1], fmask[:, 1, :],
                                            ALU.subtract, ALU.add))
                ins = V.scalar_tensor_tensor(S[:, P:3 * P], b, ncum[:, 1, h:h + 1],
                                             fmask[:, :, :].rearrange("p a k -> p (a k)"), ALU.subtract, ALU.add)
                if h % 2:
                    read(ins, f"fcum{h // 2}")
                    dve.wait_ge(free[turn[f"fcum{h // 2}"][0]], turn[f"fcum{h // 2}"][1] + 1)
                else:
                    link(ins)
                b = bank_of(dve, f"fS{h}")
                read(V.scalar_tensor_tensor(S, b[:, 0:3 * P], FD ** -0.5, S, ALU.mult, ALU.add), f"fS{h}")
                dve.wait_ge(free[turn[f"fS{h}"][0]], turn[f"fS{h}"][1] + 1)
                V.tensor_reduce(fmx[:, h, 0:1], S[:, 0:P], AX.X, ALU.max, negate=True).then_inc(s_fs, 1)
                V.tensor_reduce(fmx[:, h, 1:2], S[:, P:3 * P], AX.X, ALU.max, negate=True).then_inc(s_fs, 1)

            dve.wait_ge(s_fp, 2 * FH)
            link(V.reciprocal(fsum[:, :, :], fsum[:, :, :]))
            fsq = sq[:, :, :].rearrange("p a t -> p (a t)")[:, 0:FH * FD]
            for tb in range(TB):
                b = bank_of(dve, f"fo{tb}")[:, :].rearrange("p (h d) -> p h d", h=FH)
                o = fo[:, tb, :].rearrange("p (h d) -> p h d", h=FH)
                read(V.tensor_tensor(o, b, fsum[:, :, tb:tb + 1].to_broadcast([P, FH, FD]), ALU.mult), f"fo{tb}")
                dve.wait_ge(free[turn[f"fo{tb}"][0]], turn[f"fo{tb}"][1] + 1)
                if tb == 0:
                    dve.wait_ge(*full_of("fks1"))
                link(V.tensor_tensor(fsq.rearrange("p (h d) -> p h d", h=FH), o, o, ALU.mult))
                V.tensor_reduce(frs[:, tb, :], fsq.rearrange("p (h d) -> p h d", h=FH), AX.X, ALU.add).then_inc(s_arg, 1)
                root_wait()
                link(V.reciprocal(frs[:, tb, :], frs[:, tb, :]))
                V.tensor_tensor(o, o, frs[:, tb, :].unsqueeze(2).to_broadcast([P, FH, FD]), ALU.mult).then_inc(s_fo, 1)

            for tb in range(TB):
                b = bank_of(dve, f"GS{tb}")
                read(V.tensor_copy(gcum[:, tb, :, :], b[:, 0:2 * GH].rearrange("p (a h) -> p a h", a=2)), f"GS{tb}")
                dve.wait_ge(free[turn[f"GS{tb}"][0]], turn[f"GS{tb}"][1] + 1)
            V.tensor_tensor(sc4[:, :, 2, :], gcum[:, :, 1, :], gcum[:, :, 0, :], ALU.subtract).then_inc(s_garg, 1)
            for tb in range(TB):
                b = bank_of(dve, f"GB{tb}")
                for h in range(GH):
                    ins = V.scalar_tensor_tensor(dec[:, tb, h, :], b[:, P * h:P * h + P], gcum[:, tb, 0, h:h + 1],
                                                 dmask[:, :], ALU.subtract, ALU.add)
                    if h < GH - 1:
                        link(ins)
                    else:
                        ins.then_inc(s_garg, 1)

            for i in range(12):
                if i % 2 == 0:
                    dve.wait_ge(free[turn[f"gr{i // 2}"][0]], turn[f"gr{i // 2}"][1] + 1)
                link(V.tensor_scalar(cv[:, i, :], raw[:, i, 0:T], conv_w[:, i, 0:1], None, ALU.mult))
                for c in range(1, CONV):
                    ins = V.scalar_tensor_tensor(cv[:, i, :], raw[:, i, c:c + T], conv_w[:, i, c:c + 1], cv[:, i, :],
                                                 ALU.mult, ALU.add)
                    if c < CONV - 1:
                        link(ins)
                    else:
                        ins.then_inc(s_conv, 1)
            for tb in range(TB):
                dve.wait_ge(s_dec, 3 + tb)
                b = bank_of(dve, f"bB{tb}")[:, :].rearrange("p (h c) -> p h c", h=GH)
                read(V.tensor_tensor(AT[:, tb, :, :], b, dec[:, tb, :, :], ALU.mult), f"bB{tb}")
            for i in range(4):
                head_norm("gs", i, cv, [GD ** -0.5 if i < 2 else 1.0], 1, 5 + i)
            for tb in range(TB):
                b = bank_of(dve, f"fT{tb}")[:, :].rearrange("p (k t) -> p k t", k=4)
                read(V.tensor_tensor(mixT[:, 0:4, P * tb:P * tb + P], b,
                                     fout_gain[:, :].unsqueeze(2).to_broadcast([P, 4, P]), ALU.mult), f"fT{tb}")
            dve.wait_ge(s_dec, 2)
            link(V.scalar_tensor_tensor(sc4[:, :, 1, :], sc4[:, :, 0, :], -1.0, beta[:, :, :], ALU.mult, ALU.mult))
            dve.wait_ge(*full_of("vtok1"))
            for tb in range(TB):
                b = bank_of(dve, f"ktok{tb}")[:, :].rearrange("p (h d) -> p h d", h=GH)
                V.tensor_tensor(kbn[:, tb, :, :], b, sc4[:, tb, 1, :].unsqueeze(2).to_broadcast([P, GH, GD]), ALU.mult).then_inc(s_kop, 1)
                read(V.tensor_tensor(kd[:, tb, :, :], b, sc4[:, tb, 2, :].unsqueeze(2).to_broadcast([P, GH, GD]), ALU.mult), f"ktok{tb}")
                b = bank_of(dve, f"vtok{tb}")[:, :].rearrange("p (h d) -> p h d", h=GH)
                read(V.tensor_tensor(vb[:, tb, :, :], b, beta[:, tb, :].unsqueeze(2).to_broadcast([P, GH, GD]), ALU.mult), f"vtok{tb}")
            for tb in range(TB):
                dve.wait_ge(*free_of(f"bB{tb}"))
                b = bank_of(dve, f"kk{tb}")[:, :].rearrange("p (h c) -> p h c", h=GH)
                read(V.tensor_tensor(AT[:, tb, :, :], b, AT[:, tb, :, :], ALU.mult), f"kk{tb}")
                b = bank_of(dve, f"qk{tb}")[:, :].rearrange("p (h c) -> p h c", h=GH)
                read(V.tensor_tensor(qkT[:, tb, :, :], b, dec[:, tb, :, :], ALU.mult), f"qk{tb}")
            for tb in range(TB):
                V.tensor_tensor(qd[:, :, P * tb:P * tb + P], gq[:, :, P * tb:P * tb + P], expG[:, tb, :, :],
                                ALU.mult).then_inc(s_kop, 1)
            for i in range(4):
                head_norm("kxs", i, kxT, [x_gain[:, 1, c:c + 1] for c in range(2)], 2, 9 + i)

            idb = ident[:, :].unsqueeze(1).to_broadcast([P, GH, P])
            for tb in range(TB):
                dve.wait_ge(s_lvl, tb + 1)
                V.tensor_tensor(TiT[:, tb, :, :], idb, ATl[0][:, tb, :, :], ALU.subtract).then_inc(s_T0, 1)
                b = bank_of(dve, f"X0_{tb}")[:, :].rearrange("p (h c) -> p h c", h=GH)
                read(V.tensor_tensor(Ti[:, tb, :, :], idb, b, ALU.subtract), f"X0_{tb}")
            for n in range(1, len(LEVELS)):
                for tb in range(TB):
                    if n < len(LEVELS) - 1:
                        b = bank_of(dve, f"Y{n}_{tb}")[:, :].rearrange("p (h c) -> p h c", h=GH)
                        dve.wait_ge(*free_of(f"X0_{tb}" if n == 1 else f"Y{n - 1}_{tb}"))
                        read(V.tensor_tensor(Ti[:, tb, :, :], Ti[:, tb, :, :], b, ALU.subtract), f"Y{n}_{tb}")
                    b = bank_of(dve, f"YT{n}_{tb}")[:, :].rearrange("p (h c) -> p h c", h=GH)
                    if n == 1:
                        dve.wait_ge(s_T0, tb + 1)
                    else:
                        dve.wait_ge(*free_of(f"YT{n - 1}_{tb}"))
                    read(V.tensor_tensor(TiT[:, tb, :, :], TiT[:, tb, :, :], b, ALU.subtract), f"YT{n}_{tb}")

            for c in range(4):
                tb, r0 = c // 2, CHUNK * (c % 2)
                b = bank_of(dve, f"vn{c}")
                read(V.tensor_copy(vnew[r0:r0 + CHUNK, tb, :], b[r0:r0 + CHUNK, :]), f"vn{c}")
                if c < 3:
                    b = bank_of(dve, f"S{c}")[:, :].rearrange("p (h d) -> p h d", h=GH)
                    if c:
                        dve.wait_ge(*free_of(f"S{c - 1}"))
                        link(V.tensor_tensor(Sd, St, expG[:, tb, :, r0 + CHUNK - 1:r0 + CHUNK].to_broadcast([P, GH, GD]),
                                             ALU.mult))
                        dve.wait_ge(*(full_of(f"go{tb}") if c % 2 else (s_os, c // 2 + 1)))
                        read(V.tensor_tensor(St, Sd, b, ALU.add), f"S{c}")
                    else:
                        read(V.tensor_copy(St, b), f"S{c}")
            for tb in range(TB):
                dve.wait_ge(s_gsq, 2 * tb + 1)
                V.tensor_reduce(grs[:, tb, :], gsq[:, 0, :].rearrange("p (h d) -> p h d", h=GH), AX.X, ALU.add).then_inc(s_gsq, 1)
                root_wait()
                link(V.reciprocal(grs[:, tb, :], grs[:, tb, :]))
                b = bank_of(dve, f"go{tb}")[:, :].rearrange("p (h d) -> p h d", h=GH)
                g = go[:, tb, :].rearrange("p (h d) -> p h d", h=GH)
                read(V.tensor_tensor(g, b, grs[:, tb, :].unsqueeze(2).to_broadcast([P, GH, GD]), ALU.mult), f"go{tb}")
                dve.wait_ge(free[turn[f"go{tb}"][0]], turn[f"go{tb}"][1] + 1)
                V.tensor_tensor(go[:, tb, :], go[:, tb, :], zs[:, tb, :], ALU.mult).then_inc(s_go, 1)
            for tb in range(TB):
                b = bank_of(dve, f"gT{tb}")[:, :].rearrange("p (k t) -> p k t", k=4)
                read(V.tensor_scalar(mixT[:, 4:8, P * tb:P * tb + P], b, gout_gain[:, 0:1], None, ALU.mult), f"gT{tb}")
                dve.wait_ge(free[turn[f"gT{tb}"][0]], turn[f"gT{tb}"][1] + 1)

            def residual(name):
                for i in range(4):
                    b = bank_of(dve, f"{name}{i}")
                    n0 = WIDE * (i // 2)
                    dst = xs[:, i % 2, n0:n0 + WIDE]
                    read(V.tensor_tensor(dst, dst, b[:, :], ALU.add), f"{name}{i}")
                for i in range(4):
                    dve.wait_ge(*free_of(f"{name}{i}"))

            residual("wo")
            norm_rows(xs, hn, 0)
            turned("h2T", hT, 2)
            for i in range(4):
                head_norm("qxs", i, qxT, [x_gain[:, 0, c:c + 1] for c in range(2)], 2, 13 + i)

            for h in range(XH + 1):
                if h < XH:
                    b = bank_of(dve, f"xS{h}")[:, :].rearrange("p (a t) -> p a t", a=2)
                    link(V.tensor_reduce(xmx[:, h, :], b, AX.X, ALU.max))
                    V.tensor_scalar(xmx[:, h, :], xmx[:, h, :], -(XD ** -0.5), None, ALU.mult).then_inc(s_xm, 1)
                if h:
                    g = h - 1
                    dve.wait_ge(s_xe, g + 1)
                    dve.wait_ge(free[turn[f"xS{g}"][0]], turn[f"xS{g}"][1] + 1)
                    link(V.reciprocal(xsum[:, g, :], xsum[:, g, :]))
                    pv = xP[:, g % 2, :].rearrange("p (a t) -> p a t", a=2)
                    V.tensor_tensor(pv, pv, xsum[:, g, :].unsqueeze(2).to_broadcast([P, 2, T]), ALU.mult).then_inc(s_xp, 1)

            residual("xo")
            norm_rows(xs, hn, 4)
            turned("h3T", hT, 3)

            for tb in range(TB):
                b = bank_of(dve, f"lg{tb}")
                L = lg[:, tb, :]
                read(V.tensor_tensor(L, b[:, 0:NE], brt[:, :], ALU.add), f"lg{tb}")
                dve.wait_ge(free[turn[f"lg{tb}"][0]], turn[f"lg{tb}"][1] + 1)
                link(V.max(top8[:, tb, :], L))
                link(V.tensor_scalar(rcol[:, tb, 3:4], top8[:, tb, 0:1], -1.0, None, ALU.mult))
                V.tensor_scalar(rt[:, tb, 0, :], L, top8[:, tb, TOPK - 1:TOPK], None, ALU.is_gt).then_inc(s_lg, 1)
                link(V.tensor_scalar(rt[:, tb, 1, :], L, top8[:, tb, TOPK - 1:TOPK], None, ALU.is_equal))
                dve.wait_ge(s_lg, tb + 1)
                link(V.tensor_reduce(rcol[:, tb, 0:1], rt[:, tb, 0, :], AX.X, ALU.add))
                link(V.tensor_scalar(rcol[:, tb, 1:2], rcol[:, tb, 0:1], -1.0, float(TOPK), ALU.mult, ALU.add))
                link(V.tensor_tensor_scan(rt[:, tb, 2, :], ones[:, 0:NE], rt[:, tb, 1, :], 0.0, ALU.mult, ALU.add))
                link(V.scalar_tensor_tensor(rt[:, tb, 1, :], rt[:, tb, 2, :], rcol[:, tb, 1:2], rt[:, tb, 1, :],
                                            ALU.is_le, ALU.mult))
                V.tensor_tensor(sel[:, tb, :], rt[:, tb, 0, :], rt[:, tb, 1, :], ALU.add).then_inc(s_sel, 1)
                dve.wait_ge(s_sel, tb + 1)
                dve.wait_ge(s_re, tb + 1)
                link(V.tensor_tensor(comb[:, tb, :], rt[:, tb, 3, :], sel[:, tb, :], ALU.mult))
                link(V.tensor_reduce(rcol[:, tb, 2:3], comb[:, tb, :], AX.X, ALU.add))
                link(V.reciprocal(rcol[:, tb, 2:3], rcol[:, tb, 2:3]))
                V.tensor_scalar(comb[:, tb, :], comb[:, tb, :], rcol[:, tb, 2:3], None, ALU.mult).then_inc(s_comb, 1)
            dve.wait_ge(s_comb, 2)
            for tb in range(TB):
                b = bank_of(dve, f"rank{tb}")
                read(V.tensor_tensor(rt[:, tb, 0, :], b[:, 0:NE], sel[:, tb, :], ALU.mult), f"rank{tb}")
                dve.wait_ge(free[turn[f"rank{tb}"][0]], turn[f"rank{tb}"][1] + 1)
            for r in range(ROUNDS + 1):
                link(V.tensor_scalar(posx[:, :, NE * r:NE * r + NE], rt[:, :, 0, :], -1.0 - SLOTS * r, None, ALU.add))
                link(V.tensor_copy(combx[:, :, NE * r:NE * r + NE], comb[:, :, :]))
            b = bank_of(dve, "cnt")
            read(V.tensor_reduce(flag_f[:, :], b[:, 0:NE], AX.X, ALU.max), "cnt")
            dve.wait_ge(free[turn["cnt"][0]], turn["cnt"][1] + 1)
            link(V.tensor_scalar(flag_f[:, :], flag_f[:, :], float(SLOTS), None, ALU.is_gt))
            V.tensor_copy(flag[:, :], flag_f[:, :]).then_inc(s_flag, 1)
            b = bank_of(dve, "cT")
            read(V.tensor_copy(combT[:, :], b[0:NE, 0:T]), "cT")
            residual("bd")

            sel4 = Sel.rearrange("p t (a s) -> p t a s", a=2)
            cw4 = CW.rearrange("p t (a s) -> p t a s", a=2)

            def cols(buf, j):
                v = buf[:, :, 2 * j:2 * j + 2] if isinstance(j, int) else buf[:, :, bass.ds(2 * j, 2)]
                return v

            def select(j, first=False):
                for tb in range(TB):
                    for a in range(2):
                        pos = posx[:, tb, 2 * j + a:2 * j + a + 1] if isinstance(j, int) else posx[:, tb, bass.ds(2 * j + a, 1)]
                        cmb = combx[:, tb, 2 * j + a:2 * j + a + 1] if isinstance(j, int) else combx[:, tb, bass.ds(2 * j + a, 1)]
                        V.tensor_scalar(sel4[:, tb, a, :], slot_no[:, :], pos, None, ALU.is_equal).then_inc(j_sel, 1)
                        V.tensor_scalar(cw4[:, tb, a, :], slot_no[:, :], pos, cmb, ALU.is_equal, ALU.mult).then_inc(j_sel, 1)

            def gathered(j):
                for a in range(2):
                    dve.wait_ge(j_ga, 2 * j + a + 1)
                    V.tensor_tensor(hgT[:, 4 * a:4 * a + 4, :], ps[6 + a][:, :].rearrange("p (k s) -> p k s", k=4),
                                    gains[:, 3, 4 * a:4 * a + 4].unsqueeze(2).to_broadcast([P, 4, P]), ALU.mult).then_inc(j_hg, 1)

            def add(j, n):
                for tb in range(TB):
                    dve.wait_ge(j_sc, 4 * j + 2 * n + tb + 1)
                    dst = xs[:, tb, WIDE * n:WIDE * n + WIDE]
                    V.tensor_tensor(dst, dst, ps[6 + tb][:, :], ALU.add).then_inc(j_add, 1)

            def weights_turned(j):
                dve.wait_ge(j_ct, j + 1)
                V.tensor_copy(WT[:, :, :], ps[6][:, 0:T].rearrange("p (t s) -> p t s", t=TB)).then_inc(j_wt, 1)

            def job(j, first=False):
                for a in range(2):
                    if a == 0:
                        dve.wait_ge(j_gu, j + 1)
                    else:
                        dve.wait_ge(*gate_up_end(j))
                    V.tensor_scalar(gS[:, a, :], ps[a][:, :], LIMIT, None, ALU.min).then_inc(j_g, 1)
                    V.tensor_scalar(uS[:, a, :], ps[2 + a][:, :], LIMIT, -LIMIT, ALU.min, ALU.max).then_inc(j_u, 1)
                    dve.wait_ge(j_u, 2 * j + a + 1)
                    dve.wait_ge(j_g, 2 * j + a + 1)
                    V.scalar_tensor_tensor(uS[:, a, :], uS[:, a, :], 1.0, gS[:, a, :], ALU.add, ALU.mult).then_inc(j_t, 1)
                    dve.wait_ge(j_sg, 2 * j + a + 1)
                    dve.wait_ge(j_t, 2 * j + a + 1)
                    V.tensor_tensor(aS[:, a, :], uS[:, a, :], sS[:, a, :], ALU.mult).then_inc(j_a, 1)
                if not first:
                    for n in range(2):
                        add(j - 1, n)
                weights_turned(j)
                select(j + 1)
                gathered(j + 1)

            select(0)
            gathered(0)
            job(0, first=True)
            with dve.Fori(1, PAIRS) as j:
                job(j)
            more = dve.value_load(flag[0:1, 0:1], min_val=0, max_val=1)

            def last(j):
                for n in range(2):
                    add(j, n)

            with dve.If(more > 0):
                with dve.Fori(PAIRS, ROUNDS * PAIRS) as j:
                    job(j)
                last(ROUNDS * PAIRS - 1)
            with dve.Else():
                last(PAIRS - 1)

        @block.tensor
        def _(pe):
            M = nc.tensor

            def turn_rows(src, name, ready):
                for i in range(4):
                    q, tb = i % 2, i // 2
                    pe.wait_ge(s_hn, ready + tb)
                    b = into(pe, f"{name}{i}")
                    for k in range(4):
                        ins = M.transpose(b[:, P * k:P * k + P],
                                          src[:, tb, :].rearrange("p (d k) -> p k d", k=KD)[:, 4 * q + k, :], ident[:, :])
                    filled(ins, f"{name}{i}")

            def channel_banks(w, rhsT, name, i0=0):
                for i in range(2):
                    b = into(pe, f"{name}{i0 + i}")
                    for c in range(2):
                        for k in range(KD):
                            ins = M.matmul(b[:, T * c:T * c + T], w[:, k, P * (2 * i + c):P * (2 * i + c) + P], rhsT[:, k, :],
                                           start=(k == 0), stop=(k == KD - 1))
                    filled(ins, f"{name}{i0 + i}")

            def token_bank(w, lhs, name, tb):
                b = into(pe, name)
                for k in range(KD):
                    ins = M.matmul(b[:, :], lhs[:, k, P * tb:P * tb + P], w[:, k, :], start=(k == 0), stop=(k == KD - 1))
                filled(ins, name)

            def evacuated(name):
                pe.wait_ge(*free_of(name))

            pe.wait_ge(s_ident, 1)
            turn_rows(hn, "xT", 1)
            pe.wait_ge(s_par2, 32)
            for i in range(4):
                evacuated(f"xT{i}")
            for tb in range(TB):
                b = into(pe, f"gate{tb}")
                for k in range(KD):
                    ins = M.matmul(b[:, 0:16], hT[:, k, P * tb:P * tb + P], wsm[:, k, :], start=(k == 0), stop=(k == KD - 1))
                filled(ins, f"gate{tb}")

            def sumsq(name, src, i, width):
                b = into(pe, f"{name}{i}")
                q = sq[:, 2 * (i % 2):2 * (i % 2) + 2, :].rearrange("p a t -> p (a t)")
                if width == 1:
                    M.matmul(b[:, 0:T], ones[:, :], q[:, 0:T], start=True, stop=False)
                    ins = M.matmul(b[:, 0:T], ones[:, :], q[:, T:2 * T], start=False, stop=True)
                else:
                    ins = M.matmul(b[:, :], src[:, :], q, start=True, stop=True)
                filled(ins, f"{name}{i}")

            channel_banks(pre_w(pe, 0), hT, "fq")
            turn_rows(mn, "mT", 3)
            channel_banks(pre_w(pe, 1), hT, "fk")
            pe.wait_ge(s_const, 1)
            pe.wait_ge(s_nlf, 2)
            b = into(pe, "cumT0")
            filled(M.matmul(b[:, 0:FH], prefix[:, :], nlf[:, 0, :], start=True, stop=True), "cumT0")
            b = into(pe, "cumT1")
            M.matmul(b[:, 0:FH], ones[:, :], nlf[:, 0, :], start=True, stop=False)
            filled(M.matmul(b[:, 0:FH], prefix[:, :], nlf[:, 1, :], start=False, stop=True), "cumT1")
            for i in range(2):
                evacuated(f"fq{i}")
                sumsq("fqs", cones, i, 2)
            for i in range(2):
                evacuated(f"fk{i}")
                sumsq("fks", cones, i, 2)
            w = pre_w(pe, 2)
            for tb in range(TB):
                token_bank(w, hT, f"fv{tb}", tb)
            for i in range(2):
                evacuated(f"fv{i}")
            pe.wait_ge(s_nrm, 4)

            for h in range(FH + 2):
                if h < FH:
                    if h % 2 == 0:
                        b = into(pe, f"fcum{h // 2}")
                        for c in range(2):
                            row = [nlf[:, tb, h + c:h + c + 1].to_broadcast([P, P]) for tb in range(TB)]
                            M.matmul(b[:, T * c:T * c + P], row[0], prefix[:, :], start=True, stop=True)
                            M.matmul(b[:, T * c + P:T * c + T], row[0], ones[:, :], start=True, stop=False)
                            ins = M.matmul(b[:, T * c + P:T * c + T], row[1], prefix[:, :], start=False, stop=True)
                        filled(ins, f"fcum{h // 2}")
                    b = into(pe, f"fS{h}")
                    M.matmul(b[:, 0:P], fqz[:, h, 0:P], fkT[:, h // 2, 0:P], start=True, stop=True)
                    filled(M.matmul(b[:, P:3 * P], fqz[:, h, P:T], fkT[:, h // 2, :], start=True, stop=True), f"fS{h}")
                if 1 <= h <= FH:
                    g = h - 1
                    pe.wait_ge(s_fp, 2 * h)
                    b = into(pe, f"fPT{g}")
                    for i in range(3):
                        ins = M.transpose(b[:, P * i:P * i + P], fP[:, g % 2, P * i:P * i + P], ident[:, :])
                    filled(ins, f"fPT{g}")
                if h >= 2:
                    g = h - 2
                    evacuated(f"fPT{g}")
                    if g == 0:
                        o0, o1 = into(pe, "fo0"), into(pe, "fo1")
                    pt, c0 = fPT[:, g % 2, :], FD * g
                    i0 = M.matmul(o0[:, c0:c0 + FD], pt[:, 0:P], fv[:, 0, c0:c0 + FD], start=True, stop=True)
                    M.matmul(o1[:, c0:c0 + FD], pt[:, P:2 * P], fv[:, 0, c0:c0 + FD], start=True, stop=False)
                    i1 = M.matmul(o1[:, c0:c0 + FD], pt[:, 2 * P:3 * P], fv[:, 1, c0:c0 + FD], start=False, stop=True)
                    if g < FH - 1:
                        i1.then_inc(s_pv, 1)
                    else:
                        filled(i0, "fo0")
                        filled(i1, "fo1")

            for tb in range(TB):
                b = into(pe, f"GS{tb}")
                M.matmul(b[:, 0:GH], cprefix[:, :], gg[:, tb, :], start=True, stop=True)
                filled(M.matmul(b[:, GH:2 * GH], cones[:, :], gg[:, tb, :], start=True, stop=True), f"GS{tb}")
            for name, src, rhs in (("GB", gg, cprefix), ("bB", beta, ident)):
                for tb in range(TB):
                    b = into(pe, f"{name}{tb}")
                    for h in range(GH):
                        ins = M.matmul(b[:, P * h:P * h + P], src[:, tb, h:h + 1].to_broadcast([P, P]), rhs[:, :],
                                       start=True, stop=True)
                    filled(ins, f"{name}{tb}")
            for c in range(3):
                channel_banks(pre_w(pe, 3 + c), hT, "gr", 2 * c)
            for i in range(4):
                pe.wait_ge(s_sq, i + 1)
                sumsq("gs", ones, i, 2)
            w = pre_w(pe, 6)
            for tb in range(TB):
                token_bank(w, hT, f"z{tb}", tb)
            for tb in range(TB):
                pe.wait_ge(s_fo, tb + 1)
                b = into(pe, f"fT{tb}")
                for k in range(4):
                    ins = M.transpose(b[:, P * k:P * k + P], fo[:, tb, P * k:P * k + P], ident[:, :])
                filled(ins, f"fT{tb}")
            for i in range(4):
                evacuated(f"mT{i}")
            channel_banks(pre_w(pe, 7), mT, "kx", 0)
            pe.wait_ge(s_nrm, 8)
            pe.wait_ge(s_silu, 3)
            for tb in range(TB):
                for name, src in (("ktok", gk), ("vtok", gvT)):
                    b = into(pe, f"{name}{tb}")
                    for h in range(GH):
                        ins = M.transpose(b[:, P * h:P * h + P], src[:, h, P * tb:P * tb + P], ident[:, :])
                    filled(ins, f"{name}{tb}")
            for name, rhs in (("kk", gk), ("qk", gq)):
                for tb in range(TB):
                    b = into(pe, f"{name}{tb}")
                    for h in range(GH):
                        ins = M.matmul(b[:, P * h:P * h + P], gk[:, h, P * tb:P * tb + P], rhs[:, h, P * tb:P * tb + P],
                                       start=True, stop=True)
                    filled(ins, f"{name}{tb}")
            channel_banks(pre_w(pe, 8), mT, "kx", 2)
            for i in range(4):
                evacuated(f"kx{i}")
                sumsq("kxs", ones, i, 1)
            for tb in range(TB):
                pe.wait_ge(s_lvl, tb + 1)
                b = into(pe, f"X0_{tb}")
                for h in range(GH):
                    ins = M.matmul(b[:, P * h:P * h + P], ATl[0][:, tb, h, :], ident[:, :], start=True, stop=True)
                filled(ins, f"X0_{tb}")
            for n in range(1, len(LEVELS)):
                for tb in range(TB):
                    pe.wait_ge(s_lvl, 2 * n + tb + 1)
                    if n == 1:
                        pe.wait_ge(s_T0, tb + 1)
                        evacuated(f"X0_{tb}")
                    else:
                        evacuated(f"Y{n - 1}_{tb}")
                        evacuated(f"YT{n - 1}_{tb}")
                    b = into(pe, f"X{n}_{tb}")
                    for h in range(GH):
                        ins = M.matmul(b[:, P * h:P * h + P], ATl[n % 2][:, tb, h, :], Ti[:, tb, h, :], start=True, stop=True)
                    filled(ins, f"X{n}_{tb}")
                for tb in range(TB):
                    evacuated(f"X{n}_{tb}")
                    if n < len(LEVELS) - 1:
                        b = into(pe, f"Y{n}_{tb}")
                        for h in range(GH):
                            ins = M.matmul(b[:, P * h:P * h + P], TiT[:, tb, h, :], Xi[:, tb, h, :], start=True, stop=True)
                        filled(ins, f"Y{n}_{tb}")
                    b = into(pe, f"YT{n}_{tb}")
                    for h in range(GH):
                        ins = M.matmul(b[:, P * h:P * h + P], Xi[:, tb, h, :], TiT[:, tb, h, :], start=True, stop=True)
                    filled(ins, f"YT{n}_{tb}")
            for tb in range(TB):
                evacuated(f"YT{len(LEVELS) - 1}_{tb}")
            evacuated("ktok1")
            evacuated("vtok1")
            evacuated("vtok0")
            evacuated("qk1")
            evacuated("qk0")
            pe.wait_ge(s_kop, 4)
            for tb in range(TB):
                b = into(pe, f"w{tb}")
                for h in range(GH):
                    ins = M.matmul(b[:, P * h:P * h + P], kbn[:, tb, h, :], TiT[:, tb, h, :], start=True, stop=True)
                filled(ins, f"w{tb}")
            def values_part(c, tb, k0, k1):
                name = f"vx{2 * c + tb}"
                if k0 == 0:
                    into(pe, name)
                w = pre_w(pe, 9 if c == 0 else 14)
                b = ps[turn[name][0]]
                for k in range(k0, k1):
                    ins = M.matmul(b[:, :], mT[:, k, P * tb:P * tb + P], w[:, k, :], start=(k == 0), stop=(k == KD - 1))
                if k1 == KD:
                    filled(ins, name)

            go_b = {}
            for c in range(4):
                tb, r0 = c // 2, CHUNK * (c % 2)
                rows = slice(r0, r0 + CHUNK)
                if c == 1:
                    evacuated("w0")
                    evacuated("w1")
                if c:
                    evacuated(f"S{c - 1}")
                b = into(pe, f"vn{c}")
                for h in range(GH):
                    o = b[rows, P * h:P * h + P]
                    ins = M.matmul(o, TiT[:, tb, h, rows], vb[:, tb, h, :], start=True, stop=(c == 0))
                    if c:
                        ins = M.matmul(o, wTn[:, tb, h, rows], St[:, h, :], start=False, stop=True)
                filled(ins, f"vn{c}")
                values_part(0, c // 2, 4 * (c % 2), 4 * (c % 2) + 2)
                evacuated(f"vn{c}")
                if c < 3:
                    b = into(pe, f"S{c}")
                    for h in range(GH):
                        ins = M.matmul(b[:, P * h:P * h + P], kd[rows, tb, h, :], vnew[rows, tb, P * h:P * h + P], start=True, stop=True)
                    filled(ins, f"S{c}")
                if c % 2 == 0:
                    go_b[tb] = into(pe, f"go{tb}")
                for h in range(GH):
                    o = go_b[tb][rows, P * h:P * h + P]
                    if c:
                        M.matmul(o, qd[:, h, P * tb + r0:P * tb + r0 + CHUNK], St[:, h, :], start=True, stop=False)
                    ins = M.matmul(o, qkT[rows, tb, h, rows], vnew[rows, tb, P * h:P * h + P], start=(c == 0), stop=True)
                if c % 2:
                    filled(ins, f"go{tb}")
                else:
                    ins.then_inc(s_os, 1)
                values_part(0, c // 2, 4 * (c % 2) + 2, 4 * (c % 2) + 4)
            for tb in range(TB):
                pe.wait_ge(s_go, tb + 1)
                b = into(pe, f"gT{tb}")
                for k in range(4):
                    ins = M.transpose(b[:, P * k:P * k + P], go[:, tb, P * k:P * k + P], ident[:, :])
                filled(ins, f"gT{tb}")
            evacuated("gT0")
            evacuated("gT1")
            evacuated("fT0")
            evacuated("fT1")

            def output_projection(f, name):
                for c in range(2):
                    w = pre_w(pe, f + c)
                    for tb in range(TB):
                        token_bank(w, mixT, f"{name}{2 * c + tb}", tb)

            output_projection(10, "wo")
            turn_rows(hn, "h2T", 5)
            for i in range(4):
                evacuated(f"h2T{i}")
            for c in range(2):
                channel_banks(pre_w(pe, 12 + c), hT, "qx", 2 * c)
                for i in (2 * c, 2 * c + 1):
                    evacuated(f"qx{i}")
                    sumsq("qxs", ones, i, 1)
            for tb in range(TB):
                values_part(1, tb, 0, KD)
            pe.wait_ge(s_nrm, 16)
            for h in range(XH + 2):
                if h < XH:
                    b = into(pe, f"xS{h}")
                    for qb in range(2):
                        for c in range(2):
                            ins = M.matmul(b[:, T * qb:T * qb + T], qxT[:, 2 * h + c, P * qb:P * qb + P], kxT[:, 2 * h + c, :],
                                           start=(c == 0), stop=(c == 1))
                    filled(ins, f"xS{h}")
                if 1 <= h <= XH:
                    g = h - 1
                    pe.wait_ge(s_xp, h)
                    b = into(pe, f"xPT{g}")
                    for mb in range(2):
                        for qb in range(2):
                            ins = M.transpose(b[:, T * mb + P * qb:T * mb + P * qb + P],
                                              xP[:, g % 2, T * qb + P * mb:T * qb + P * mb + P], ident[:, :])
                    filled(ins, f"xPT{g}")
                if h >= 2:
                    g = h - 2
                    if g == 0:
                        evacuated("vx2")
                        evacuated("vx3")
                    evacuated(f"xPT{g}")
                    b = into(pe, f"xO{g}")
                    for c in range(2):
                        for mb in range(2):
                            ins = M.matmul(b[:, T * c:T * c + T], vx[:, mb, XD * g + P * c:XD * g + P * c + P],
                                           xPT[:, g % 2, T * mb:T * mb + T], start=(mb == 0), stop=(mb == 1))
                    filled(ins, f"xO{g}")
            for g in range(XH):
                evacuated(f"xO{g}")
            output_projection(15, "xo")
            turn_rows(hn, "h3T", 7)
            for i in range(4):
                evacuated(f"h3T{i}")
            pe.wait_ge(s_par, 16 * 14)
            for tb in range(TB):
                b = into(pe, f"lg{tb}")
                for k in range(KD):
                    ins = M.matmul(b[:, 0:NE], hT[:, k, P * tb:P * tb + P], wr[:, k, :], start=(k == 0), stop=(k == KD - 1))
                filled(ins, f"lg{tb}")
            pe.wait_ge(s_sel, 1)
            b = into(pe, "rank0")
            filled(M.matmul(b[:, 0:NE], prefix[:, :], sel[:, 0, :], start=True, stop=True), "rank0")
            pe.wait_ge(s_sel, 2)
            b = into(pe, "rank1")
            M.matmul(b[:, 0:NE], ones[:, :], sel[:, 0, :], start=True, stop=False)
            filled(M.matmul(b[:, 0:NE], prefix[:, :], sel[:, 1, :], start=False, stop=True), "rank1")
            b = into(pe, "cnt")
            M.matmul(b[:, 0:NE], ones[:, :], sel[:, 0, :], start=True, stop=False)
            filled(M.matmul(b[:, 0:NE], ones[:, :], sel[:, 1, :], start=False, stop=True), "cnt")
            pe.wait_ge(s_comb, 2)
            b = into(pe, "cT")
            for tb in range(TB):
                ins = M.transpose(b[0:NE, P * tb:P * tb + P], comb[:, tb, :], ident[:, :])
            filled(ins, "cT")
            evacuated("cT")
            pe.wait_ge(s_bdn, 16)
            for i in range(4):
                b = into(pe, f"bd{i}")
                filled(M.matmul(b[:, :], combT[:, P * (i % 2):P * (i % 2) + P], bdn[:, WIDE * (i // 2):WIDE * (i // 2) + WIDE],
                                start=True, stop=True), f"bd{i}")
            for name in ("cT", "cnt", "rank0", "rank1", "bd0", "bd1", "bd2", "bd3", "h3T0", "h3T1", "lg0", "lg1"):
                evacuated(name)

            rows_k = hn[:, :, :].rearrange("p t (d k) -> p t k d", k=KD)

            def gather(j):
                pe.wait_ge(j_sel, 8 * j + 8)
                for a in range(2):
                    for q in range(4):
                        for tb in range(TB):
                            ins = M.matmul(ps[6 + a][:, P * q:P * q + P], rows_k[:, tb, 4 * a + q, :], Sel[:, tb, :],
                                           start=(tb == 0), stop=(tb == 1))
                    ins.then_inc(j_ga, 1)

            def scatter(j, n):
                for tb in range(TB):
                    M.matmul(ps[6 + tb][:, :], WT[:, tb, :], yS[:, n, :], start=True, stop=True).then_inc(j_sc, 1)

            def job(j, first=False):
                pe.wait_ge(j_hg, 2 * j + 2)
                pe.wait_ge(s_bgu, 16 * j + 16)
                if not first:
                    pe.wait_ge(j_g, 2 * j)
                    pe.wait_ge(j_u, 2 * j)
                for b in range(4):
                    ins = M.matmul(ps[b][:, :], pairsel[:, :], bgu[:, WIDE * b:WIDE * b + WIDE], start=True, stop=False)
                ins.then_inc(j_bias, 1)
                for q in range(4):
                    w = []
                    for a in range(2):
                        m = 2 * q + a
                        pe.wait_ge(landed[m % RING], 16 * (pre_count[m % RING] + REFILLS * j + m // RING + 1))
                        w.append(slot(m % RING).rearrange("p (k n) -> p k n", k=2))
                    for kk in range(2):
                        k = 2 * q + kk
                        for b in (0, 2, 1, 3):
                            for a in range(2):
                                r = slice(SLOTS * a, SLOTS * a + SLOTS)
                                ins = M.matmul(ps[b][r, :], hgT[:, k, r], w[a][:, kk, WIDE * b:WIDE * b + WIDE],
                                               start=False, stop=(k == KD - 1))
                                if kk == 1 and b == 3:
                                    ins.then_inc(spent[(2 * q + a) % RING], 1)
                                elif k == KD - 1 and b == 2 and a == 1:
                                    ins.then_inc(j_gu, 1)
                if not first:
                    pe.wait_ge(j_y, 2 * j)
                    for n in range(2):
                        if n:
                            pe.wait_ge(j_add, 4 * (j - 1) + 2)
                        scatter(j - 1, n)
                    pe.wait_ge(j_add, 4 * j)
                for tb in range(TB):
                    ins = M.transpose(ps[6][:, P * tb:P * tb + P], CW[:, tb, :], ident[:, :])
                ins.then_inc(j_ct, 1)
                pe.wait_ge(j_wt, j + 1)
                gather(j + 1)
                for a in range(2):
                    pe.wait_ge(j_a, 2 * j + a + 1)
                    if not first:
                        pe.wait_ge(j_y, 2 * j)
                    for k in range(4):
                        ins = M.transpose(ps[4 + a][:, P * k:P * k + P], aS[:, a, P * k:P * k + P], ident[:, :])
                    ins.then_inc(j_T, 1)
                pe.wait_ge(j_aT, 2 * j + 2)
                for q in range(2):
                    w = []
                    for a in range(2):
                        m = 8 + 2 * q + a
                        pe.wait_ge(landed[m % RING], 16 * (pre_count[m % RING] + REFILLS * j + m // RING + 1))
                        w.append(slot(m % RING).rearrange("p (k n) -> p k n", k=4))
                    for kk in range(4):
                        k = 4 * q + kk
                        for b in range(2):
                            for a in range(2):
                                r = slice(SLOTS * a, SLOTS * a + SLOTS)
                                ins = M.matmul(ps[4 + b][r, :], actT[:, k, r], w[a][:, kk, WIDE * b:WIDE * b + WIDE],
                                               start=(k == 0), stop=(k == KF - 1))
                                if kk == 3 and b == 1:
                                    ins.then_inc(spent[(8 + 2 * q + a) % RING], 1)
                                elif k == KF - 1 and b == 0 and a == 1:
                                    ins.then_inc(j_D, 1)

            def last(j):
                pe.wait_ge(j_y, 2 * j + 2)
                pe.wait_ge(j_hg, 2 * j + 4)
                for n in range(2):
                    if n:
                        pe.wait_ge(j_add, 4 * j + 2)
                    scatter(j, n)

            gather(0)
            job(0, first=True)
            with pe.Fori(1, PAIRS) as j:
                job(j)
            pe.wait_ge(s_flag, 1)
            more = pe.value_load(flag[0:1, 0:1], min_val=0, max_val=1)
            with pe.If(more > 0):
                with pe.Fori(PAIRS, ROUNDS * PAIRS) as j:
                    job(j)
                last(ROUNDS * PAIRS - 1)
            with pe.Else():
                last(PAIRS - 1)


_INS = ["x", "mem", "mix_norm", "w_in", "b_forget", "fox_q_gain", "fox_k_gain", "fox_out_gain",
        "gdn_conv_w", "gdn_a_log", "gdn_dt_bias", "gdn_out_gain", "w_out",
        "xattn_norm", "mem_norm", "w_xq", "w_xkv", "xq_gain", "xk_gain", "w_xo",
        "moe_norm", "w_router", "b_router", "w_gate_up", "b_gate_up", "w_down", "b_down"]


def kernel(**inputs):
    import numpy as _np
    import concourse.bacc as _bacc
    from concourse import mybir as _mybir
    from concourse.bass_utils import run_bass_kernel_spmd as _run

    nc = _bacc.Bacc("TRN2", target_bir_lowering=False, num_devices=1)
    arrays, args = {}, []
    for name in _INS:
        a = _np.ascontiguousarray(inputs[name])
        arrays[f"in_{name}_dram"] = a
        args.append(nc.dram_tensor(f"in_{name}_dram", a.shape, _mybir.dt.from_np(a.dtype), kind="ExternalInput").ap())
    o = nc.dram_tensor("out_0_dram", (1, T, D), F32, kind="ExternalOutput").ap()
    layer_kernel(nc, *args, o)
    r = _run(nc, [arrays], core_ids=[0])
    return r.results[0]["out_0_dram"]
```

```python
from contextlib import ExitStack

import concourse.bass as bass
from concourse import mybir

F32 = mybir.dt.float32
I32 = mybir.dt.int32
ALU = mybir.AluOpType
ACT = mybir.ActivationFunctionType
AX = mybir.AxisListType

P = 128
T = 256
TB = T // P
D = 1024
KD = D // P
EPS = 1e-6
FH, FD = 8, 64
GH, GD = 4, 128
CONV = 4
CHUNK = 64
XH, XD = 4, 256
NE, TOPK = 32, 4
F = 1024
KF = F // P
LIMIT, ALPHA = 7.0, 1.702
NEG = -1.0e30
SLOTS = 64
ROUNDS = T // SLOTS
PAIRS = NE // 2
LEVELS = [1, 2, 4, 8, 16, 32]

FQ, FK, FV, FF = 0, 512, 1024, 1536
GQ, GK, GV, GA, GB, GZ = 1544, 2056, 2568, 3080, 3084, 3088

WIDE = 512
SLOT = KD * WIDE
RING = 8
OWN = 6
PRE = 3
PRE_FILLS = 17
JOB_FILLS = 12


def layer_kernel(nc, x, mem, mix_norm, w_in, b_forget, fox_q_gain, fox_k_gain, fox_out_gain,
                 gdn_conv_w, gdn_a_log, gdn_dt_bias, gdn_out_gain, w_out,
                 xattn_norm, mem_norm, w_xq, w_xkv, xq_gain, xk_gain, w_xo,
                 moe_norm, w_router, b_router, w_gate_up, b_gate_up, w_down, b_down, out):
    ctx = ExitStack()
    with ctx:
        def sb(name, shape, dt=F32):
            return ctx.enter_context(nc.sbuf_tensor(name, shape, dt))

        def sem(name):
            return ctx.enter_context(nc.semaphore(name))

        ring = sb("ring", [P, OWN * SLOT])
        xs = sb("xs", [P, TB, D])
        hn = sb("hn", [P, TB, D])
        hT = sb("hT", [P, KD, T])
        mixT = sb("mixT", [P, KD, T])
        kvx = sb("kvx", [P, 4096])
        early = sb("early", [P, 4096])
        work = sb("work", [P, 7936])
        ident = sb("ident", [P, P])
        prefix = sb("prefix", [P, P])
        ones = sb("ones", [P, P])
        cprefix = sb("cprefix", [P, P])
        cones = sb("cones", [P, P])
        fmask = sb("fmask", [P, 2, P])
        dmask = sb("dmask", [P, P])
        lmask = sb("lmask", [P, len(LEVELS), P])
        slot_no = sb("slot_no", [P, SLOTS])
        pairsel = sb("pairsel", [2, P])
        gains = sb("gains", [P, 4, KD])
        fqk_gain = sb("fqk_gain", [P, 2])
        fout_gain = sb("fout_gain", [P, 4])
        gout_gain = sb("gout_gain", [P, 1])
        conv_w = sb("conv_w", [P, 12, CONV])
        gate_b = sb("gate_b", [P, 12])
        alog = sb("alog", [P, GH])
        brt = sb("brt", [P, NE])
        x_gain = sb("x_gain", [P, 2, 2])
        wsm = sb("wsm", [P, KD, 16])
        wr = sb("wr", [P, KD, NE])
        ss = sb("ss", [P, 8])
        rs = sb("rs", [P, 8])
        gv = sb("gv", [P, TB, 16])
        gabs = sb("gabs", [P, TB, 12])
        gln = sb("gln", [P, TB, 12])
        nlf = sb("nlf", [P, TB, FH])
        ncum = sb("ncum", [P, TB, FH])
        ea = sb("ea", [P, GH])
        gg = sb("gg", [P, TB, GH])
        beta = sb("beta", [P, TB, GH])
        gcum = sb("gcum", [P, TB, 2, GH])
        sc4 = sb("sc4", [P, TB, 3, GH])
        fmx = sb("fmx", [P, FH, 2])
        fsum = sb("fsum", [P, FH, 2])
        frs = sb("frs", [P, TB, FH])
        grs = sb("grs", [P, TB, GH])
        xmx = sb("xmx", [P, XH, 2])
        xsum = sb("xsum", [P, XH, 2])
        lg = sb("lg", [P, TB, NE])
        top8 = sb("top8", [P, TB, 8])
        rt = sb("rt", [P, TB, 4, NE])
        rcol = sb("rcol", [P, TB, 4])
        sel = sb("sel", [P, TB, NE])
        comb = sb("comb", [P, TB, NE])
        combT = sb("combT", [NE, T])
        posx = sb("posx", [P, TB, (ROUNDS + 1) * NE])
        combx = sb("combx", [P, TB, (ROUNDS + 1) * NE])
        flag_f = sb("flag_f", [P, 1])
        eps = sb("eps", [P, 1])
        flag = sb("flag", [P, 1], I32)

        ps = [ctx.enter_context(nc.psum_tensor(f"ps{i}", [P, WIDE], F32)) for i in range(8)]

        def cut(buf, base, *shape):
            n = 1
            for s in shape:
                n *= s
            v = buf[:, base:base + n]
            if len(shape) == 2:
                v = v.rearrange("p (a b) -> p a b", a=shape[0])
            if len(shape) == 3:
                v = v.rearrange("p (a b c) -> p a b c", a=shape[0], b=shape[1])
            return v

        kxT = cut(kvx, 0, KD, T)
        vx = cut(kvx, 2048, TB, D)
        mn = cut(early, 0, TB, D)
        mT = cut(early, 2048, KD, T)
        kbn = cut(early, 0, TB, GH, P)
        vb = cut(early, 1024, TB, GH, P)
        fqT = cut(work, 0, 4, T)
        fqz = mixT[:, :, :]
        fkT = cut(work, 1024, 4, T)
        fv = cut(work, 2048, TB, FH * FD)
        fS = cut(work, 3072, 2, 3 * P)
        fP = cut(work, 3840, 2, 3 * P)
        fPT = cut(work, 4608, 2, 3 * P)
        fo = cut(work, 5376, TB, FH * FD)
        sq = cut(work, 6400, 4, T)
        rn = cut(work, 7424, 2, T)
        G0 = PRE * SLOT
        raw = cut(ring, G0, 12, T + CONV - 1 + 1)
        cv = cut(ring, G0 + 3120, 12, T)
        gq, gk, gvT = (cv[:, 4 * i:4 * i + 4, :] for i in range(3))
        qd = gq
        kd = cut(ring, G0 + 3120 + 8 * T, TB, GH, P)
        zs = cut(ring, G0 + 6192, TB, GH * GD)
        expG = cut(ring, G0 + 7216, TB, GH, P)
        dec = cut(ring, G0 + 8240, TB, GH, P)
        AT = cut(ring, G0 + 9264, TB, GH, P)
        qkT = cut(ring, G0 + 10288, TB, GH, P)
        assert 11312 <= (OWN - PRE) * SLOT
        ATl = [cut(work, 0, TB, GH, P), cut(work, 1024, TB, GH, P)]
        Ti = cut(work, 2048, TB, GH, P)
        TiT = cut(work, 3072, TB, GH, P)
        Xi = cut(work, 4096, TB, GH, P)
        wTn = hn[:, 0, :].rearrange("p (t h c) -> p t h c", t=TB, h=GH)
        vnew = hn[:, 1, :].rearrange("p (t n) -> p t n", t=TB)
        St = cut(ring, G0 + 0, GH, P)
        Sd = cut(ring, G0 + 512, GH, P)
        go = cut(ring, G0 + 1024, TB, GH * GD)
        gsq = cut(ring, G0 + 2048, 1, GH * GD)
        qxT = cut(work, 0, KD, T)
        xP = cut(work, 2048, XH, 2 * T)
        xPT = cut(work, 4096, 2, 2 * T)
        hgT = cut(work, 0, KD, P)
        actT = cut(work, 1024, KF, P)
        gS = cut(work, 2048, 2, WIDE)
        uS = cut(work, 3072, 2, WIDE)
        sS = cut(work, 4096, 2, WIDE)
        aS = cut(work, 5120, 2, WIDE)
        yS = cut(work, 6144, 2, WIDE)
        WT = cut(work, 7168, TB, P)
        Sel = cut(work, 7424, TB, P)
        CW = cut(work, 7680, TB, P)
        bgu = mixT[0:2, :, :].rearrange("p a t -> p (a t)")
        bdn = work[0:NE, 1024:1024 + D]

        landed = [sem(f"landed{i}") for i in range(RING)]
        spent = [sem(f"spent{i}") for i in range(RING)]
        full = [sem(f"full{i}") for i in range(8)]
        free = [sem(f"free{i}") for i in range(8)]
        s_mem, s_x = sem("mem_loaded"), [sem(f"x_loaded{tb}") for tb in range(TB)]
        s_par, s_par2 = sem("params_loaded"), sem("gate_weights_loaded")
        s_bgu = sem("expert_bias_loaded")
        s_const = sem("constants_built")
        s_gc = sem("pool_step")
        s_lvl = sem("level_masked")
        s_dv, s_ac = sem("dve_step"), sem("act_step")
        s_ss, s_hn, s_hT = sem("squares_summed"), sem("rows_normalised"), sem("transposed")
        s_raw, s_sq, s_nrm = sem("projection_copied"), sem("squared"), sem("head_normed")
        s_tok = sem("token_values_copied")
        s_gv, s_gln, s_nlf = (sem(n) for n in (
            "gates_in", "gates_logged", "gates_done"))
        s_fs, s_fp, s_fpt, s_fo, s_mix = (sem(n) for n in (
            "fox_scores", "fox_probs", "fox_probs_turned", "fox_out", "mixed"))
        s_conv, s_silu = sem("conv_done"), sem("silu_done")
        s_garg, s_dec, s_kop, s_AT = (sem(n) for n in (
            "decay_argument", "decays_done", "gdn_operands", "gdn_matrices"))
        s_X, s_T, s_w = sem("inverse_product"), sem("inverse_level"), sem("gdn_w")
        s_vn, s_S, s_go, s_gsq = sem("gdn_vnew"), sem("gdn_state"), sem("gdn_out"), sem("gdn_squares")
        s_res = sem("residual_added")
        s_xm, s_xe, s_xp, s_xpt, s_xo = (sem(n) for n in (
            "xattn_max", "xattn_exp", "xattn_probs", "xattn_probs_turned", "xattn_out"))
        s_lg, s_re, s_sel, s_comb, s_combT, s_pos = (sem(n) for n in (
            "logits", "router_exp", "selected", "combine_weights", "combine_turned", "positions"))
        s_flag = sem("overflow_flag")
        j_sel, j_wt, j_hg, j_bias, j_gu = (sem(n) for n in (
            "job_selection", "job_weights_turned", "job_rows_gathered", "job_bias_used", "job_gate_up"))
        j_g, j_u, j_sg, j_a, j_T, j_aT = (sem(n) for n in (
            "job_gate", "job_up", "job_sigmoid", "job_act", "job_act_turn", "job_act_turned"))
        j_D, j_y, j_sc, j_add, j_ga, j_ct = (sem(n) for n in (
            "job_down", "job_rows_out", "job_scattered", "job_added", "job_gather", "job_weights_turn"))
        j_t = sem("job_product")
        s_pv, s_os, s_T0, s_bdn = (sem(n) for n in (
            "fox_values_used", "gdn_state_read", "inverse_start", "down_bias_loaded"))
        s_ident, s_gain = sem("identity_built"), sem("norm_gains_loaded")
        s_arg, s_root = sem("root_argument"), sem("root_taken")
        s_out = sem("stored")

        turn = {}
        uses = [0] * 8

        def plan(name, bank):
            turn[name] = (bank, uses[bank])
            uses[bank] += 1

        rot = [0]

        def plan_next(*names):
            for n in names:
                plan(n, rot[0] % 8)
                rot[0] += 1

        plan_next(*[f"xT{i}" for i in range(4)])
        plan_next("gate0", "gate1")
        plan_next("fq0", "fq1")
        plan_next(*[f"mT{i}" for i in range(4)])
        plan_next("fqs0", "fqs1", "fk0", "fk1", "cumT0", "cumT1", "fks0", "fks1", "fv0", "fv1")
        for h in range(FH + 2):
            if h < FH:
                if h % 2 == 0:
                    plan(f"fcum{h // 2}", 6 + h // 2 % 2)
                plan(f"fS{h}", h % 2)
            if 1 <= h <= FH:
                plan(f"fPT{h - 1}", 2 + (h - 1) % 2)
        plan("fo0", 4)
        plan("fo1", 5)
        rot[0] = 0
        plan_next("GS0", "GS1", "GB0", "GB1", "bB0", "bB1")
        plan_next(*[f"gr{i}" for i in range(5)])
        plan_next("gs0", "gs1", "gr5", "gs2", "gs3")
        plan_next("z0", "z1", "fT0", "fT1", "kx0", "kx1")
        plan_next("kk0", "kk1", "ktok0", "vtok0", "ktok1", "vtok1", "qk0", "qk1")
        plan_next("kxs0", "kxs1", "X0_0", "X0_1", "kx2", "kx3", "kxs2", "kxs3")
        for n in range(len(LEVELS)):
            if n:
                plan(f"X{n}_0", 0)
                plan(f"X{n}_1", 1)
            if n > 0:
                for tb in range(TB):
                    if n < len(LEVELS) - 1:
                        plan(f"Y{n}_{tb}", 2 + tb)
                    plan(f"YT{n}_{tb}", 4 + tb)
        plan("w0", 6)
        plan("w1", 7)
        plan("vx0", 6)
        plan("vx1", 7)
        for c in range(4):
            plan(f"vn{c}", c % 2)
            if c % 2 == 0:
                plan(f"go{c // 2}", 4 + c // 2)
            if c < 3:
                plan(f"S{c}", 2 + c % 2)
        plan("gT0", 6)
        plan("gT1", 7)
        rot[0] = 0
        plan_next(*[f"wo{i}" for i in range(4)])
        plan_next("vx2", "vx3")
        plan_next(*[f"h2T{i}" for i in range(4)])
        plan_next("qx0", "qx1", "qx2", "qxs0", "qxs1", "qx3", "qxs2", "qxs3")
        for h in range(XH):
            plan(f"xS{h}", (0, 1, 6, 7)[h])
            plan(f"xPT{h}", 2 + h % 2)
            plan(f"xO{h}", 4 + h % 2)
        rot[0] = 0
        plan_next(*[f"xo{i}" for i in range(4)])
        plan_next(*[f"h3T{i}" for i in range(4)])
        plan_next("lg0", "lg1")
        plan("rank0", 0)
        plan("rank1", 1)
        plan("cnt", 2)
        plan("cT", 3)
        for i in range(4):
            plan(f"bd{i}", 4 + i % 2)

        def into(pe, name):
            bank, before = turn[name]
            if before:
                pe.wait_ge(free[bank], before)
            return ps[bank]

        def filled(ins, name):
            ins.then_inc(full[turn[name][0]], 1)

        def bank_of(eng, name):
            bank, before = turn[name]
            eng.wait_ge(full[bank], before + 1)
            return ps[bank]

        def read(ins, name):
            ins.then_inc(free[turn[name][0]], 1)

        dma_gates = [w_in[0].rearrange("(p k) n -> p k n", k=KD)]
        w_in_v = dma_gates[0]
        xkv_v = w_xkv[0].rearrange("(p k) n -> p k n", k=KD)
        xq_v = w_xq[0].rearrange("(p k) n -> p k n", k=KD)
        out_v = w_out[0].rearrange("(k p) n -> p k n", p=P)
        xo_v = w_xo[0].rearrange("(k p) n -> p k n", p=P)
        pre_fills = ([w_in_v[:, :, c:c + WIDE] for c in (FQ, FK, FV, GQ, GK, GV, GZ)]
                     + [xkv_v[:, :, WIDE * c:WIDE * c + WIDE] for c in range(3)]
                     + [out_v[:, :, WIDE * c:WIDE * c + WIDE] for c in range(2)]
                     + [xkv_v[:, :, 3 * WIDE:4 * WIDE]]
                     + [xq_v[:, :, WIDE * c:WIDE * c + WIDE] for c in range(2)]
                     + [xo_v[:, :, WIDE * c:WIDE * c + WIDE] for c in range(2)])
        assert len(pre_fills) == PRE_FILLS
        last_bank = ["fq1", "fk1", "fv1", "gr1", "gr3", "gr5", "z1", "kx1", "kx3", "vx1",
                     "wo1", "wo3", "vx3", "qx1", "qx3", "xo1", "xo3"]
        pre_count = [len(range(s, PRE_FILLS, PRE)) if s < PRE else 0 for s in range(RING)]

        def slot(s):
            if s < OWN:
                return ring[:, s * SLOT:(s + 1) * SLOT]
            return (early, kvx)[s - OWN][:, :]

        block = ctx.enter_context(nc.Block())

        def pre_w(pe, f):
            pe.wait_ge(landed[f % PRE], 16 * (f // PRE + 1))
            return slot(f % PRE).rearrange("p (k n) -> p k n", k=KD)

        def full_of(name):
            return full[turn[name][0]], turn[name][1] + 1

        def free_of(name):
            return free[turn[name][0]], turn[name][1] + 1

        gu_v = w_gate_up[0].rearrange("e (p k) n -> e p k n", k=KD)
        dn_v = w_down[0].rearrange("e (k p) n -> e p k n", p=P)

        job_fills = [(a, "gu", q) for q in range(4) for a in range(2)] + \
                    [(a, "dn", q) for q in range(2) for a in range(2)]
        TURNS = 2 * JOB_FILLS // RING

        def slot_of(p, m):
            return (JOB_FILLS * p + m) % RING

        def fills_before(i, p, m):
            return TURNS * i + (JOB_FILLS * p + m) // RING

        def gate_up_end(i, p):
            return spent[slot_of(p, 7)], fills_before(i, p, 7) + 1

        def down_end(i, p):
            return spent[slot_of(p, 11)], fills_before(i, p, 11) + 1

        @block.sync
        def _(sp):
            def pre_fill(f):
                if f >= PRE:
                    sp.wait_ge(*full_of(last_bank[f - PRE]))
                sp.dma_start(slot(f % PRE).rearrange("p (k n) -> p k n", k=KD), pre_fills[f]).then_inc(landed[f % PRE], 16)

            def expert_fill(i, p, m, pair, fresh=False):
                a, kind, q = job_fills[m]
                s = slot_of(p, m)
                if not fresh:
                    sp.wait_ge(spent[s], fills_before(i, p, m))
                e = 2 * pair + a
                view, nk = (gu_v, 2) if kind == "gu" else (dn_v, 4)
                if isinstance(e, int):
                    src = view[e, :, nk * q:nk * q + nk, :]
                else:
                    src = view[bass.ds(e, 1), :, nk * q:nk * q + nk, :].rearrange("e p k n -> p (e k) n")
                sp.dma_start(slot(s).rearrange("p (k n) -> p k n", k=nk), src).then_inc(landed[s], 16)

            def job(i, p, pair):
                sp.wait_ge(j_bias, 2 * i + p)
                sp.dma_start(bgu, b_gate_up[0, bass.ds(2 * pair, 2), :]).then_inc(s_bgu, 16)
                for m in range(JOB_FILLS):
                    expert_fill(i, p, m, pair)

            out_v = out[0].rearrange("(t p) d -> p t d", p=P)

            def store(jobs):
                for n in range(2):
                    sp.wait_ge(j_add, 4 * jobs - 2 + 2 * n)
                    c = slice(WIDE * n, WIDE * n + WIDE)
                    sp.dma_start(out_v[:, :, c], xs[:, :, c]).then_inc(s_out, 16)

            def load(dst, src, s=s_par):
                sp.dma_start(dst, src, allow_slow_non_contiguous=True).then_inc(s, 16)

            for tb in range(TB):
                load(xs[:, tb, :], x[0, P * tb:P * tb + P, :], s_x[tb])
            for tb in range(TB):
                sp.wait_ge(s_x[tb], 16)
            pre_fill(0)
            load(mn, mem[0].rearrange("(t p) d -> p t d", p=P), s_mem)
            for i, g in enumerate((fox_q_gain, fox_k_gain)):
                load(fqk_gain[0:FD, i:i + 1], g[0].rearrange("(p o) -> p o", o=1))
                load(fqk_gain[FD:P, i:i + 1], g[0].rearrange("(p o) -> p o", o=1))
            load(fout_gain[:, :], fox_out_gain[0].rearrange("(j a) d -> (a d) j", a=2))
            load(gout_gain[:, :], gdn_out_gain[0].rearrange("(p o) -> p o", o=1))
            load(conv_w[:, :, :], gdn_conv_w[0].rearrange("(j p) k -> p j k", p=P))
            load(gate_b[:, 0:FH], b_forget[0:1, :].to_broadcast([P, FH]))
            load(gate_b[:, FH:12], gdn_dt_bias[0:1, :].to_broadcast([P, GH]))
            load(alog[:, :], gdn_a_log[0:1, :].to_broadcast([P, GH]))
            load(brt[:, :], b_router[0:1, :].to_broadcast([P, NE]))
            for i, g in enumerate((xq_gain, xk_gain)):
                load(x_gain[:, i, :], g[0].rearrange("(j p) -> p j", p=P))
            load(wr[:, :, :], w_router[0].rearrange("(p k) n -> p k n", k=KD))
            for f in range(1, PRE_FILLS - 3):
                pre_fill(f)
            sp.wait_ge(*free_of("gT1"))
            for m in range(PRE, OWN):
                expert_fill(0, 0, m, 0, fresh=True)
            for f in range(PRE_FILLS - 3, PRE_FILLS):
                pre_fill(f)
            for m, name in ((6, "vx3"), (2, "qx3"), (7, f"xO{XH - 1}"), (0, "xo1"), (1, "xo3")):
                sp.wait_ge(*full_of(name))
                if m == 1:
                    sp.dma_start(bgu, b_gate_up[0, 0:2, :]).then_inc(s_bgu, 16)
                expert_fill(0, 0, m, 0, fresh=True)
                if m == 7:
                    sp.dma_start(bdn, b_down[0]).then_inc(s_bdn, 16)
            for m in range(RING, JOB_FILLS):
                expert_fill(0, 0, m, 0)
            job(0, 1, 1)
            with sp.Fori(1, PAIRS // 2) as i:
                for p in range(2):
                    job(i, p, 2 * i + p)
            sp.wait_ge(s_flag, 1)
            more = sp.value_load(flag[0:1, 0:1], min_val=0, max_val=1)
            with sp.If(more > 0):
                with sp.Fori(1, ROUNDS) as r:
                    with sp.Fori(0, PAIRS // 2) as i:
                        for p in range(2):
                            job(r * (PAIRS // 2) + i, p, 2 * i + p)
                store(ROUNDS * PAIRS)
            with sp.Else():
                store(PAIRS)
            sp.wait_ge(s_out, 16 * 2)

        @block.gpsimd
        def _(pool):
            steps = [0]

            def step(ins):
                steps[0] += 1
                ins.then_inc(s_gc, 1)
                pool.wait_ge(s_gc, steps[0])

            def keep(out_, pattern, base, mult, fill, op=ALU.is_ge):
                step(pool.affine_select(out=out_, in_=out_, compare_op=op, fill=fill, base=base,
                                        pattern=pattern, channel_multiplier=mult))

            step(pool.memset(ident[:, :], 0.0))
            step(pool.memset(eps[:, :], EPS))
            keep(ident[:, :], [[-1, P]], 0, 1, 1.0, ALU.not_equal)
            pool.memset(fqz, 0.0).then_inc(s_ident, 1)
            step(pool.memset(ones[:, :], 1.0))
            step(pool.memset(prefix[:, :], 1.0))
            keep(prefix[:, :], [[1, P]], 0, -1, 0.0)
            step(pool.memset(cones[:, :], 0.0))
            step(pool.memset(cones[0:CHUNK, 0:CHUNK], 1.0))
            step(pool.memset(cones[CHUNK:P, CHUNK:P], 1.0))
            step(pool.tensor_tensor(cprefix[:, :], cones[:, :], prefix[:, :], ALU.mult))
            step(pool.memset(fmask[:, :, :], 0.0))
            keep(fmask[:, 1, :], [[-1, P]], 0, 1, NEG)
            step(pool.tensor_scalar(dmask[:, :], cprefix[:, :], -NEG, NEG, ALU.mult, ALU.add))
            step(pool.memset(lmask[:, :, :], 0.0))
            for n, w in enumerate(LEVELS):
                nb = P // (2 * w)
                upper = lmask[:, n, :].rearrange("p (b u w) -> p b u w", b=nb, u=2)[:, :, 1, :]
                step(pool.memset(upper, 1.0))
                keep(upper, [[-2 * w, nb], [0, w]], 0, 1, 0.0)
                keep(upper, [[2 * w, nb], [0, w]], w - 1, -1, 0.0)
            step(pool.iota(slot_no[:, :], pattern=[[1, SLOTS]], base=0, channel_multiplier=0,
                           allow_small_or_imprecise_dtypes=True))
            step(pool.memset(pairsel[:, :], 1.0))
            keep(pairsel[:, :], [[-1, P]], SLOTS - 1, SLOTS, 0.0)
            keep(pairsel[:, :], [[1, P]], 0, -SLOTS, 0.0)
            pool.memset(raw[:, :, 0:CONV - 1], 0.0).then_inc(s_const, 1)

            for n in range(len(LEVELS)):
                if n == 2:
                    pool.wait_ge(s_T0, 2)
                for tb in range(TB):
                    if n == 0:
                        pool.wait_ge(s_fo, TB)
                        pool.wait_ge(*free_of(f"kk{tb}"))
                        pool.wait_ge(*free_of(f"fT{tb}"))
                    if n >= 2:
                        pool.wait_ge(*full_of(f"X{n - 2}_{tb}"))
                    pool.tensor_tensor(ATl[n % 2][:, tb, :, :], AT[:, tb, :, :],
                                       lmask[:, n:n + 1, :].to_broadcast([P, GH, P]), ALU.mult).then_inc(s_lvl, 1)

        @block.scalar
        def _(act):
            def load(dst, src, s):
                act.dma_start(dst, src, allow_slow_non_contiguous=True).then_inc(s, 16)

            for i, g in enumerate((mix_norm, mem_norm, xattn_norm, moe_norm)):
                load(gains[:, i, :], g[0].rearrange("(p k) -> p k", k=KD), s_gain)
            load(wsm[:, :, 0:8], w_in_v[:, :, FF:FF + 8], s_par2)
            load(wsm[:, :, 8:16], w_in_v[:, :, GA:GA + 8], s_par2)

            steps = [0]

            def link(ins):
                steps[0] += 1
                ins.then_inc(s_ac, 1)
                act.wait_ge(s_ac, steps[0])


            def root(dst, src, n):
                return act.activation(dst, src, ACT.Sqrt, scale=1.0 / n, bias=eps[:, 0:1])

            squares = [0]

            def root_mean_squares(src, junk, cols, arrived):
                for tb in range(TB):
                    for s, v in arrived[tb]:
                        act.wait_ge(s, v)
                    c = slice(cols + tb, cols + tb + 1)
                    act.activation(junk[:, tb, :], src[:, tb, :], ACT.Square, accum_out=ss[:, c]).then_inc(s_ss, 1)
                    squares[0] += 1
                    act.wait_ge(s_ss, squares[0])
                    root(rs[:, c], ss[:, c], D).then_inc(s_root, 1)

            def head_roots(name, i, n, before, tiles=2):
                b = bank_of(act, f"{name}{i}")
                if before > 0:
                    act.wait_ge(s_nrm, before)
                r = rn[:, :, :] if tiles == 2 else rn[:, i % 2:i % 2 + 1, :]
                read(root(r, b[:, 0:tiles * T].rearrange("p (a t) -> p a t", a=tiles), n), f"{name}{i}")

            act.wait_ge(s_ident, 1)
            junk = cut(kvx, 0, TB, D)
            root_mean_squares(xs, junk, 2, [[(s_x[tb], 16)] for tb in range(TB)])
            root_mean_squares(mn, junk, 0, [[(s_mem, 16)], []])

            def project(name, dst, banks, sq_read, raws):
                for i in banks:
                    b = bank_of(act, f"{name}{i}")[:, :].rearrange("p (a t) -> p a t", a=2)
                    act.activation(dst[:, 2 * i:2 * i + 2, :], b, ACT.Copy).then_inc(s_raw, 1)
                    if sq_read[i] is not None:
                        s, v = sq_read[i]
                        act.wait_ge(s, v)
                    act.wait_ge(s_raw, raws + i + 1)
                    ins = act.activation(sq[:, 2 * (i % 2):2 * (i % 2) + 2, :], b, ACT.Square)
                    read(ins, f"{name}{i}")

            act.wait_ge(s_gv, 2)
            act.wait_ge(*free_of("gate0"))
            act.wait_ge(*free_of("gate1"))
            link(act.activation(gabs[:, :, :], gv[:, :, 0:12], ACT.Abs))
            link(act.activation(gabs[:, :, :], gabs[:, :, :], ACT.Exp, scale=-1.0))
            act.activation(gln[:, :, :], gabs[:, :, :], ACT.Ln, bias=1.0).then_inc(s_gln, 1)
            act.activation(beta[:, :, :], gv[:, :, 12:16], ACT.Exp, scale=-1.0).then_inc(s_gln, 1)
            act.wait_ge(s_par, 16 * 14)
            act.activation(ea[:, :], alog[:, :], ACT.Exp).then_inc(s_gln, 1)
            project("fq", fqT, range(2), [None, None], 0)
            for i in range(2):
                head_roots("fqs", i, FD, i)
            project("fk", fkT, range(2), [full_of("fqs0"), full_of("fqs1")], 2)
            for i in range(2):
                head_roots("fks", i, FD, 2 + i)
            for i in range(2):
                b = bank_of(act, f"fv{i}")
                read(act.activation(fv[:, i, :], b[:, :], ACT.Copy), f"fv{i}")

            for h in range(FH + 1):
                if h < FH:
                    act.wait_ge(s_fs, 2 * h + 2)
                    if h >= 2:
                        act.wait_ge(*full_of(f"fPT{h - 2}"))
                    act.activation(fP[:, h % 2, 0:P], fS[:, h % 2, 0:P], ACT.Exp, bias=fmx[:, h, 0:1],
                                   accum_out=fsum[:, h, 0:1]).then_inc(s_fp, 1)
                    act.activation(fP[:, h % 2, P:3 * P], fS[:, h % 2, P:3 * P], ACT.Exp, bias=fmx[:, h, 1:2],
                                   accum_out=fsum[:, h, 1:2]).then_inc(s_fp, 1)
                if h >= 1:
                    b = bank_of(act, f"fPT{h - 1}")
                    if h >= 3:
                        act.wait_ge(s_pv, h - 2)
                    ins = act.activation(fPT[:, (h - 1) % 2, :], b[:, 0:3 * P], ACT.Copy)
                    read(ins, f"fPT{h - 1}")

            for tb in range(TB):
                act.wait_ge(s_arg, tb + 1)
                root(frs[:, tb, :], frs[:, tb, :], FD).then_inc(s_root, 1)

            act.wait_ge(s_garg, 1)
            act.activation(sc4[:, :, 0, :], gcum[:, :, 0, :], ACT.Exp).then_inc(s_dec, 1)
            act.activation(sc4[:, :, 2, :], sc4[:, :, 2, :], ACT.Exp).then_inc(s_dec, 1)
            for tb in range(TB):
                act.wait_ge(s_garg, 2 + tb)
                b = bank_of(act, f"GB{tb}")
                read(act.activation(expG[:, tb, :, :], b[:, :].rearrange("p (h c) -> p h c", h=GH), ACT.Exp), f"GB{tb}")
                act.activation(dec[:, tb, :, :], dec[:, tb, :, :], ACT.Exp).then_inc(s_dec, 1)
            def raw_in(i):
                b = bank_of(act, f"gr{i}")[:, :].rearrange("p (a t) -> p a t", a=2)
                read(act.activation(raw[:, 2 * i:2 * i + 2, CONV - 1:CONV - 1 + T], b, ACT.Copy), f"gr{i}")

            def silu(i):
                act.wait_ge(s_conv, 4 * i + 4)
                act.activation(cv[:, 4 * i:4 * i + 4, :], cv[:, 4 * i:4 * i + 4, :], ACT.Silu).then_inc(s_silu, 1)

            for i in range(4):
                raw_in(i)
            for i in range(4):
                if i % 2 == 0:
                    silu(i // 2)
                    act.wait_ge(s_silu, i // 2 + 1)
                if i == 0:
                    act.wait_ge(s_fo, TB)
                if i >= 2:
                    act.wait_ge(*full_of(f"gs{i - 2}"))
                act.activation(sq[:, 2 * (i % 2):2 * (i % 2) + 2, :], cv[:, 2 * i:2 * i + 2, :], ACT.Square).then_inc(s_sq, 1)
                if i % 2:
                    raw_in(4 + i // 2)
            for i in range(4):
                head_roots("gs", i, 1.0, 4 + i)
            silu(2)
            for i in range(2):
                b = bank_of(act, f"z{i}")
                read(act.activation(zs[:, i, :], b[:, :], ACT.Silu), f"z{i}")
            for i0 in (0, 2):
                project("kx", kxT, range(i0, i0 + 2), [full_of("gs2"), full_of("gs3"), full_of("kxs0"), full_of("kxs1")], 4)
                for i in (i0, i0 + 1):
                    head_roots("kxs", i, XD, max(8, 8 + i - 1), tiles=1)
            for n in range(1, len(LEVELS)):
                for tb in range(TB):
                    b = bank_of(act, f"X{n}_{tb}")
                    if n >= 2:
                        act.wait_ge(*full_of(f"YT{n - 1}_{tb}"))
                    read(act.activation(Xi[:, tb, :, :], b[:, :].rearrange("p (h c) -> p h c", h=GH), ACT.Copy), f"X{n}_{tb}")
            for tb in range(TB):
                b = bank_of(act, f"w{tb}")
                read(act.activation(wTn[:, tb, :, :], b[:, :].rearrange("p (h c) -> p h c", h=GH), ACT.Copy), f"w{tb}")
            def memory_values(i):
                b = bank_of(act, f"vx{i}")
                read(act.activation(vx[:, i % 2, WIDE * (i // 2):WIDE * (i // 2) + WIDE], b[:, :], ACT.Copy), f"vx{i}")

            memory_values(0)
            memory_values(1)
            for tb in range(TB):
                b = bank_of(act, f"go{tb}")
                act.activation(gsq[:, 0, :], b[:, :], ACT.Square).then_inc(s_gsq, 1)
                act.wait_ge(s_gsq, 2 * tb + 2)
                root(grs[:, tb, :], grs[:, tb, :], GD).then_inc(s_root, 1)

            root_mean_squares(xs, cut(work, 0, TB, D), 0, [[free_of(f"wo{tb}"), free_of(f"wo{2 + tb}")] for tb in range(TB)])
            memory_values(2)
            memory_values(3)
            qx_read = [full_of("kxs2"), full_of("kxs3"), full_of("qxs0"), full_of("qxs1")]
            project("qx", qxT, range(2), qx_read, 8)
            for i in range(4):
                if i < 2:
                    head_roots("qxs", i, XD, 12 + i - 1, tiles=1)
                    project("qx", qxT, [2 + i], qx_read, 8)
            for i in range(2, 4):
                head_roots("qxs", i, XD, 12 + i - 1, tiles=1)

            def exps(h):
                act.wait_ge(s_xm, h + 1)
                b = bank_of(act, f"xS{h}")[:, :].rearrange("p (a t) -> p a t", a=2)
                for qb in range(2):
                    ins = act.activation(xP[:, h, T * qb:T * qb + T], b[:, qb, :], ACT.Exp, scale=XD ** -0.5,
                                         bias=xmx[:, h, qb:qb + 1], accum_out=xsum[:, h, qb:qb + 1])
                    if qb:
                        read(ins, f"xS{h}")
                    else:
                        ins.then_inc(s_xe, 1)

            def turned_probs(h):
                b = bank_of(act, f"xPT{h}")
                if h >= 2:
                    act.wait_ge(*full_of(f"xO{h - 2}"))
                read(act.activation(xPT[:, h % 2, :], b[:, :], ACT.Copy), f"xPT{h}")

            def outputs(h):
                b = bank_of(act, f"xO{h}")[:, :].rearrange("p (a t) -> p a t", a=2)
                read(act.activation(mixT[:, 2 * h:2 * h + 2, :], b, ACT.Copy), f"xO{h}")

            for step, h in (("S", 0), ("S", 1), ("S", 2), ("T", 0), ("S", 3), ("T", 1), ("O", 0), ("T", 2), ("O", 1),
                            ("T", 3), ("O", 2), ("O", 3)):
                if step == "S":
                    exps(h)
                elif step == "T":
                    turned_probs(h)
                else:
                    outputs(h)

            root_mean_squares(xs, cut(work, 2048, TB, D), 4, [[free_of(f"xo{tb}"), free_of(f"xo{2 + tb}")] for tb in range(TB)])
            for tb in range(TB):
                act.wait_ge(s_lg, tb + 1)
                act.activation(rt[:, tb, 3, :], lg[:, tb, :], ACT.Exp, bias=rcol[:, tb, 3:4]).then_inc(s_re, 1)

            def job(i, p):
                j = 2 * i + p
                for a in range(2):
                    act.wait_ge(j_g, 2 * j + a + 1)
                    act.activation(sS[:, a, :], gS[:, a, :], ACT.Sigmoid, scale=ALPHA).then_inc(j_sg, 1)
                for a in range(2):
                    act.wait_ge(j_T, 2 * j + a + 1)
                    act.activation(actT[:, 4 * a:4 * a + 4, :], ps[a][:, :].rearrange("p (k s) -> p k s", k=4),
                                   ACT.Copy).then_inc(j_aT, 1)
                for a in range(2):
                    if a == 0:
                        act.wait_ge(j_D, j + 1)
                    else:
                        act.wait_ge(*down_end(i, p))
                    act.activation(yS[:, a, :], ps[4 + a][:, :], ACT.Copy).then_inc(j_y, 1)

            def jobs(i0, i1):
                with act.Fori(i0, i1) as i:
                    job(i, 1)
                    job(i + 1, 0)

            job(0, 0)
            jobs(0, PAIRS // 2 - 1)
            act.wait_ge(s_flag, 1)
            more = act.value_load(flag[0:1, 0:1], min_val=0, max_val=1)
            with act.If(more > 0):
                jobs(PAIRS // 2 - 1, ROUNDS * PAIRS // 2 - 1)
                job(ROUNDS * PAIRS // 2 - 1, 1)
            with act.Else():
                job(PAIRS // 2 - 1, 1)

        @block.vector
        def _(dve):
            V = nc.vector
            steps = [0]

            def link(ins):
                steps[0] += 1
                ins.then_inc(s_dv, 1)
                dve.wait_ge(s_dv, steps[0])

            rooted = [0]

            def root_wait():
                rooted[0] += 1
                dve.wait_ge(s_root, rooted[0])


            def norm_rows(src, dst, cols, blocks=range(TB)):
                for tb in blocks:
                    root_wait()
                    r = rs[:, cols + tb:cols + tb + 1]
                    link(V.reciprocal(r, r))
                    V.tensor_scalar(dst[:, tb, :], src[:, tb, :], r, None, ALU.mult).then_inc(s_hn, 1)

            def turned(name, dst, gain, banks=range(4)):
                for i in banks:
                    q, tb = i % 2, i // 2
                    b = bank_of(dve, f"{name}{i}")[:, :].rearrange("p (k t) -> p k t", k=4)
                    ins = V.tensor_tensor(dst[:, 4 * q:4 * q + 4, P * tb:P * tb + P], b,
                                          gains[:, gain, 4 * q:4 * q + 4].unsqueeze(2).to_broadcast([P, 4, P]), ALU.mult)
                    read(ins, f"{name}{i}")

            norm_rows(xs, hn, 2)
            dve.wait_ge(s_gain, 16 * 4)
            turned("xT", hT, 0)
            norm_rows(mn, mn, 0)
            dve.wait_ge(s_par, 16 * 14)

            for tb in range(TB):
                b = bank_of(dve, f"gate{tb}")
                V.tensor_tensor(gv[:, tb, 0:12], b[:, 0:12], gate_b[:, :], ALU.add).then_inc(s_gv, 1)
                read(V.tensor_copy(gv[:, tb, 12:16], b[:, 12:16]), f"gate{tb}")
            def head_norm(name, i, dst, gain, tiles, root):
                dve.wait_ge(*free_of(f"{name}{i}"))
                r = rn[:, :, :] if tiles == 1 else rn[:, i % 2:i % 2 + 1, :]
                link(V.reciprocal(r, r))
                for c in range(tiles):
                    n = 2 // tiles
                    d = dst[:, 2 * i + c:2 * i + c + n, :]
                    ins = V.scalar_tensor_tensor(d, d, gain[c], r, ALU.mult, ALU.mult)
                    if c == tiles - 1:
                        ins.then_inc(s_nrm, 1)
                        dve.wait_ge(s_nrm, root)
                    else:
                        link(ins)

            dve.wait_ge(s_gln, 3)
            link(V.tensor_scalar(nlf[:, :, :], gv[:, :, 0:8], -1.0, 0.0, ALU.mult, ALU.max))
            V.tensor_tensor(nlf[:, :, :], nlf[:, :, :], gln[:, :, 0:8], ALU.add).then_inc(s_nlf, 1)
            link(V.tensor_scalar(gg[:, :, :], gv[:, :, 8:12], 0.0, None, ALU.max))
            link(V.tensor_tensor(gg[:, :, :], gg[:, :, :], gln[:, :, 8:12], ALU.add))
            link(V.scalar_tensor_tensor(gg[:, :, :], gg[:, :, :], -1.0,
                                        ea[:, :].unsqueeze(1).to_broadcast([P, TB, GH]), ALU.mult, ALU.mult))
            link(V.tensor_scalar(beta[:, :, :], beta[:, :, :], 1.0, None, ALU.add))
            V.reciprocal(beta[:, :, :], beta[:, :, :]).then_inc(s_nlf, 1)
            dve.wait_ge(s_nlf, 2)
            turned("mT", mT, 1)
            for i in range(2):
                dve.wait_ge(*free_of(f"fqs{i}"))
                link(V.reciprocal(rn[:, :, :], rn[:, :, :]))
                for half in range(2):
                    r = slice(FD * half, FD * half + FD)
                    d = fqz.rearrange("p (t a) n -> p t a n", a=2)[r, 2 * i:2 * i + 2, half, :]
                    ins = V.scalar_tensor_tensor(d, fqT[r, 2 * i:2 * i + 2, :], fqk_gain[r, 0:1], rn[r, :, :],
                                                 ALU.mult, ALU.mult)
                    if half:
                        ins.then_inc(s_nrm, 1)
                        dve.wait_ge(s_nrm, i + 1)
                    else:
                        link(ins)
            for i in range(2):
                head_norm("fks", i, fkT, [fqk_gain[:, 1:2]], 1, 3 + i)
            for tb in range(TB):
                b = bank_of(dve, f"cumT{tb}")
                read(V.tensor_copy(ncum[:, tb, :], b[:, 0:FH]), f"cumT{tb}")

            dve.wait_ge(s_const, 1)
            dve.wait_ge(free[turn["cumT1"][0]], turn["cumT1"][1] + 1)
            dve.wait_ge(free[turn["cumT0"][0]], turn["cumT0"][1] + 1)
            for h in range(FH):
                S = fS[:, h % 2, :]
                if h >= 2:
                    dve.wait_ge(s_fp, 2 * (h - 1))
                b = bank_of(dve, f"fcum{h // 2}")[:, T * (h % 2):T * (h % 2) + T]
                link(V.scalar_tensor_tensor(S[:, 0:P], b[:, 0:P], ncum[:, 0, h:h + 1], fmask[:, 1, :],
                                            ALU.subtract, ALU.add))
                ins = V.scalar_tensor_tensor(S[:, P:3 * P], b, ncum[:, 1, h:h + 1],
                                             fmask[:, :, :].rearrange("p a k -> p (a k)"), ALU.subtract, ALU.add)
                if h % 2:
                    read(ins, f"fcum{h // 2}")
                    dve.wait_ge(free[turn[f"fcum{h // 2}"][0]], turn[f"fcum{h // 2}"][1] + 1)
                else:
                    link(ins)
                b = bank_of(dve, f"fS{h}")
                read(V.scalar_tensor_tensor(S, b[:, 0:3 * P], FD ** -0.5, S, ALU.mult, ALU.add), f"fS{h}")
                dve.wait_ge(free[turn[f"fS{h}"][0]], turn[f"fS{h}"][1] + 1)
                V.tensor_reduce(fmx[:, h, 0:1], S[:, 0:P], AX.X, ALU.max, negate=True).then_inc(s_fs, 1)
                V.tensor_reduce(fmx[:, h, 1:2], S[:, P:3 * P], AX.X, ALU.max, negate=True).then_inc(s_fs, 1)

            dve.wait_ge(s_fp, 2 * FH)
            link(V.reciprocal(fsum[:, :, :], fsum[:, :, :]))
            fsq = sq[:, :, :].rearrange("p a t -> p (a t)")[:, 0:FH * FD]
            for tb in range(TB):
                b = bank_of(dve, f"fo{tb}")[:, :].rearrange("p (h d) -> p h d", h=FH)
                o = fo[:, tb, :].rearrange("p (h d) -> p h d", h=FH)
                read(V.tensor_tensor(o, b, fsum[:, :, tb:tb + 1].to_broadcast([P, FH, FD]), ALU.mult), f"fo{tb}")
                dve.wait_ge(free[turn[f"fo{tb}"][0]], turn[f"fo{tb}"][1] + 1)
                if tb == 0:
                    dve.wait_ge(*full_of("fks1"))
                link(V.tensor_tensor(fsq.rearrange("p (h d) -> p h d", h=FH), o, o, ALU.mult))
                V.tensor_reduce(frs[:, tb, :], fsq.rearrange("p (h d) -> p h d", h=FH), AX.X, ALU.add).then_inc(s_arg, 1)
                root_wait()
                link(V.reciprocal(frs[:, tb, :], frs[:, tb, :]))
                V.tensor_tensor(o, o, frs[:, tb, :].unsqueeze(2).to_broadcast([P, FH, FD]), ALU.mult).then_inc(s_fo, 1)

            for tb in range(TB):
                b = bank_of(dve, f"GS{tb}")
                read(V.tensor_copy(gcum[:, tb, :, :], b[:, 0:2 * GH].rearrange("p (a h) -> p a h", a=2)), f"GS{tb}")
                dve.wait_ge(free[turn[f"GS{tb}"][0]], turn[f"GS{tb}"][1] + 1)
            V.tensor_tensor(sc4[:, :, 2, :], gcum[:, :, 1, :], gcum[:, :, 0, :], ALU.subtract).then_inc(s_garg, 1)
            for tb in range(TB):
                b = bank_of(dve, f"GB{tb}")
                for h in range(GH):
                    ins = V.scalar_tensor_tensor(dec[:, tb, h, :], b[:, P * h:P * h + P], gcum[:, tb, 0, h:h + 1],
                                                 dmask[:, :], ALU.subtract, ALU.add)
                    if h < GH - 1:
                        link(ins)
                    else:
                        ins.then_inc(s_garg, 1)

            for i in range(12):
                if i == 4:
                    for tb in range(TB):
                        dve.wait_ge(s_dec, 3 + tb)
                        b = bank_of(dve, f"bB{tb}")[:, :].rearrange("p (h c) -> p h c", h=GH)
                        read(V.tensor_tensor(AT[:, tb, :, :], b, dec[:, tb, :, :], ALU.mult), f"bB{tb}")
                if i % 2 == 0:
                    dve.wait_ge(free[turn[f"gr{i // 2}"][0]], turn[f"gr{i // 2}"][1] + 1)
                link(V.tensor_scalar(cv[:, i, :], raw[:, i, 0:T], conv_w[:, i, 0:1], None, ALU.mult))
                for c in range(1, CONV):
                    ins = V.scalar_tensor_tensor(cv[:, i, :], raw[:, i, c:c + T], conv_w[:, i, c:c + 1], cv[:, i, :],
                                                 ALU.mult, ALU.add)
                    if c < CONV - 1:
                        link(ins)
                    else:
                        ins.then_inc(s_conv, 1)
            for i in range(4):
                head_norm("gs", i, cv, [GD ** -0.5 if i < 2 else 1.0], 1, 5 + i)
            for tb in range(TB):
                b = bank_of(dve, f"fT{tb}")[:, :].rearrange("p (k t) -> p k t", k=4)
                read(V.tensor_tensor(mixT[:, 0:4, P * tb:P * tb + P], b,
                                     fout_gain[:, :].unsqueeze(2).to_broadcast([P, 4, P]), ALU.mult), f"fT{tb}")
            for tb in range(TB):
                dve.wait_ge(*free_of(f"bB{tb}"))
                b = bank_of(dve, f"kk{tb}")[:, :].rearrange("p (h c) -> p h c", h=GH)
                read(V.tensor_tensor(AT[:, tb, :, :], b, AT[:, tb, :, :], ALU.mult), f"kk{tb}")
            dve.wait_ge(s_dec, 2)
            link(V.scalar_tensor_tensor(sc4[:, :, 1, :], sc4[:, :, 0, :], -1.0, beta[:, :, :], ALU.mult, ALU.mult))
            dve.wait_ge(*full_of("vtok1"))
            for tb in range(TB):
                b = bank_of(dve, f"ktok{tb}")[:, :].rearrange("p (h d) -> p h d", h=GH)
                V.tensor_tensor(kbn[:, tb, :, :], b, sc4[:, tb, 1, :].unsqueeze(2).to_broadcast([P, GH, GD]), ALU.mult).then_inc(s_kop, 1)
                read(V.tensor_tensor(kd[:, tb, :, :], b, sc4[:, tb, 2, :].unsqueeze(2).to_broadcast([P, GH, GD]), ALU.mult), f"ktok{tb}")
                b = bank_of(dve, f"vtok{tb}")[:, :].rearrange("p (h d) -> p h d", h=GH)
                read(V.tensor_tensor(vb[:, tb, :, :], b, beta[:, tb, :].unsqueeze(2).to_broadcast([P, GH, GD]), ALU.mult), f"vtok{tb}")
            for tb in range(TB):
                b = bank_of(dve, f"qk{tb}")[:, :].rearrange("p (h c) -> p h c", h=GH)
                read(V.tensor_tensor(qkT[:, tb, :, :], b, dec[:, tb, :, :], ALU.mult), f"qk{tb}")
            for tb in range(TB):
                V.tensor_tensor(qd[:, :, P * tb:P * tb + P], gq[:, :, P * tb:P * tb + P], expG[:, tb, :, :],
                                ALU.mult).then_inc(s_kop, 1)
            def key_norms(i):
                head_norm("kxs", i, kxT, [x_gain[:, 1, c:c + 1] for c in range(2)], 2, 9 + i)

            idb = ident[:, :].unsqueeze(1).to_broadcast([P, GH, P])
            for tb in range(TB):
                dve.wait_ge(s_lvl, tb + 1)
                V.tensor_tensor(TiT[:, tb, :, :], idb, ATl[0][:, tb, :, :], ALU.subtract).then_inc(s_T0, 1)
                b = bank_of(dve, f"X0_{tb}")[:, :].rearrange("p (h c) -> p h c", h=GH)
                read(V.tensor_tensor(Ti[:, tb, :, :], idb, b, ALU.subtract), f"X0_{tb}")
            for i in range(4):
                key_norms(i)
            for n in range(1, len(LEVELS)):
                for tb in range(TB):
                    if n < len(LEVELS) - 1:
                        b = bank_of(dve, f"Y{n}_{tb}")[:, :].rearrange("p (h c) -> p h c", h=GH)
                        dve.wait_ge(*free_of(f"X0_{tb}" if n == 1 else f"Y{n - 1}_{tb}"))
                        read(V.tensor_tensor(Ti[:, tb, :, :], Ti[:, tb, :, :], b, ALU.subtract), f"Y{n}_{tb}")
                    b = bank_of(dve, f"YT{n}_{tb}")[:, :].rearrange("p (h c) -> p h c", h=GH)
                    if n == 1:
                        dve.wait_ge(s_T0, tb + 1)
                    else:
                        dve.wait_ge(*free_of(f"YT{n - 1}_{tb}"))
                    read(V.tensor_tensor(TiT[:, tb, :, :], TiT[:, tb, :, :], b, ALU.subtract), f"YT{n}_{tb}")

            for c in range(4):
                tb, r0 = c // 2, CHUNK * (c % 2)
                b = bank_of(dve, f"vn{c}")
                read(V.tensor_copy(vnew[r0:r0 + CHUNK, tb, :], b[r0:r0 + CHUNK, :]), f"vn{c}")
                if c < 3:
                    b = bank_of(dve, f"S{c}")[:, :].rearrange("p (h d) -> p h d", h=GH)
                    if c:
                        dve.wait_ge(*free_of(f"S{c - 1}"))
                        link(V.tensor_tensor(Sd, St, expG[:, tb, :, r0 + CHUNK - 1:r0 + CHUNK].to_broadcast([P, GH, GD]),
                                             ALU.mult))
                        dve.wait_ge(*(full_of(f"go{tb}") if c % 2 else (s_os, c // 2 + 1)))
                        read(V.tensor_tensor(St, Sd, b, ALU.add), f"S{c}")
                    else:
                        read(V.tensor_copy(St, b), f"S{c}")
            for tb in range(TB):
                dve.wait_ge(s_gsq, 2 * tb + 1)
                V.tensor_reduce(grs[:, tb, :], gsq[:, 0, :].rearrange("p (h d) -> p h d", h=GH), AX.X, ALU.add).then_inc(s_gsq, 1)
                root_wait()
                link(V.reciprocal(grs[:, tb, :], grs[:, tb, :]))
                b = bank_of(dve, f"go{tb}")[:, :].rearrange("p (h d) -> p h d", h=GH)
                g = go[:, tb, :].rearrange("p (h d) -> p h d", h=GH)
                read(V.tensor_tensor(g, b, grs[:, tb, :].unsqueeze(2).to_broadcast([P, GH, GD]), ALU.mult), f"go{tb}")
                dve.wait_ge(free[turn[f"go{tb}"][0]], turn[f"go{tb}"][1] + 1)
                V.tensor_tensor(go[:, tb, :], go[:, tb, :], zs[:, tb, :], ALU.mult).then_inc(s_go, 1)
            for tb in range(TB):
                b = bank_of(dve, f"gT{tb}")[:, :].rearrange("p (k t) -> p k t", k=4)
                read(V.tensor_scalar(mixT[:, 4:8, P * tb:P * tb + P], b, gout_gain[:, 0:1], None, ALU.mult), f"gT{tb}")
                dve.wait_ge(free[turn[f"gT{tb}"][0]], turn[f"gT{tb}"][1] + 1)

            def residual(name, banks=range(4)):
                for i in banks:
                    b = bank_of(dve, f"{name}{i}")
                    n0 = WIDE * (i // 2)
                    dst = xs[:, i % 2, n0:n0 + WIDE]
                    read(V.tensor_tensor(dst, dst, b[:, :], ALU.add), f"{name}{i}")
                for i in banks:
                    dve.wait_ge(*free_of(f"{name}{i}"))

            residual("wo")
            norm_rows(xs, hn, 0)
            turned("h2T", hT, 2)
            for i in range(4):
                head_norm("qxs", i, qxT, [x_gain[:, 0, c:c + 1] for c in range(2)], 2, 13 + i)

            def row_max(h):
                b = bank_of(dve, f"xS{h}")[:, :].rearrange("p (a t) -> p a t", a=2)
                link(V.tensor_reduce(xmx[:, h, :], b, AX.X, ALU.max))
                V.tensor_scalar(xmx[:, h, :], xmx[:, h, :], -(XD ** -0.5), None, ALU.mult).then_inc(s_xm, 1)

            def over_sums(h):
                dve.wait_ge(s_xe, h + 1)
                dve.wait_ge(*free_of(f"xS{h}"))
                link(V.reciprocal(xsum[:, h, :], xsum[:, h, :]))
                pv = xP[:, h, :].rearrange("p (a t) -> p a t", a=2)
                V.tensor_tensor(pv, pv, xsum[:, h, :].unsqueeze(2).to_broadcast([P, 2, T]), ALU.mult).then_inc(s_xp, 1)

            row_max(0)
            row_max(1)
            over_sums(0)
            row_max(2)
            over_sums(1)
            row_max(3)
            over_sums(2)
            over_sums(3)

            residual("xo", range(3))
            norm_rows(xs, hn, 4, [0])
            turned("h3T", hT, 3, range(2))
            residual("xo", [3])
            norm_rows(xs, hn, 4, [1])
            turned("h3T", hT, 3, range(2, 4))

            for tb in range(TB):
                b = bank_of(dve, f"lg{tb}")
                L = lg[:, tb, :]
                read(V.tensor_tensor(L, b[:, 0:NE], brt[:, :], ALU.add), f"lg{tb}")
                dve.wait_ge(free[turn[f"lg{tb}"][0]], turn[f"lg{tb}"][1] + 1)
                link(V.max(top8[:, tb, :], L))
                link(V.tensor_scalar(rcol[:, tb, 3:4], top8[:, tb, 0:1], -1.0, None, ALU.mult))
                V.tensor_scalar(rt[:, tb, 0, :], L, top8[:, tb, TOPK - 1:TOPK], None, ALU.is_gt).then_inc(s_lg, 1)
                link(V.tensor_scalar(rt[:, tb, 1, :], L, top8[:, tb, TOPK - 1:TOPK], None, ALU.is_equal))
                dve.wait_ge(s_lg, tb + 1)
                link(V.tensor_reduce(rcol[:, tb, 0:1], rt[:, tb, 0, :], AX.X, ALU.add))
                link(V.tensor_scalar(rcol[:, tb, 1:2], rcol[:, tb, 0:1], -1.0, float(TOPK), ALU.mult, ALU.add))
                link(V.tensor_tensor_scan(rt[:, tb, 2, :], ones[:, 0:NE], rt[:, tb, 1, :], 0.0, ALU.mult, ALU.add))
                link(V.scalar_tensor_tensor(rt[:, tb, 1, :], rt[:, tb, 2, :], rcol[:, tb, 1:2], rt[:, tb, 1, :],
                                            ALU.is_le, ALU.mult))
                V.tensor_tensor(sel[:, tb, :], rt[:, tb, 0, :], rt[:, tb, 1, :], ALU.add).then_inc(s_sel, 1)
                dve.wait_ge(s_sel, tb + 1)
                dve.wait_ge(s_re, tb + 1)
                link(V.tensor_tensor(comb[:, tb, :], rt[:, tb, 3, :], sel[:, tb, :], ALU.mult))
                link(V.tensor_reduce(rcol[:, tb, 2:3], comb[:, tb, :], AX.X, ALU.add))
                link(V.reciprocal(rcol[:, tb, 2:3], rcol[:, tb, 2:3]))
                V.tensor_scalar(comb[:, tb, :], comb[:, tb, :], rcol[:, tb, 2:3], None, ALU.mult).then_inc(s_comb, 1)
            dve.wait_ge(s_comb, 2)
            for tb in range(TB):
                b = bank_of(dve, f"rank{tb}")
                read(V.tensor_tensor(rt[:, tb, 0, :], b[:, 0:NE], sel[:, tb, :], ALU.mult), f"rank{tb}")
                dve.wait_ge(free[turn[f"rank{tb}"][0]], turn[f"rank{tb}"][1] + 1)
            def places(r):
                link(V.tensor_scalar(posx[:, :, NE * r:NE * r + NE], rt[:, :, 0, :], -1.0 - SLOTS * r, None, ALU.add))
                link(V.tensor_copy(combx[:, :, NE * r:NE * r + NE], comb[:, :, :]))

            places(0)
            sel4 = Sel.rearrange("p t (a s) -> p t a s", a=2)
            cw4 = CW.rearrange("p t (a s) -> p t a s", a=2)

            def cols(buf, j):
                v = buf[:, :, 2 * j:2 * j + 2] if isinstance(j, int) else buf[:, :, bass.ds(2 * j, 2)]
                return v

            def select(j, first=False):
                for tb in range(TB):
                    for a in range(2):
                        pos = posx[:, tb, 2 * j + a:2 * j + a + 1] if isinstance(j, int) else posx[:, tb, bass.ds(2 * j + a, 1)]
                        cmb = combx[:, tb, 2 * j + a:2 * j + a + 1] if isinstance(j, int) else combx[:, tb, bass.ds(2 * j + a, 1)]
                        V.tensor_scalar(sel4[:, tb, a, :], slot_no[:, :], pos, None, ALU.is_equal).then_inc(j_sel, 1)
                        V.tensor_scalar(cw4[:, tb, a, :], slot_no[:, :], pos, cmb, ALU.is_equal, ALU.mult).then_inc(j_sel, 1)

            def gathered(j):
                for a in range(2):
                    dve.wait_ge(j_ga, 2 * j + a + 1)
                    V.tensor_tensor(hgT[:, 4 * a:4 * a + 4, :], ps[6 + a][:, :].rearrange("p (k s) -> p k s", k=4),
                                    gains[:, 3, 4 * a:4 * a + 4].unsqueeze(2).to_broadcast([P, 4, P]), ALU.mult).then_inc(j_hg, 1)

            select(0)
            gathered(0)
            for r in range(1, ROUNDS + 1):
                places(r)
            b = bank_of(dve, "cnt")
            read(V.tensor_reduce(flag_f[:, :], b[:, 0:NE], AX.X, ALU.max), "cnt")
            dve.wait_ge(free[turn["cnt"][0]], turn["cnt"][1] + 1)
            link(V.tensor_scalar(flag_f[:, :], flag_f[:, :], float(SLOTS), None, ALU.is_gt))
            V.tensor_copy(flag[:, :], flag_f[:, :]).then_inc(s_flag, 1)
            b = bank_of(dve, "cT")
            read(V.tensor_copy(combT[:, :], b[0:NE, 0:T]), "cT")
            residual("bd", range(2))

            def add(j, n, banks):
                for tb in range(TB):
                    dve.wait_ge(j_sc, 4 * j + 2 * n + tb + 1)
                    dst = xs[:, tb, WIDE * n:WIDE * n + WIDE]
                    V.tensor_tensor(dst, dst, ps[banks[tb]][:, :], ALU.add).then_inc(j_add, 1)

            def job(i, p, first=False, last=False):
                j = 2 * i + p
                for a in range(2):
                    if a == 0:
                        dve.wait_ge(j_gu, j + 1)
                    else:
                        dve.wait_ge(*gate_up_end(i, p))
                    V.tensor_scalar(gS[:, a, :], ps[a][:, :], LIMIT, None, ALU.min).then_inc(j_g, 1)
                    V.tensor_scalar(uS[:, a, :], ps[2 + a][:, :], LIMIT, -LIMIT, ALU.min, ALU.max).then_inc(j_u, 1)
                    dve.wait_ge(j_u, 2 * j + a + 1)
                    dve.wait_ge(j_g, 2 * j + a + 1)
                    V.scalar_tensor_tensor(uS[:, a, :], uS[:, a, :], 1.0, gS[:, a, :], ALU.add, ALU.mult).then_inc(j_t, 1)
                    dve.wait_ge(j_sg, 2 * j + a + 1)
                    dve.wait_ge(j_t, 2 * j + a + 1)
                    V.tensor_tensor(aS[:, a, :], uS[:, a, :], sS[:, a, :], ALU.mult).then_inc(j_a, 1)
                if first:
                    residual("bd", range(2, 4))
                else:
                    add(j - 1, 0, (6, 7))
                    add(j - 1, 1, (4, 5))
                dve.wait_ge(j_ct, j + 1)
                V.tensor_copy(WT[:, :, :], ps[2][:, 0:T].rearrange("p (t s) -> p t s", t=TB)).then_inc(j_wt, 1)
                if last:
                    add(j, 0, (6, 7))
                    add(j, 1, (0, 1))
                else:
                    select(j + 1)
                    gathered(j + 1)

            def jobs(i0, i1):
                with dve.Fori(i0, i1) as i:
                    job(i, 1)
                    job(i + 1, 0)

            job(0, 0, first=True)
            jobs(0, PAIRS // 2 - 1)
            more = dve.value_load(flag[0:1, 0:1], min_val=0, max_val=1)
            with dve.If(more > 0):
                jobs(PAIRS // 2 - 1, ROUNDS * PAIRS // 2 - 1)
                job(ROUNDS * PAIRS // 2 - 1, 1, last=True)
            with dve.Else():
                job(PAIRS // 2 - 1, 1, last=True)

        @block.tensor
        def _(pe):
            M = nc.tensor

            def turn_rows(src, name, ready, banks=range(4)):
                for i in banks:
                    q, tb = i % 2, i // 2
                    pe.wait_ge(s_hn, ready + tb)
                    b = into(pe, f"{name}{i}")
                    for k in range(4):
                        ins = M.transpose(b[:, P * k:P * k + P],
                                          src[:, tb, :].rearrange("p (d k) -> p k d", k=KD)[:, 4 * q + k, :], ident[:, :])
                    filled(ins, f"{name}{i}")

            def channel_banks(w, rhsT, name, i0=0, banks=range(2)):
                for i in banks:
                    b = into(pe, f"{name}{i0 + i}")
                    for c in range(2):
                        for k in range(KD):
                            ins = M.matmul(b[:, T * c:T * c + T], w[:, k, P * (2 * i + c):P * (2 * i + c) + P], rhsT[:, k, :],
                                           start=(k == 0), stop=(k == KD - 1))
                    filled(ins, f"{name}{i0 + i}")

            def token_bank(w, lhs, name, tb):
                b = into(pe, name)
                for k in range(KD):
                    ins = M.matmul(b[:, :], lhs[:, k, P * tb:P * tb + P], w[:, k, :], start=(k == 0), stop=(k == KD - 1))
                filled(ins, name)

            def evacuated(name):
                pe.wait_ge(*free_of(name))

            pe.wait_ge(s_ident, 1)
            turn_rows(hn, "xT", 1)
            pe.wait_ge(s_par2, 32)
            for i in range(4):
                evacuated(f"xT{i}")
            for tb in range(TB):
                b = into(pe, f"gate{tb}")
                for k in range(KD):
                    ins = M.matmul(b[:, 0:16], hT[:, k, P * tb:P * tb + P], wsm[:, k, :], start=(k == 0), stop=(k == KD - 1))
                filled(ins, f"gate{tb}")

            def sumsq(name, src, i, width):
                b = into(pe, f"{name}{i}")
                q = sq[:, 2 * (i % 2):2 * (i % 2) + 2, :].rearrange("p a t -> p (a t)")
                if width == 1:
                    M.matmul(b[:, 0:T], ones[:, :], q[:, 0:T], start=True, stop=False)
                    ins = M.matmul(b[:, 0:T], ones[:, :], q[:, T:2 * T], start=False, stop=True)
                else:
                    ins = M.matmul(b[:, :], src[:, :], q, start=True, stop=True)
                filled(ins, f"{name}{i}")

            channel_banks(pre_w(pe, 0), hT, "fq")
            turn_rows(mn, "mT", 3)
            pe.wait_ge(s_const, 1)
            for i in range(2):
                evacuated(f"fq{i}")
                sumsq("fqs", cones, i, 2)
            channel_banks(pre_w(pe, 1), hT, "fk")
            pe.wait_ge(s_nlf, 2)
            b = into(pe, "cumT0")
            filled(M.matmul(b[:, 0:FH], prefix[:, :], nlf[:, 0, :], start=True, stop=True), "cumT0")
            b = into(pe, "cumT1")
            M.matmul(b[:, 0:FH], ones[:, :], nlf[:, 0, :], start=True, stop=False)
            filled(M.matmul(b[:, 0:FH], prefix[:, :], nlf[:, 1, :], start=False, stop=True), "cumT1")
            for i in range(2):
                evacuated(f"fk{i}")
                sumsq("fks", cones, i, 2)
            w = pre_w(pe, 2)
            for tb in range(TB):
                token_bank(w, hT, f"fv{tb}", tb)
            for i in range(2):
                evacuated(f"fv{i}")
            pe.wait_ge(s_nrm, 4)

            for h in range(FH + 2):
                if h < FH:
                    if h % 2 == 0:
                        b = into(pe, f"fcum{h // 2}")
                        for c in range(2):
                            row = [nlf[:, tb, h + c:h + c + 1].to_broadcast([P, P]) for tb in range(TB)]
                            M.matmul(b[:, T * c:T * c + P], row[0], prefix[:, :], start=True, stop=True)
                            M.matmul(b[:, T * c + P:T * c + T], row[0], ones[:, :], start=True, stop=False)
                            ins = M.matmul(b[:, T * c + P:T * c + T], row[1], prefix[:, :], start=False, stop=True)
                        filled(ins, f"fcum{h // 2}")
                    b = into(pe, f"fS{h}")
                    M.matmul(b[:, 0:P], fqz[:, h, 0:P], fkT[:, h // 2, 0:P], start=True, stop=True)
                    filled(M.matmul(b[:, P:3 * P], fqz[:, h, P:T], fkT[:, h // 2, :], start=True, stop=True), f"fS{h}")
                if 1 <= h <= FH:
                    g = h - 1
                    pe.wait_ge(s_fp, 2 * h)
                    b = into(pe, f"fPT{g}")
                    for i in range(3):
                        ins = M.transpose(b[:, P * i:P * i + P], fP[:, g % 2, P * i:P * i + P], ident[:, :])
                    filled(ins, f"fPT{g}")
                if h >= 2:
                    g = h - 2
                    evacuated(f"fPT{g}")
                    if g == 0:
                        o0, o1 = into(pe, "fo0"), into(pe, "fo1")
                    pt, c0 = fPT[:, g % 2, :], FD * g
                    i0 = M.matmul(o0[:, c0:c0 + FD], pt[:, 0:P], fv[:, 0, c0:c0 + FD], start=True, stop=True)
                    M.matmul(o1[:, c0:c0 + FD], pt[:, P:2 * P], fv[:, 0, c0:c0 + FD], start=True, stop=False)
                    i1 = M.matmul(o1[:, c0:c0 + FD], pt[:, 2 * P:3 * P], fv[:, 1, c0:c0 + FD], start=False, stop=True)
                    if g < FH - 1:
                        i1.then_inc(s_pv, 1)
                    else:
                        filled(i0, "fo0")
                        filled(i1, "fo1")

            for tb in range(TB):
                b = into(pe, f"GS{tb}")
                M.matmul(b[:, 0:GH], cprefix[:, :], gg[:, tb, :], start=True, stop=True)
                filled(M.matmul(b[:, GH:2 * GH], cones[:, :], gg[:, tb, :], start=True, stop=True), f"GS{tb}")
            for name, src, rhs in (("GB", gg, cprefix), ("bB", beta, ident)):
                for tb in range(TB):
                    b = into(pe, f"{name}{tb}")
                    for h in range(GH):
                        ins = M.matmul(b[:, P * h:P * h + P], src[:, tb, h:h + 1].to_broadcast([P, P]), rhs[:, :],
                                       start=True, stop=True)
                    filled(ins, f"{name}{tb}")
            for c in range(2):
                channel_banks(pre_w(pe, 3 + c), hT, "gr", 2 * c)
            w = pre_w(pe, 5)
            for half in range(2):
                channel_banks(w, hT, "gr", 4, [half])
                for i in (2 * half, 2 * half + 1):
                    pe.wait_ge(s_sq, i + 1)
                    sumsq("gs", ones, i, 2)
            w = pre_w(pe, 6)
            for tb in range(TB):
                token_bank(w, hT, f"z{tb}", tb)
            for tb in range(TB):
                pe.wait_ge(s_fo, tb + 1)
                b = into(pe, f"fT{tb}")
                for k in range(4):
                    ins = M.transpose(b[:, P * k:P * k + P], fo[:, tb, P * k:P * k + P], ident[:, :])
                filled(ins, f"fT{tb}")
            for i in range(4):
                evacuated(f"mT{i}")
            channel_banks(pre_w(pe, 7), mT, "kx", 0)
            def key_products(name, rhs):
                for tb in range(TB):
                    b = into(pe, f"{name}{tb}")
                    for h in range(GH):
                        ins = M.matmul(b[:, P * h:P * h + P], gk[:, h, P * tb:P * tb + P], rhs[:, h, P * tb:P * tb + P],
                                       start=True, stop=True)
                    filled(ins, f"{name}{tb}")

            pe.wait_ge(s_nrm, 8)
            key_products("kk", gk)
            pe.wait_ge(s_silu, 3)
            for tb in range(TB):
                for name, src in (("ktok", gk), ("vtok", gvT)):
                    b = into(pe, f"{name}{tb}")
                    for h in range(GH):
                        ins = M.transpose(b[:, P * h:P * h + P], src[:, h, P * tb:P * tb + P], ident[:, :])
                    filled(ins, f"{name}{tb}")
            key_products("qk", gq)
            for i in range(2):
                evacuated(f"kx{i}")
                sumsq("kxs", ones, i, 1)
            for tb in range(TB):
                pe.wait_ge(s_lvl, tb + 1)
                b = into(pe, f"X0_{tb}")
                for h in range(GH):
                    ins = M.transpose(b[:, P * h:P * h + P], ATl[0][:, tb, h, :], ident[:, :])
                filled(ins, f"X0_{tb}")
            channel_banks(pre_w(pe, 8), mT, "kx", 2)
            for i in range(2, 4):
                evacuated(f"kx{i}")
                sumsq("kxs", ones, i, 1)
            for n in range(1, len(LEVELS)):
                for tb in range(TB):
                    pe.wait_ge(s_lvl, 2 * n + tb + 1)
                    if n == 1:
                        pe.wait_ge(s_T0, tb + 1)
                        evacuated(f"X0_{tb}")
                    else:
                        evacuated(f"Y{n - 1}_{tb}")
                        evacuated(f"YT{n - 1}_{tb}")
                    b = into(pe, f"X{n}_{tb}")
                    for h in range(GH):
                        ins = M.matmul(b[:, P * h:P * h + P], ATl[n % 2][:, tb, h, :], Ti[:, tb, h, :], start=True, stop=True)
                    filled(ins, f"X{n}_{tb}")
                for tb in range(TB):
                    evacuated(f"X{n}_{tb}")
                    if n < len(LEVELS) - 1:
                        b = into(pe, f"Y{n}_{tb}")
                        for h in range(GH):
                            ins = M.matmul(b[:, P * h:P * h + P], TiT[:, tb, h, :], Xi[:, tb, h, :], start=True, stop=True)
                        filled(ins, f"Y{n}_{tb}")
                    b = into(pe, f"YT{n}_{tb}")
                    for h in range(GH):
                        ins = M.matmul(b[:, P * h:P * h + P], Xi[:, tb, h, :], TiT[:, tb, h, :], start=True, stop=True)
                    filled(ins, f"YT{n}_{tb}")
            for tb in range(TB):
                evacuated(f"YT{len(LEVELS) - 1}_{tb}")
            evacuated("ktok1")
            evacuated("vtok1")
            evacuated("vtok0")
            evacuated("qk1")
            evacuated("qk0")
            pe.wait_ge(s_kop, 4)
            for tb in range(TB):
                b = into(pe, f"w{tb}")
                for h in range(GH):
                    ins = M.matmul(b[:, P * h:P * h + P], kbn[:, tb, h, :], TiT[:, tb, h, :], start=True, stop=True)
                filled(ins, f"w{tb}")
            def values_part(c, tb, k0, k1):
                name = f"vx{2 * c + tb}"
                if k0 == 0:
                    into(pe, name)
                w = pre_w(pe, 9 if c == 0 else 12)
                b = ps[turn[name][0]]
                for k in range(k0, k1):
                    ins = M.matmul(b[:, :], mT[:, k, P * tb:P * tb + P], w[:, k, :], start=(k == 0), stop=(k == KD - 1))
                if k1 == KD:
                    filled(ins, name)

            go_b = {}
            for c in range(4):
                tb, r0 = c // 2, CHUNK * (c % 2)
                rows = slice(r0, r0 + CHUNK)
                if c == 1:
                    evacuated("w0")
                    evacuated("w1")
                if c:
                    evacuated(f"S{c - 1}")
                b = into(pe, f"vn{c}")
                for h in range(GH):
                    o = b[rows, P * h:P * h + P]
                    ins = M.matmul(o, TiT[:, tb, h, rows], vb[:, tb, h, :], start=True, stop=(c == 0))
                    if c:
                        ins = M.matmul(o, wTn[:, tb, h, rows], St[:, h, :], start=False, stop=True)
                filled(ins, f"vn{c}")
                values_part(0, c // 2, 4 * (c % 2), 4 * (c % 2) + 2)
                evacuated(f"vn{c}")
                if c < 3:
                    b = into(pe, f"S{c}")
                    for h in range(GH):
                        ins = M.matmul(b[:, P * h:P * h + P], kd[rows, tb, h, :], vnew[rows, tb, P * h:P * h + P], start=True, stop=True)
                    filled(ins, f"S{c}")
                if c % 2 == 0:
                    go_b[tb] = into(pe, f"go{tb}")
                for h in range(GH):
                    o = go_b[tb][rows, P * h:P * h + P]
                    if c:
                        M.matmul(o, qd[:, h, P * tb + r0:P * tb + r0 + CHUNK], St[:, h, :], start=True, stop=False)
                    ins = M.matmul(o, qkT[rows, tb, h, rows], vnew[rows, tb, P * h:P * h + P], start=(c == 0), stop=True)
                if c % 2:
                    filled(ins, f"go{tb}")
                else:
                    ins.then_inc(s_os, 1)
                values_part(0, c // 2, 4 * (c % 2) + 2, 4 * (c % 2) + 4)
            for tb in range(TB):
                pe.wait_ge(s_go, tb + 1)
                b = into(pe, f"gT{tb}")
                for k in range(4):
                    ins = M.transpose(b[:, P * k:P * k + P], go[:, tb, P * k:P * k + P], ident[:, :])
                filled(ins, f"gT{tb}")
            evacuated("gT0")
            evacuated("gT1")
            evacuated("fT0")
            evacuated("fT1")

            for c in range(2):
                w = pre_w(pe, 10 + c)
                for tb in range(TB):
                    token_bank(w, mixT, f"wo{2 * c + tb}", tb)
            for tb in range(TB):
                values_part(1, tb, 0, KD)
            turn_rows(hn, "h2T", 5)
            for i in range(4):
                evacuated(f"h2T{i}")
            channel_banks(pre_w(pe, 13), hT, "qx")
            w = pre_w(pe, 14)
            for half in range(2):
                channel_banks(w, hT, "qx", 2, [half])
                for i in (0, 1) if half == 0 else (2, 3):
                    evacuated(f"qx{i}")
                    sumsq("qxs", ones, i, 1)
            def scores(h):
                pe.wait_ge(s_nrm, 13 + h)
                b = into(pe, f"xS{h}")
                for qb in range(2):
                    for c in range(2):
                        ins = M.matmul(b[:, T * qb:T * qb + T], qxT[:, 2 * h + c, P * qb:P * qb + P], kxT[:, 2 * h + c, :],
                                       start=(c == 0), stop=(c == 1))
                filled(ins, f"xS{h}")

            def turn_probs(h):
                pe.wait_ge(s_xp, h + 1)
                b = into(pe, f"xPT{h}")
                for mb in range(2):
                    for qb in range(2):
                        ins = M.transpose(b[:, T * mb + P * qb:T * mb + P * qb + P],
                                          xP[:, h, T * qb + P * mb:T * qb + P * mb + P], ident[:, :])
                filled(ins, f"xPT{h}")

            def weighted_values(h):
                evacuated(f"xPT{h}")
                b = into(pe, f"xO{h}")
                for c in range(2):
                    for mb in range(2):
                        ins = M.matmul(b[:, T * c:T * c + T], vx[:, mb, XD * h + P * c:XD * h + P * c + P],
                                       xPT[:, h % 2, T * mb:T * mb + T], start=(mb == 0), stop=(mb == 1))
                filled(ins, f"xO{h}")

            evacuated("vx2")
            evacuated("vx3")
            scores(0)
            scores(1)
            scores(2)
            turn_probs(0)
            scores(3)
            turn_probs(1)
            weighted_values(0)
            turn_probs(2)
            weighted_values(1)
            turn_probs(3)
            weighted_values(2)
            weighted_values(3)
            for g in range(XH):
                evacuated(f"xO{g}")
            w = pre_w(pe, 15)
            token_bank(w, mixT, "xo0", 0)
            token_bank(w, mixT, "xo1", 1)
            w = pre_w(pe, 16)
            token_bank(w, mixT, "xo2", 0)
            b = into(pe, "xo3")
            for k in range(KD):
                if k == KD // 2:
                    turn_rows(hn, "h3T", 7, range(2))
                ins = M.matmul(b[:, :], mixT[:, k, P:T], w[:, k, :], start=(k == 0), stop=(k == KD - 1))
            filled(ins, "xo3")
            pe.wait_ge(s_par, 16 * 14)
            for tb in range(TB):
                if tb:
                    turn_rows(hn, "h3T", 7, range(2, 4))
                for i in (2 * tb, 2 * tb + 1):
                    evacuated(f"h3T{i}")
                b = into(pe, f"lg{tb}")
                for k in range(KD):
                    ins = M.matmul(b[:, 0:NE], hT[:, k, P * tb:P * tb + P], wr[:, k, :], start=(k == 0), stop=(k == KD - 1))
                filled(ins, f"lg{tb}")
            pe.wait_ge(s_sel, 1)
            b = into(pe, "rank0")
            filled(M.matmul(b[:, 0:NE], prefix[:, :], sel[:, 0, :], start=True, stop=True), "rank0")
            pe.wait_ge(s_sel, 2)
            b = into(pe, "rank1")
            M.matmul(b[:, 0:NE], ones[:, :], sel[:, 0, :], start=True, stop=False)
            filled(M.matmul(b[:, 0:NE], prefix[:, :], sel[:, 1, :], start=False, stop=True), "rank1")
            b = into(pe, "cnt")
            M.matmul(b[:, 0:NE], ones[:, :], sel[:, 0, :], start=True, stop=False)
            filled(M.matmul(b[:, 0:NE], ones[:, :], sel[:, 1, :], start=False, stop=True), "cnt")
            def down_biases(i0):
                for i in (i0, i0 + 1):
                    b = into(pe, f"bd{i}")
                    filled(M.matmul(b[:, :], combT[:, P * (i % 2):P * (i % 2) + P], bdn[:, WIDE * (i // 2):WIDE * (i // 2) + WIDE],
                                    start=True, stop=True), f"bd{i}")

            rows_k = hn[:, :, :].rearrange("p t (d k) -> p t k d", k=KD)

            def gather(j):
                pe.wait_ge(j_sel, 8 * j + 8)
                for a in range(2):
                    for q in range(4):
                        for tb in range(TB):
                            ins = M.matmul(ps[6 + a][:, P * q:P * q + P], rows_k[:, tb, 4 * a + q, :], Sel[:, tb, :],
                                           start=(tb == 0), stop=(tb == 1))
                    ins.then_inc(j_ga, 1)

            def scatter(n, banks):
                for tb in range(TB):
                    M.matmul(ps[banks[tb]][:, :], WT[:, tb, :], yS[:, n, :], start=True, stop=True).then_inc(j_sc, 1)

            def tiles(i, p, ms, k):
                w = []
                for m in ms:
                    s = slot_of(p, m)
                    before = pre_count[s] + fills_before(i, p, m)
                    pe.wait_ge(landed[s], 16 * (before + 1))
                    w.append(slot(s).rearrange("p (k n) -> p k n", k=k))
                return w

            def job(i, p, first=False, last=False):
                j = 2 * i + p
                pe.wait_ge(j_hg, 2 * j + 2)
                pe.wait_ge(s_bgu, 16 * j + 16)
                if not first:
                    pe.wait_ge(j_g, 2 * j)
                    pe.wait_ge(j_u, 2 * j)
                    pe.wait_ge(j_wt, j)
                for b in range(4):
                    ins = M.matmul(ps[b][:, :], pairsel[:, :], bgu[:, WIDE * b:WIDE * b + WIDE], start=True, stop=False)
                ins.then_inc(j_bias, 1)
                for q in range(4):
                    w = tiles(i, p, (2 * q, 2 * q + 1), 2)
                    order = [(kk, b) for kk in range(2) for b in range(4)] if q < 3 else \
                            [(kk, b) for bs in ((0, 2), (1, 3)) for kk in range(2) for b in bs]
                    for kk, b in order:
                        k = 2 * q + kk
                        for a in range(2):
                            r = slice(SLOTS * a, SLOTS * a + SLOTS)
                            ins = M.matmul(ps[b][r, :], hgT[:, k, r], w[a][:, kk, WIDE * b:WIDE * b + WIDE],
                                           start=False, stop=(k == KD - 1))
                            if kk == 1 and b == 3:
                                ins.then_inc(spent[slot_of(p, 2 * q + a)], 1)
                            elif k == KD - 1 and b == 2 and a == 1:
                                ins.then_inc(j_gu, 1)
                if first:
                    down_biases(2)
                else:
                    pe.wait_ge(j_y, 2 * j)
                    for n in range(2):
                        scatter(n, ((6, 7), (4, 5))[n])
                pe.wait_ge(j_u, 2 * j + 1)
                for tb in range(TB):
                    ins = M.transpose(ps[2][:, P * tb:P * tb + P], CW[:, tb, :], ident[:, :])
                ins.then_inc(j_ct, 1)
                for a in range(2):
                    pe.wait_ge(j_a, 2 * j + a + 1)
                    for k in range(4):
                        ins = M.transpose(ps[a][:, P * k:P * k + P], aS[:, a, P * k:P * k + P], ident[:, :])
                    ins.then_inc(j_T, 1)
                pe.wait_ge(j_aT, 2 * j + 2)
                if first:
                    for b in range(2):
                        evacuated(f"bd{2 + b}")
                else:
                    pe.wait_ge(j_add, 4 * j)
                for q in range(2):
                    w = tiles(i, p, (8 + 2 * q, 9 + 2 * q), 4)
                    order = [(kk, b) for kk in range(4) for b in range(2)] if q == 0 else \
                            [(kk, b) for b in range(2) for kk in range(4)]
                    for kk, b in order:
                        k = 4 * q + kk
                        for a in range(2):
                            r = slice(SLOTS * a, SLOTS * a + SLOTS)
                            ins = M.matmul(ps[4 + b][r, :], actT[:, k, r], w[a][:, kk, WIDE * b:WIDE * b + WIDE],
                                           start=(k == 0), stop=(k == KF - 1))
                            if kk == 3 and b == 1:
                                ins.then_inc(spent[slot_of(p, 8 + 2 * q + a)], 1)
                            elif k == KF - 1 and b == 0 and a == 1:
                                ins.then_inc(j_D, 1)
                    if q == 0 and not last:
                        gather(j + 1)
                if last:
                    pe.wait_ge(j_wt, j + 1)
                    for n in range(2):
                        pe.wait_ge(j_y, 2 * j + n + 1)
                        scatter(n, ((6, 7), (0, 1))[n])

            def jobs(i0, i1):
                with pe.Fori(i0, i1) as i:
                    job(i, 1)
                    job(i + 1, 0)

            for name in [n for n in turn if turn[n][0] in (6, 7) and turn[n][1] == uses[turn[n][0]] - 1]:
                evacuated(name)
            gather(0)
            pe.wait_ge(s_comb, 2)
            b = into(pe, "cT")
            for tb in range(TB):
                ins = M.transpose(b[0:NE, P * tb:P * tb + P], comb[:, tb, :], ident[:, :])
            filled(ins, "cT")
            evacuated("cT")
            pe.wait_ge(s_bdn, 16)
            down_biases(0)
            for name in ("rank0", "rank1", "cnt"):
                evacuated(name)
            job(0, 0, first=True)
            jobs(0, PAIRS // 2 - 1)
            pe.wait_ge(s_flag, 1)
            more = pe.value_load(flag[0:1, 0:1], min_val=0, max_val=1)
            with pe.If(more > 0):
                jobs(PAIRS // 2 - 1, ROUNDS * PAIRS // 2 - 1)
                job(ROUNDS * PAIRS // 2 - 1, 1, last=True)
            with pe.Else():
                job(PAIRS // 2 - 1, 1, last=True)


_INS = ["x", "mem", "mix_norm", "w_in", "b_forget", "fox_q_gain", "fox_k_gain", "fox_out_gain",
        "gdn_conv_w", "gdn_a_log", "gdn_dt_bias", "gdn_out_gain", "w_out",
        "xattn_norm", "mem_norm", "w_xq", "w_xkv", "xq_gain", "xk_gain", "w_xo",
        "moe_norm", "w_router", "b_router", "w_gate_up", "b_gate_up", "w_down", "b_down"]


def kernel(**inputs):
    import numpy as _np
    import concourse.bacc as _bacc
    from concourse import mybir as _mybir
    from concourse.bass_utils import run_bass_kernel_spmd as _run

    nc = _bacc.Bacc("TRN2", target_bir_lowering=False, num_devices=1)
    arrays, args = {}, []
    for name in _INS:
        a = _np.ascontiguousarray(inputs[name])
        arrays[f"in_{name}_dram"] = a
        args.append(nc.dram_tensor(f"in_{name}_dram", a.shape, _mybir.dt.from_np(a.dtype), kind="ExternalInput").ap())
    o = nc.dram_tensor("out_0_dram", (1, T, D), F32, kind="ExternalOutput").ap()
    layer_kernel(nc, *args, o)
    r = _run(nc, [arrays], core_ids=[0])
    return r.results[0]["out_0_dram"]
```

```python
from contextlib import ExitStack

import concourse.bass as bass
from concourse import mybir

F32 = mybir.dt.float32
I32 = mybir.dt.int32
ALU = mybir.AluOpType
ACT = mybir.ActivationFunctionType
AX = mybir.AxisListType

P = 128
T = 256
TB = T // P
D = 1024
KD = D // P
EPS = 1e-6
FH, FD = 8, 64
GH, GD = 4, 128
CONV = 4
CHUNK = 64
XH, XD = 4, 256
NE, TOPK = 32, 4
F = 1024
KF = F // P
LIMIT, ALPHA = 7.0, 1.702
NEG = -1.0e30
SLOTS = 64
ROUNDS = T // SLOTS
PAIRS = NE // 2
LEVELS = [1, 2, 4, 8, 16, 32]

FQ, FK, FV, FF = 0, 512, 1024, 1536
GQ, GK, GV, GA, GB, GZ = 1544, 2056, 2568, 3080, 3084, 3088

WIDE = 512
SLOT = KD * WIDE
RING = 8
OWN = 6
PRE = 3
PRE_FILLS = 17
WARM_UP = 24
JOB_FILLS = 12


def layer_kernel(nc, x, mem, mix_norm, w_in, b_forget, fox_q_gain, fox_k_gain, fox_out_gain,
                 gdn_conv_w, gdn_a_log, gdn_dt_bias, gdn_out_gain, w_out,
                 xattn_norm, mem_norm, w_xq, w_xkv, xq_gain, xk_gain, w_xo,
                 moe_norm, w_router, b_router, w_gate_up, b_gate_up, w_down, b_down, out):
    ctx = ExitStack()
    with ctx:
        def sb(name, shape, dt=F32):
            return ctx.enter_context(nc.sbuf_tensor(name, shape, dt))

        def sem(name):
            return ctx.enter_context(nc.semaphore(name))

        ring = sb("ring", [P, OWN * SLOT])
        xs = sb("xs", [P, TB, D])
        hn = sb("hn", [P, TB, D])
        hT = sb("hT", [P, KD, T])
        mixT = sb("mixT", [P, KD, T])
        kvx = sb("kvx", [P, 4096])
        early = sb("early", [P, 4096])
        work = sb("work", [P, 7936])
        ident = sb("ident", [P, P])
        prefix = sb("prefix", [P, P])
        ones = sb("ones", [P, P])
        cprefix = sb("cprefix", [P, P])
        cones = sb("cones", [P, P])
        fmask = sb("fmask", [P, 2, P])
        dmask = sb("dmask", [P, P])
        lmask = sb("lmask", [P, len(LEVELS), P])
        slot_no = sb("slot_no", [P, SLOTS])
        pairsel = sb("pairsel", [2, P])
        gains = sb("gains", [P, 4, KD])
        fqk_gain = sb("fqk_gain", [P, 2])
        fout_gain = sb("fout_gain", [P, 4])
        gout_gain = sb("gout_gain", [P, 1])
        conv_w = sb("conv_w", [P, 12, CONV])
        gate_b = sb("gate_b", [P, 12])
        alog = sb("alog", [P, GH])
        brt = sb("brt", [P, NE])
        x_gain = sb("x_gain", [P, 2, 2])
        wsm = sb("wsm", [P, KD, 16])
        wr = sb("wr", [P, KD, NE])
        ss = sb("ss", [P, 8])
        rs = sb("rs", [P, 8])
        gv = sb("gv", [P, TB, 16])
        gabs = sb("gabs", [P, TB, 12])
        gln = sb("gln", [P, TB, 12])
        nlf = sb("nlf", [P, TB, FH])
        ncum = sb("ncum", [P, TB, FH])
        ea = sb("ea", [P, GH])
        gg = sb("gg", [P, TB, GH])
        beta = sb("beta", [P, TB, GH])
        gcum = sb("gcum", [P, TB, 2, GH])
        sc4 = sb("sc4", [P, TB, 3, GH])
        fmx = sb("fmx", [P, FH, 2])
        fsum = sb("fsum", [P, FH, 2])
        frs = sb("frs", [P, TB, FH])
        grs = sb("grs", [P, TB, GH])
        xqk_gain = sb("xqk_gain", [P, 2])
        xqr = sb("xqr", [P, TB, XH])
        xmx = sb("xmx", [P, XH, 2])
        xsum = sb("xsum", [P, XH, 2])
        lg = sb("lg", [P, TB, NE])
        top8 = sb("top8", [P, TB, 8])
        rt = sb("rt", [P, TB, 4, NE])
        rcol = sb("rcol", [P, TB, 4])
        sel = sb("sel", [P, TB, NE])
        combT = sb("combT", [NE, T])
        posx = sb("posx", [P, TB, (ROUNDS + 1) * NE])
        combx = sb("combx", [P, TB, (ROUNDS + 1) * NE])
        comb = combx[:, :, 0:NE]
        flag_f = sb("flag_f", [P, 1])
        eps = sb("eps", [P, 1])
        flag = sb("flag", [P, 1], I32)

        ps = [ctx.enter_context(nc.psum_tensor(f"ps{i}", [P, WIDE], F32)) for i in range(8)]

        def cut(buf, base, *shape):
            n = 1
            for s in shape:
                n *= s
            v = buf[:, base:base + n]
            if len(shape) == 2:
                v = v.rearrange("p (a b) -> p a b", a=shape[0])
            if len(shape) == 3:
                v = v.rearrange("p (a b c) -> p a b c", a=shape[0], b=shape[1])
            return v

        kxT = cut(kvx, 0, KD, T)
        vx = cut(kvx, 2048, TB, D)
        mn = cut(early, 0, TB, D)
        mT = cut(early, 2048, KD, T)
        kbn = cut(early, 0, TB, GH, P)
        vb = cut(early, 1024, TB, GH, P)
        fqT = cut(work, 0, 4, T)
        fqz = mixT[:, :, :]
        fkT = cut(work, 1024, 4, T)
        fv = cut(work, 2048, TB, FH * FD)
        fS = cut(work, 3072, 2, 3 * P)
        fP = cut(work, 3840, 2, 3 * P)
        fPT = cut(work, 4608, 2, 3 * P)
        fo = cut(work, 5376, TB, FH * FD)
        sq = cut(work, 6400, 4, T)
        rn = cut(work, 7424, 2, T)
        G0 = PRE * SLOT
        raw = cut(ring, G0, 12, T + CONV - 1 + 1)
        cv = cut(ring, G0 + 3120, 12, T)
        gq, gk, gvT = (cv[:, 4 * i:4 * i + 4, :] for i in range(3))
        qd = gq
        kd = cut(ring, G0 + 3120 + 8 * T, TB, GH, P)
        zs = cut(ring, G0 + 6192, TB, GH * GD)
        expG = cut(ring, G0 + 7216, TB, GH, P)
        dec = cut(ring, G0 + 8240, TB, GH, P)
        AT = cut(ring, G0 + 9264, TB, GH, P)
        qkT = cut(ring, G0 + 10288, TB, GH, P)
        assert 11312 <= (OWN - PRE) * SLOT
        ATl = [cut(work, base, TB, GH, P) for base in (0, 1024, 5120)]
        Ti = cut(work, 2048, TB, GH, P)
        TiT = cut(work, 3072, TB, GH, P)
        Xi = cut(work, 4096, TB, GH, P)
        wTn = hn[:, 0, :].rearrange("p (t h c) -> p t h c", t=TB, h=GH)
        vnew = hn[:, 1, :].rearrange("p (t n) -> p t n", t=TB)
        St = cut(ring, G0 + 0, GH, P)
        Sd = cut(ring, G0 + 512, GH, P)
        go = cut(ring, G0 + 1024, TB, GH * GD)
        gsq = cut(ring, G0 + 2048, 1, GH * GD)
        qxT = cut(work, 0, KD, T)
        xP = cut(work, 2048, XH, 2 * T)
        xPT = cut(work, 4096, 2, 2 * T)
        hgT = cut(work, 0, KD, P)
        actT = cut(work, 1024, KF, P)
        gS = cut(work, 2048, 2, WIDE)
        uS = cut(work, 3072, 2, WIDE)
        sS = cut(work, 4096, 2, WIDE)
        aS = cut(work, 5120, 2, WIDE)
        yS = cut(work, 6144, 2, WIDE)
        WT = cut(work, 7168, TB, P)
        Sel = cut(work, 7424, TB, P)
        CW = cut(work, 7680, TB, P)
        bgu0 = work[0:2, 5120:5120 + 2 * F]
        bgu = mixT[0:2, :, :].rearrange("p a t -> p (a t)")
        bdn = work[0:NE, 1024:1024 + D]

        landed = [sem(f"landed{i}") for i in range(RING)]
        spent = [sem(f"spent{i}") for i in range(RING)]
        full = [sem(f"full{i}") for i in range(8)]
        free = [sem(f"free{i}") for i in range(8)]
        s_x = [sem(f"x_loaded{tb}") for tb in range(TB)]
        s_mem, s_gain = sem("mem_loaded"), sem("mix_gain_loaded")
        s_par, s_par2 = sem("params_loaded"), sem("gate_weights_loaded")
        s_bgu, s_bdn = sem("expert_bias_loaded"), sem("down_bias_loaded")
        s_out = sem("stored")
        s_ident, s_const = sem("identity_built"), sem("constants_built")
        s_gc, s_dv, s_ac = sem("pool_step"), sem("dve_step"), sem("act_step")
        s_ss, s_hn = sem("squares_summed"), sem("rows_normalised")
        s_arg, s_root = sem("root_argument"), sem("root_taken")
        s_raw, s_sq, s_nrm = sem("projection_copied"), sem("squared"), sem("head_normed")
        s_gv, s_gln, s_nlf = sem("gates_in"), sem("gates_logged"), sem("gates_done")
        s_fs, s_fp, s_pv, s_fo = (sem(n) for n in ("fox_scores", "fox_probs", "fox_values_used", "fox_out"))
        s_conv, s_silu = sem("conv_done"), sem("silu_done")
        s_garg, s_dec, s_kop = (sem(n) for n in ("decay_argument", "decays_done", "gdn_operands"))
        s_lvl, s_T0 = sem("level_masked"), sem("inverse_start")
        s_os, s_go, s_gsq = sem("gdn_state_read"), sem("gdn_out"), sem("gdn_squares")
        s_qs = sem("query_squares_summed")
        s_xm, s_xe, s_xp = (sem(n) for n in ("xattn_max", "xattn_exp", "xattn_probs"))
        s_lg, s_re, s_sel, s_comb, s_flag = (sem(n) for n in (
            "logits", "router_exp", "selected", "combine_weights", "overflow_flag"))
        j_sel, j_ct, j_wt, j_ga, j_hg = (sem(n) for n in (
            "job_selection", "job_weights_turn", "job_weights_turned", "job_gather", "job_rows_gathered"))
        j_bias, j_gu, j_g, j_u, j_t, j_sg, j_a = (sem(n) for n in (
            "job_bias_used", "job_gate_up", "job_gate", "job_up", "job_product", "job_sigmoid", "job_act"))
        j_T, j_aT, j_D, j_y, j_sc, j_add = (sem(n) for n in (
            "job_act_turn", "job_act_turned", "job_down", "job_rows_out", "job_scattered", "job_added"))

        turn = {}
        uses = [0] * 8

        def plan(name, bank):
            turn[name] = (bank, uses[bank])
            uses[bank] += 1

        rot = [0]

        def plan_next(*names):
            for n in names:
                plan(n, rot[0] % 8)
                rot[0] += 1

        plan_next(*[f"xT{i}" for i in range(4)])
        plan_next("gate0", "gate1")
        plan_next("fq0", "fq1")
        plan_next(*[f"mT{i}" for i in range(4)])
        plan_next("fqs0", "fqs1", "fk0", "fk1", "cumT0", "cumT1", "fks0", "fks1", "fv0", "fv1")
        plan("gr0", 7)
        for h in range(FH + 2):
            if h < FH:
                if h % 2 == 0:
                    plan(f"fcum{h // 2}", 6)
                plan(f"fS{h}", h % 2)
            if 1 <= h <= FH:
                plan(f"fPT{h - 1}", 2 + (h - 1) % 2)
        plan("fo0", 4)
        plan("fo1", 5)
        rot[0] = 0
        plan_next("GS0", "GS1", "GB0", "GB1")
        plan("bB0", 6)
        plan("bB1", 7)
        for i, bank in enumerate((4, 5, 0, 1)):
            plan(f"gr{1 + i}", bank)
        rot[0] = 2
        plan_next("gs0", "gs1", "gr5", "gs2", "gs3")
        plan_next("z0", "z1", "fT0", "fT1", "kx0", "kx1")
        plan_next("kk0", "kk1", "ktok0", "vtok0", "ktok1", "vtok1", "qk0", "qk1")
        plan_next("kxs0", "kxs1", "X0_0", "X0_1", "kx2", "kx3", "kxs2", "kxs3")
        for n in range(len(LEVELS)):
            if n:
                plan(f"X{n}_0", 0)
                plan(f"X{n}_1", 1)
            if n > 0:
                for tb in range(TB):
                    if n < len(LEVELS) - 1:
                        plan(f"Y{n}_{tb}", 2 + tb)
                    plan(f"YT{n}_{tb}", 4 + tb)
        plan("w0", 6)
        plan("w1", 7)
        plan("vx0", 6)
        plan("vx1", 7)
        for c in range(4):
            plan(f"vn{c}", c % 2)
            if c % 2 == 0:
                plan(f"go{c // 2}", 4 + c // 2)
            if c < 3:
                plan(f"S{c}", 2 + c % 2)
        plan("gT0", 6)
        plan("gT1", 7)
        rot[0] = 0
        plan_next(*[f"wo{i}" for i in range(4)])
        plan_next("vx2", "vx3")
        for name, bank in (("h2T0", 6), ("h2T1", 7), ("h2T2", 0), ("h2T3", 1), ("qx0", 2), ("qx1", 3), ("qx2", 4),
                           ("qs", 6), ("qx3", 0)):
            plan(name, bank)
        for h in range(XH):
            plan(f"xS{h}", (3, 4, 7, 2)[h])
            plan(f"xPT{h}", h % 2)
            plan(f"xO{h}", (6, 5)[h % 2])
        rot[0] = 0
        plan_next(*[f"xo{i}" for i in range(4)])
        plan_next(*[f"h3T{i}" for i in range(4)])
        for name, bank in (("lg0", 4), ("lg1", 5), ("rank0", 4), ("rank1", 5), ("cT", 4), ("bd0", 5), ("bd1", 4),
                           ("bd2", 5), ("bd3", 4), ("cnt", 7)):
            plan(name, bank)

        def into(pe, name):
            bank, before = turn[name]
            if before:
                pe.wait_ge(free[bank], before)
            return ps[bank]

        def filled(ins, name):
            ins.then_inc(full[turn[name][0]], 1)

        def bank_of(eng, name):
            bank, before = turn[name]
            eng.wait_ge(full[bank], before + 1)
            return ps[bank]

        def read(ins, name):
            ins.then_inc(free[turn[name][0]], 1)


        w_in_v = w_in[0].rearrange("(p k) n -> p k n", k=KD)
        xkv_v = w_xkv[0].rearrange("(p k) n -> p k n", k=KD)
        xq_v = w_xq[0].rearrange("(p k) n -> p k n", k=KD)
        out_v = w_out[0].rearrange("(k p) n -> p k n", p=P)
        xo_v = w_xo[0].rearrange("(k p) n -> p k n", p=P)
        pre_fills = ([w_in_v[:, :, c:c + WIDE] for c in (FQ, FK, FV, GQ, GK, GV, GZ)]
                     + [xkv_v[:, :, WIDE * c:WIDE * c + WIDE] for c in range(3)]
                     + [out_v[:, :, WIDE * c:WIDE * c + WIDE] for c in range(2)]
                     + [xkv_v[:, :, 3 * WIDE:4 * WIDE]]
                     + [xq_v[:, :, WIDE * c:WIDE * c + WIDE] for c in range(2)]
                     + [xo_v[:, :, WIDE * c:WIDE * c + WIDE] for c in range(2)])
        assert len(pre_fills) == PRE_FILLS
        last_bank = ["fq1", "fk1", "fv1", "gr1", "gr3", "gr5", "z1", "kx1", "kx3", "vx1",
                     "wo1", "wo3", "vx3", "qx1", "qx3", "xo1", "xo3"]
        pre_count = [len(range(s, PRE_FILLS, PRE)) if s < PRE else 0 for s in range(RING)]

        def slot(s):
            if s < OWN:
                return ring[:, s * SLOT:(s + 1) * SLOT]
            return (early, kvx)[s - OWN][:, :]

        block = ctx.enter_context(nc.Block())

        def pre_w(pe, f):
            pe.wait_ge(landed[f % PRE], 16 * (f // PRE + 1))
            return slot(f % PRE).rearrange("p (k n) -> p k n", k=KD)

        def full_of(name):
            return full[turn[name][0]], turn[name][1] + 1

        def free_of(name):
            return free[turn[name][0]], turn[name][1] + 1

        gu_v = w_gate_up[0].rearrange("e (p k) n -> e p k n", k=KD)
        dn_v = w_down[0].rearrange("e (k p) n -> e p k n", p=P)

        job_fills = [(a, "gu", q) for q in range(4) for a in range(2)] + \
                    [(a, "dn", q) for q in range(2) for a in range(2)]
        TURNS = 2 * JOB_FILLS // RING

        def slot_of(p, m):
            return (JOB_FILLS * p + m) % RING

        def fills_before(i, p, m):
            return TURNS * i + (JOB_FILLS * p + m) // RING

        def gate_up_end(i, p):
            return spent[slot_of(p, 7)], fills_before(i, p, 7) + 1

        def down_end(i, p):
            return spent[slot_of(p, 11)], fills_before(i, p, 11) + 1

        @block.sync
        def _(sp):
            def pre_fill(f):
                if f >= PRE:
                    sp.wait_ge(*full_of(last_bank[f - PRE]))
                sp.dma_start(slot(f % PRE).rearrange("p (k n) -> p k n", k=KD), pre_fills[f]).then_inc(landed[f % PRE], 16)

            def expert_fill(i, p, m, pair, fresh=False):
                a, kind, q = job_fills[m]
                s = slot_of(p, m)
                if not fresh:
                    sp.wait_ge(spent[s], fills_before(i, p, m))
                e = 2 * pair + a
                view, nk = (gu_v, 2) if kind == "gu" else (dn_v, 4)
                if isinstance(e, int):
                    src = view[e, :, nk * q:nk * q + nk, :]
                else:
                    src = view[bass.ds(e, 1), :, nk * q:nk * q + nk, :].rearrange("e p k n -> p (e k) n")
                sp.dma_start(slot(s).rearrange("p (k n) -> p k n", k=nk), src).then_inc(landed[s], 16)

            def job(i, p, pair):
                sp.wait_ge(j_bias, 2 * i + p)
                sp.dma_start(bgu, b_gate_up[0, bass.ds(2 * pair, 2), :]).then_inc(s_bgu, 16)
                for m in range(JOB_FILLS):
                    expert_fill(i, p, m, pair)

            rows_out = out[0].rearrange("(t p) d -> p t d", p=P)

            def store(jobs):
                for n in range(2):
                    sp.wait_ge(j_add, 4 * jobs - 2 + 2 * n)
                    c = slice(WIDE * n, WIDE * n + WIDE)
                    sp.dma_start(rows_out[:, :, c], xs[:, :, c]).then_inc(s_out, 16)

            def load(dst, src, s=s_par):
                sp.dma_start(dst, src, allow_slow_non_contiguous=True).then_inc(s, 16)

            for tb in range(TB):
                load(xs[:, tb, :], x[0, P * tb:P * tb + P, :], s_x[tb])
            for tb in range(TB):
                sp.wait_ge(s_x[tb], 16)
            pre_fill(0)
            load(mn, mem[0].rearrange("(t p) d -> p t d", p=P), s_mem)
            for i, g in enumerate((fox_q_gain, fox_k_gain)):
                load(fqk_gain[0:FD, i:i + 1], g[0].rearrange("(p o) -> p o", o=1))
                load(fqk_gain[FD:P, i:i + 1], g[0].rearrange("(p o) -> p o", o=1))
            load(fout_gain[:, :], fox_out_gain[0].rearrange("(j a) d -> (a d) j", a=2))
            load(gout_gain[:, :], gdn_out_gain[0].rearrange("(p o) -> p o", o=1))
            load(conv_w[:, :, :], gdn_conv_w[0].rearrange("(j p) k -> p j k", p=P))
            load(gate_b[:, 0:FH], b_forget[0:1, :].to_broadcast([P, FH]))
            load(gate_b[:, FH:12], gdn_dt_bias[0:1, :].to_broadcast([P, GH]))
            load(alog[:, :], gdn_a_log[0:1, :].to_broadcast([P, GH]))
            load(brt[:, :], b_router[0:1, :].to_broadcast([P, NE]))
            for i, g in enumerate((xq_gain, xk_gain)):
                load(x_gain[:, i, :], g[0].rearrange("(j p) -> p j", p=P))
            load(wr[:, :, :], w_router[0].rearrange("(p k) n -> p k n", k=KD))
            for f in range(1, PRE_FILLS - 3):
                pre_fill(f)
            sp.wait_ge(*free_of("gT1"))
            for m in range(PRE, OWN):
                expert_fill(0, 0, m, 0, fresh=True)
            for f in range(PRE_FILLS - 3, PRE_FILLS):
                pre_fill(f)
            for m, name in ((6, "vx3"), (2, "qx3"), (7, f"xO{XH - 1}"), (0, "xo1"), (1, "xo3")):
                sp.wait_ge(*full_of(name))
                if m == 2:
                    sp.wait_ge(*full_of("qs"))
                    sp.dma_start(bgu0, b_gate_up[0, 0:2, :]).then_inc(s_bgu, 16)
                if m == 7:
                    sp.dma_start(bdn, b_down[0]).then_inc(s_bdn, 16)
                expert_fill(0, 0, m, 0, fresh=True)
            for m in range(RING, JOB_FILLS):
                expert_fill(0, 0, m, 0)
            job(0, 1, 1)
            with sp.Fori(1, PAIRS // 2) as i:
                for p in range(2):
                    job(i, p, 2 * i + p)
            sp.wait_ge(s_flag, 1)
            more = sp.value_load(flag[0:1, 0:1], min_val=0, max_val=1)
            with sp.If(more > 0):
                with sp.Fori(1, ROUNDS) as r:
                    with sp.Fori(0, PAIRS // 2) as i:
                        for p in range(2):
                            job(r * (PAIRS // 2) + i, p, 2 * i + p)
                store(ROUNDS * PAIRS)
            with sp.Else():
                store(PAIRS)
            sp.wait_ge(s_out, 16 * 2)

        @block.gpsimd
        def _(pool):
            steps = [0]

            def step(ins):
                steps[0] += 1
                ins.then_inc(s_gc, 1)
                pool.wait_ge(s_gc, steps[0])

            def keep(out_, pattern, base, mult, fill, op=ALU.is_ge):
                step(pool.affine_select(out=out_, in_=out_, compare_op=op, fill=fill, base=base,
                                        pattern=pattern, channel_multiplier=mult))

            step(pool.memset(ident[:, :], 0.0))
            step(pool.memset(eps[:, :], EPS))
            keep(ident[:, :], [[-1, P]], 0, 1, 1.0, ALU.not_equal)
            pool.memset(fqz, 0.0).then_inc(s_ident, 1)
            step(pool.memset(ones[:, :], 1.0))
            step(pool.memset(prefix[:, :], 1.0))
            keep(prefix[:, :], [[1, P]], 0, -1, 0.0)
            step(pool.memset(cones[:, :], 0.0))
            step(pool.memset(cones[0:CHUNK, 0:CHUNK], 1.0))
            step(pool.memset(cones[CHUNK:P, CHUNK:P], 1.0))
            step(pool.tensor_tensor(cprefix[:, :], cones[:, :], prefix[:, :], ALU.mult))
            step(pool.memset(fmask[:, :, :], 0.0))
            keep(fmask[:, 1, :], [[-1, P]], 0, 1, NEG)
            step(pool.tensor_scalar(dmask[:, :], cprefix[:, :], -NEG, NEG, ALU.mult, ALU.add))
            step(pool.memset(lmask[:, :, :], 0.0))
            for n, w in enumerate(LEVELS):
                nb = P // (2 * w)
                upper = lmask[:, n, :].rearrange("p (b u w) -> p b u w", b=nb, u=2)[:, :, 1, :]
                step(pool.memset(upper, 1.0))
                keep(upper, [[-2 * w, nb], [0, w]], 0, 1, 0.0)
                keep(upper, [[2 * w, nb], [0, w]], w - 1, -1, 0.0)
            step(pool.iota(slot_no[:, :], pattern=[[1, SLOTS]], base=1, channel_multiplier=0,
                           allow_small_or_imprecise_dtypes=True))
            step(pool.memset(pairsel[:, :], 1.0))
            keep(pairsel[:, :], [[-1, P]], SLOTS - 1, SLOTS, 0.0)
            keep(pairsel[:, :], [[1, P]], 0, -SLOTS, 0.0)
            pool.memset(raw[:, :, 0:CONV - 1], 0.0).then_inc(s_const, 1)

            for n in range(len(LEVELS)):
                if n == 3:
                    pool.wait_ge(s_T0, 2)
                for tb in range(TB):
                    if n == 0:
                        pool.wait_ge(s_fo, TB)
                        pool.wait_ge(*free_of(f"kk{tb}"))
                        pool.wait_ge(*free_of(f"fT{tb}"))
                    if n >= 3:
                        pool.wait_ge(*full_of(f"X{n - 3}_{tb}"))
                    pool.tensor_tensor(ATl[n % 3][:, tb, :, :], AT[:, tb, :, :],
                                       lmask[:, n:n + 1, :].to_broadcast([P, GH, P]), ALU.mult).then_inc(s_lvl, 1)

        @block.scalar
        def _(act):
            def load(dst, src, s):
                act.dma_start(dst, src, allow_slow_non_contiguous=True).then_inc(s, 16)

            load(gains[:, 0, :], mix_norm[0].rearrange("(p k) -> p k", k=KD), s_gain)
            load(wsm[:, :, 0:8], w_in_v[:, :, FF:FF + 8], s_par2)
            load(wsm[:, :, 8:16], w_in_v[:, :, GA:GA + 8], s_par2)
            for i, g in enumerate((mem_norm, xattn_norm, moe_norm)):
                load(gains[:, 1 + i, :], g[0].rearrange("(p k) -> p k", k=KD), s_par)

            steps = [0]

            def link(ins):
                steps[0] += 1
                ins.then_inc(s_ac, 1)
                act.wait_ge(s_ac, steps[0])


            def root(dst, src, n):
                return act.activation(dst, src, ACT.Sqrt, scale=1.0 / n, bias=eps[:, 0:1])

            squares = [0]

            def root_mean_squares(src, junk, cols, arrived):
                for tb in range(TB):
                    for s, v in arrived[tb]:
                        act.wait_ge(s, v)
                    c = slice(cols + tb, cols + tb + 1)
                    act.activation(junk[:, tb, :], src[:, tb, :], ACT.Square, accum_out=ss[:, c]).then_inc(s_ss, 1)
                    squares[0] += 1
                    act.wait_ge(s_ss, squares[0])
                    root(rs[:, c], ss[:, c], D).then_inc(s_root, 1)

            def head_roots(name, i, n, before, tiles=2):
                b = bank_of(act, f"{name}{i}")
                if before > 0:
                    act.wait_ge(s_nrm, before)
                r = rn[:, :, :] if tiles == 2 else rn[:, i % 2:i % 2 + 1, :]
                read(root(r, b[:, 0:tiles * T].rearrange("p (a t) -> p a t", a=tiles), n), f"{name}{i}")

            act.wait_ge(s_ident, 1)
            root(rs[:, 7:8], eps[:, 0:1], 1.0)
            junk = cut(kvx, 0, TB, D)
            root_mean_squares(xs, junk, 2, [[(s_x[tb], 16)] for tb in range(TB)])
            root_mean_squares(mn, junk, 0, [[(s_mem, 16)], []])

            def project(name, dst, banks, sq_read, raws):
                for i in banks:
                    b = bank_of(act, f"{name}{i}")[:, :].rearrange("p (a t) -> p a t", a=2)
                    act.activation(dst[:, 2 * i:2 * i + 2, :], b, ACT.Copy).then_inc(s_raw, 1)
                    if sq_read[i] is not None:
                        s, v = sq_read[i]
                        act.wait_ge(s, v)
                    act.wait_ge(s_raw, raws + i + 1)
                    ins = act.activation(sq[:, 2 * (i % 2):2 * (i % 2) + 2, :], b, ACT.Square)
                    read(ins, f"{name}{i}")

            act.wait_ge(s_gv, 2)
            act.wait_ge(*free_of("gate0"))
            act.wait_ge(*free_of("gate1"))
            link(act.activation(gabs[:, :, :], gv[:, :, 0:12], ACT.Abs))
            link(act.activation(gabs[:, :, :], gabs[:, :, :], ACT.Exp, scale=-1.0))
            act.activation(gln[:, :, :], gabs[:, :, :], ACT.Ln, bias=1.0).then_inc(s_gln, 1)
            act.activation(beta[:, :, :], gv[:, :, 12:16], ACT.Exp, scale=-1.0).then_inc(s_gln, 1)
            act.wait_ge(s_par, 16 * 17)
            act.activation(ea[:, :], alog[:, :], ACT.Exp).then_inc(s_gln, 1)
            project("fq", fqT, range(2), [None, None], 0)
            for i in range(2):
                head_roots("fqs", i, FD, i)
            project("fk", fkT, range(2), [full_of("fqs0"), full_of("fqs1")], 2)
            for i in range(2):
                head_roots("fks", i, FD, 2 + i)
            for i in range(2):
                b = bank_of(act, f"fv{i}")
                read(act.activation(fv[:, i, :], b[:, :], ACT.Copy), f"fv{i}")

            for h in range(FH + 1):
                if h < FH:
                    act.wait_ge(s_fs, 2 * h + 2)
                    if h >= 2:
                        act.wait_ge(*full_of(f"fPT{h - 2}"))
                    act.activation(fP[:, h % 2, 0:P], fS[:, h % 2, 0:P], ACT.Exp, bias=fmx[:, h, 0:1],
                                   accum_out=fsum[:, h, 0:1]).then_inc(s_fp, 1)
                    act.activation(fP[:, h % 2, P:3 * P], fS[:, h % 2, P:3 * P], ACT.Exp, bias=fmx[:, h, 1:2],
                                   accum_out=fsum[:, h, 1:2]).then_inc(s_fp, 1)
                if h >= 1:
                    b = bank_of(act, f"fPT{h - 1}")
                    if h >= 3:
                        act.wait_ge(s_pv, h - 2)
                    ins = act.activation(fPT[:, (h - 1) % 2, :], b[:, 0:3 * P], ACT.Copy)
                    read(ins, f"fPT{h - 1}")

            def raw_in(i):
                b = bank_of(act, f"gr{i}")[:, :].rearrange("p (a t) -> p a t", a=2)
                read(act.activation(raw[:, 2 * i:2 * i + 2, CONV - 1:CONV - 1 + T], b, ACT.Copy), f"gr{i}")

            act.wait_ge(s_const, 1)
            raw_in(0)
            for tb in range(TB):
                act.wait_ge(s_arg, tb + 1)
                root(frs[:, tb, :], frs[:, tb, :], FD).then_inc(s_root, 1)

            act.wait_ge(s_garg, 1)
            act.activation(sc4[:, :, 0, :], gcum[:, :, 0, :], ACT.Exp).then_inc(s_dec, 1)
            act.activation(sc4[:, :, 2, :], sc4[:, :, 2, :], ACT.Exp).then_inc(s_dec, 1)
            for tb in range(TB):
                act.wait_ge(s_garg, 2 + tb)
                b = bank_of(act, f"GB{tb}")
                read(act.activation(expG[:, tb, :, :], b[:, :].rearrange("p (h c) -> p h c", h=GH), ACT.Exp), f"GB{tb}")
                act.activation(dec[:, tb, :, :], dec[:, tb, :, :], ACT.Exp).then_inc(s_dec, 1)
            def silu(i):
                act.wait_ge(s_conv, 4 * i + 4)
                act.activation(cv[:, 4 * i:4 * i + 4, :], cv[:, 4 * i:4 * i + 4, :], ACT.Silu).then_inc(s_silu, 1)

            for i in range(1, 4):
                raw_in(i)
            for i in range(4):
                if i % 2 == 0:
                    silu(i // 2)
                    act.wait_ge(s_silu, i // 2 + 1)
                if i == 0:
                    act.wait_ge(s_fo, TB)
                if i >= 2:
                    act.wait_ge(*full_of(f"gs{i - 2}"))
                act.activation(sq[:, 2 * (i % 2):2 * (i % 2) + 2, :], cv[:, 2 * i:2 * i + 2, :], ACT.Square).then_inc(s_sq, 1)
                if i % 2:
                    raw_in(4 + i // 2)
            for i in range(4):
                head_roots("gs", i, 1.0, 4 + i)
            silu(2)
            for i in range(2):
                b = bank_of(act, f"z{i}")
                read(act.activation(zs[:, i, :], b[:, :], ACT.Silu), f"z{i}")
            for i0 in (0, 2):
                project("kx", kxT, range(i0, i0 + 2), [full_of("gs2"), full_of("gs3"), full_of("kxs0"), full_of("kxs1")], 4)
                for i in (i0, i0 + 1):
                    head_roots("kxs", i, XD, max(8, 8 + i - 1), tiles=1)
            for n in range(1, len(LEVELS)):
                for tb in range(TB):
                    b = bank_of(act, f"X{n}_{tb}")
                    if n >= 2:
                        act.wait_ge(*full_of(f"YT{n - 1}_{tb}"))
                    read(act.activation(Xi[:, tb, :, :], b[:, :].rearrange("p (h c) -> p h c", h=GH), ACT.Copy), f"X{n}_{tb}")
            for tb in range(TB):
                b = bank_of(act, f"w{tb}")
                read(act.activation(wTn[:, tb, :, :], b[:, :].rearrange("p (h c) -> p h c", h=GH), ACT.Copy), f"w{tb}")
            def memory_values(i):
                b = bank_of(act, f"vx{i}")
                read(act.activation(vx[:, i % 2, WIDE * (i // 2):WIDE * (i // 2) + WIDE], b[:, :], ACT.Copy), f"vx{i}")

            memory_values(0)
            memory_values(1)
            for tb in range(TB):
                b = bank_of(act, f"go{tb}")
                act.activation(gsq[:, 0, :], b[:, :], ACT.Square).then_inc(s_gsq, 1)
                act.wait_ge(s_gsq, 2 * tb + 2)
                root(grs[:, tb, :], grs[:, tb, :], GD).then_inc(s_root, 1)

            root_mean_squares(xs, cut(work, 0, TB, D), 0, [[free_of(f"wo{tb}"), free_of(f"wo{2 + tb}")] for tb in range(TB)])
            memory_values(2)
            project("qx", qxT, range(4), [full_of("kxs2"), full_of("kxs3"), (s_qs, 1), (s_qs, 2)], 8)
            b = bank_of(act, "qs")
            read(root(xqr[:, :, :], b[:, 0:TB * XH].rearrange("p (t h) -> p t h", t=TB), XD), "qs")

            def exps(h):
                act.wait_ge(s_xm, h + 1)
                b = bank_of(act, f"xS{h}")[:, :].rearrange("p (a t) -> p a t", a=2)
                for qb in range(2):
                    ins = act.activation(xP[:, h, T * qb:T * qb + T], b[:, qb, :], ACT.Exp, scale=xqr[:, qb, h:h + 1],
                                         bias=xmx[:, h, qb:qb + 1], accum_out=xsum[:, h, qb:qb + 1])
                    if qb:
                        read(ins, f"xS{h}")
                    else:
                        ins.then_inc(s_xe, 1)

            def turned_probs(h):
                b = bank_of(act, f"xPT{h}")
                if h >= 2:
                    act.wait_ge(*full_of(f"xO{h - 2}"))
                read(act.activation(xPT[:, h % 2, :], b[:, :], ACT.Copy), f"xPT{h}")

            def outputs(h):
                b = bank_of(act, f"xO{h}")[:, :].rearrange("p (a t) -> p a t", a=2)
                read(act.activation(mixT[:, 2 * h:2 * h + 2, :], b, ACT.Copy), f"xO{h}")

            for step, h in (("S", 0), ("S", 1), ("S", 2), ("T", 0), ("S", 3), ("T", 1), ("O", 0), ("T", 2), ("O", 1),
                            ("T", 3), ("O", 2), ("O", 3)):
                if step == "S":
                    exps(h)
                elif step == "T":
                    if h == 0:
                        memory_values(3)
                    turned_probs(h)
                else:
                    outputs(h)

            root(rs[:, 7:8], eps[:, 0:1], 1.0)
            root_mean_squares(xs, cut(work, 2048, TB, D), 4, [[free_of(f"xo{tb}"), free_of(f"xo{2 + tb}")] for tb in range(TB)])
            for tb in range(TB):
                act.wait_ge(s_lg, tb + 1)
                act.activation(rt[:, tb, 3, :], lg[:, tb, :], ACT.Exp, bias=rcol[:, tb, 3:4]).then_inc(s_re, 1)
            b = bank_of(act, "cT")
            read(act.activation(combT[:, :], b[0:NE, 0:T], ACT.Copy), "cT")

            def job(i, p):
                j = 2 * i + p
                for a in range(2):
                    act.wait_ge(j_g, 2 * j + a + 1)
                    act.activation(sS[:, a, :], gS[:, a, :], ACT.Sigmoid, scale=ALPHA).then_inc(j_sg, 1)
                for a in range(2):
                    act.wait_ge(j_T, 2 * j + a + 1)
                    act.activation(actT[:, 4 * a:4 * a + 4, :], ps[a][:, :].rearrange("p (k s) -> p k s", k=4),
                                   ACT.Copy).then_inc(j_aT, 1)
                for a in range(2):
                    if a == 0:
                        act.wait_ge(j_D, j + 1)
                    else:
                        act.wait_ge(*down_end(i, p))
                    act.activation(yS[:, a, :], ps[4 + a][:, :], ACT.Copy).then_inc(j_y, 1)

            def jobs(i0, i1):
                with act.Fori(i0, i1) as i:
                    job(i, 1)
                    job(i + 1, 0)

            job(0, 0)
            jobs(0, PAIRS // 2 - 1)
            act.wait_ge(s_flag, 1)
            more = act.value_load(flag[0:1, 0:1], min_val=0, max_val=1)
            with act.If(more > 0):
                jobs(PAIRS // 2 - 1, ROUNDS * PAIRS // 2 - 1)
                job(ROUNDS * PAIRS // 2 - 1, 1)
            with act.Else():
                job(PAIRS // 2 - 1, 1)

        @block.vector
        def _(dve):
            V = nc.vector
            steps = [0]

            def link(ins):
                steps[0] += 1
                ins.then_inc(s_dv, 1)
                dve.wait_ge(s_dv, steps[0])

            rooted = [0]

            def root_wait():
                rooted[0] += 1
                dve.wait_ge(s_root, rooted[0])

            def norm_rows(src, dst, cols, blocks=range(TB)):
                for tb in blocks:
                    root_wait()
                    r = rs[:, cols + tb:cols + tb + 1]
                    link(V.reciprocal(r, r))
                    V.tensor_scalar(dst[:, tb, :], src[:, tb, :], r, None, ALU.mult).then_inc(s_hn, 1)

            def turned(name, dst, gain, banks=range(4)):
                for i in banks:
                    q, tb = i % 2, i // 2
                    b = bank_of(dve, f"{name}{i}")[:, :].rearrange("p (k t) -> p k t", k=4)
                    ins = V.tensor_tensor(dst[:, 4 * q:4 * q + 4, P * tb:P * tb + P], b,
                                          gains[:, gain, 4 * q:4 * q + 4].unsqueeze(2).to_broadcast([P, 4, P]), ALU.mult)
                    read(ins, f"{name}{i}")

            norm_rows(xs, hn, 2)
            dve.wait_ge(s_gain, 16)
            turned("xT", hT, 0)
            norm_rows(mn, mn, 0)
            dve.wait_ge(s_par, 16 * 17)

            for tb in range(TB):
                b = bank_of(dve, f"gate{tb}")
                V.tensor_tensor(gv[:, tb, 0:12], b[:, 0:12], gate_b[:, :], ALU.add).then_inc(s_gv, 1)
                read(V.tensor_copy(gv[:, tb, 12:16], b[:, 12:16]), f"gate{tb}")
            def head_norm(name, i, dst, gain, tiles, root):
                dve.wait_ge(*free_of(f"{name}{i}"))
                r = rn[:, :, :] if tiles == 1 else rn[:, i % 2:i % 2 + 1, :]
                link(V.reciprocal(r, r))
                for c in range(tiles):
                    n = 2 // tiles
                    d = dst[:, 2 * i + c:2 * i + c + n, :]
                    ins = V.scalar_tensor_tensor(d, d, gain[c], r, ALU.mult, ALU.mult)
                    if c == tiles - 1:
                        ins.then_inc(s_nrm, 1)
                        dve.wait_ge(s_nrm, root)
                    else:
                        link(ins)

            dve.wait_ge(s_gln, 3)
            link(V.tensor_scalar(nlf[:, :, :], gv[:, :, 0:8], -1.0, 0.0, ALU.mult, ALU.max))
            V.tensor_tensor(nlf[:, :, :], nlf[:, :, :], gln[:, :, 0:8], ALU.add).then_inc(s_nlf, 1)
            link(V.tensor_scalar(gg[:, :, :], gv[:, :, 8:12], 0.0, None, ALU.max))
            link(V.tensor_tensor(gg[:, :, :], gg[:, :, :], gln[:, :, 8:12], ALU.add))
            link(V.scalar_tensor_tensor(gg[:, :, :], gg[:, :, :], -1.0,
                                        ea[:, :].unsqueeze(1).to_broadcast([P, TB, GH]), ALU.mult, ALU.mult))
            link(V.tensor_scalar(beta[:, :, :], beta[:, :, :], 1.0, None, ALU.add))
            V.reciprocal(beta[:, :, :], beta[:, :, :]).then_inc(s_nlf, 1)
            dve.wait_ge(s_nlf, 2)
            turned("mT", mT, 1)
            for i in range(2):
                dve.wait_ge(*free_of(f"fqs{i}"))
                link(V.reciprocal(rn[:, :, :], rn[:, :, :]))
                for half in range(2):
                    r = slice(FD * half, FD * half + FD)
                    d = fqz.rearrange("p (t a) n -> p t a n", a=2)[r, 2 * i:2 * i + 2, half, :]
                    ins = V.scalar_tensor_tensor(d, fqT[r, 2 * i:2 * i + 2, :], fqk_gain[r, 0:1], rn[r, :, :],
                                                 ALU.mult, ALU.mult)
                    if half:
                        ins.then_inc(s_nrm, 1)
                        dve.wait_ge(s_nrm, i + 1)
                    else:
                        link(ins)
            for i in range(2):
                head_norm("fks", i, fkT, [fqk_gain[:, 1:2]], 1, 3 + i)
            for tb in range(TB):
                b = bank_of(dve, f"cumT{tb}")
                read(V.tensor_copy(ncum[:, tb, :], b[:, 0:FH]), f"cumT{tb}")

            dve.wait_ge(s_const, 1)
            dve.wait_ge(*free_of("cumT1"))
            dve.wait_ge(*free_of("cumT0"))
            for h in range(FH):
                S = fS[:, h % 2, :]
                if h >= 2:
                    dve.wait_ge(s_fp, 2 * (h - 1))
                b = bank_of(dve, f"fcum{h // 2}")[:, T * (h % 2):T * (h % 2) + T]
                link(V.scalar_tensor_tensor(S[:, 0:P], b[:, 0:P], ncum[:, 0, h:h + 1], fmask[:, 1, :],
                                            ALU.subtract, ALU.add))
                ins = V.scalar_tensor_tensor(S[:, P:3 * P], b, ncum[:, 1, h:h + 1],
                                             fmask[:, :, :].rearrange("p a k -> p (a k)"), ALU.subtract, ALU.add)
                if h % 2:
                    read(ins, f"fcum{h // 2}")
                    dve.wait_ge(*free_of(f"fcum{h // 2}"))
                else:
                    link(ins)
                b = bank_of(dve, f"fS{h}")
                read(V.scalar_tensor_tensor(S, b[:, 0:3 * P], FD ** -0.5, S, ALU.mult, ALU.add), f"fS{h}")
                dve.wait_ge(*free_of(f"fS{h}"))
                V.tensor_reduce(fmx[:, h, 0:1], S[:, 0:P], AX.X, ALU.max, negate=True).then_inc(s_fs, 1)
                V.tensor_reduce(fmx[:, h, 1:2], S[:, P:3 * P], AX.X, ALU.max, negate=True).then_inc(s_fs, 1)

            dve.wait_ge(s_fp, 2 * FH)
            link(V.reciprocal(fsum[:, :, :], fsum[:, :, :]))
            fsq = sq[:, :, :].rearrange("p a t -> p (a t)")[:, 0:FH * FD]
            for tb in range(TB):
                b = bank_of(dve, f"fo{tb}")[:, :].rearrange("p (h d) -> p h d", h=FH)
                o = fo[:, tb, :].rearrange("p (h d) -> p h d", h=FH)
                read(V.tensor_tensor(o, b, fsum[:, :, tb:tb + 1].to_broadcast([P, FH, FD]), ALU.mult), f"fo{tb}")
                dve.wait_ge(*free_of(f"fo{tb}"))
                if tb == 0:
                    dve.wait_ge(*full_of("fks1"))
                link(V.tensor_tensor(fsq.rearrange("p (h d) -> p h d", h=FH), o, o, ALU.mult))
                V.tensor_reduce(frs[:, tb, :], fsq.rearrange("p (h d) -> p h d", h=FH), AX.X, ALU.add).then_inc(s_arg, 1)
                root_wait()
                link(V.reciprocal(frs[:, tb, :], frs[:, tb, :]))
                V.tensor_tensor(o, o, frs[:, tb, :].unsqueeze(2).to_broadcast([P, FH, FD]), ALU.mult).then_inc(s_fo, 1)

            for tb in range(TB):
                b = bank_of(dve, f"GS{tb}")
                read(V.tensor_copy(gcum[:, tb, :, :], b[:, 0:2 * GH].rearrange("p (a h) -> p a h", a=2)), f"GS{tb}")
                dve.wait_ge(*free_of(f"GS{tb}"))
            V.tensor_tensor(sc4[:, :, 2, :], gcum[:, :, 1, :], gcum[:, :, 0, :], ALU.subtract).then_inc(s_garg, 1)
            for tb in range(TB):
                b = bank_of(dve, f"GB{tb}")
                for h in range(GH):
                    ins = V.scalar_tensor_tensor(dec[:, tb, h, :], b[:, P * h:P * h + P], gcum[:, tb, 0, h:h + 1],
                                                 dmask[:, :], ALU.subtract, ALU.add)
                    if h < GH - 1:
                        link(ins)
                    else:
                        ins.then_inc(s_garg, 1)

            for i in range(12):
                if i == 4:
                    for tb in range(TB):
                        dve.wait_ge(s_dec, 3 + tb)
                        b = bank_of(dve, f"bB{tb}")[:, :].rearrange("p (h c) -> p h c", h=GH)
                        read(V.tensor_tensor(AT[:, tb, :, :], b, dec[:, tb, :, :], ALU.mult), f"bB{tb}")
                if i % 2 == 0:
                    dve.wait_ge(*free_of(f"gr{i // 2}"))
                link(V.tensor_scalar(cv[:, i, :], raw[:, i, 0:T], conv_w[:, i, 0:1], None, ALU.mult))
                for c in range(1, CONV):
                    ins = V.scalar_tensor_tensor(cv[:, i, :], raw[:, i, c:c + T], conv_w[:, i, c:c + 1], cv[:, i, :],
                                                 ALU.mult, ALU.add)
                    if c < CONV - 1:
                        link(ins)
                    else:
                        ins.then_inc(s_conv, 1)
            for i in range(4):
                head_norm("gs", i, cv, [GD ** -0.5 if i < 2 else 1.0], 1, 5 + i)
            for tb in range(TB):
                b = bank_of(dve, f"fT{tb}")[:, :].rearrange("p (k t) -> p k t", k=4)
                read(V.tensor_tensor(mixT[:, 0:4, P * tb:P * tb + P], b,
                                     fout_gain[:, :].unsqueeze(2).to_broadcast([P, 4, P]), ALU.mult), f"fT{tb}")
            for tb in range(TB):
                dve.wait_ge(*free_of(f"bB{tb}"))
                b = bank_of(dve, f"kk{tb}")[:, :].rearrange("p (h c) -> p h c", h=GH)
                read(V.tensor_tensor(AT[:, tb, :, :], b, AT[:, tb, :, :], ALU.mult), f"kk{tb}")
            dve.wait_ge(s_dec, 2)
            link(V.scalar_tensor_tensor(sc4[:, :, 1, :], sc4[:, :, 0, :], -1.0, beta[:, :, :], ALU.mult, ALU.mult))
            dve.wait_ge(*full_of("vtok1"))
            for tb in range(TB):
                b = bank_of(dve, f"ktok{tb}")[:, :].rearrange("p (h d) -> p h d", h=GH)
                V.tensor_tensor(kbn[:, tb, :, :], b, sc4[:, tb, 1, :].unsqueeze(2).to_broadcast([P, GH, GD]), ALU.mult).then_inc(s_kop, 1)
                read(V.tensor_tensor(kd[:, tb, :, :], b, sc4[:, tb, 2, :].unsqueeze(2).to_broadcast([P, GH, GD]), ALU.mult), f"ktok{tb}")
                b = bank_of(dve, f"vtok{tb}")[:, :].rearrange("p (h d) -> p h d", h=GH)
                read(V.tensor_tensor(vb[:, tb, :, :], b, beta[:, tb, :].unsqueeze(2).to_broadcast([P, GH, GD]), ALU.mult), f"vtok{tb}")
            for tb in range(TB):
                b = bank_of(dve, f"qk{tb}")[:, :].rearrange("p (h c) -> p h c", h=GH)
                read(V.tensor_tensor(qkT[:, tb, :, :], b, dec[:, tb, :, :], ALU.mult), f"qk{tb}")
            for tb in range(TB):
                V.tensor_tensor(qd[:, :, P * tb:P * tb + P], gq[:, :, P * tb:P * tb + P], expG[:, tb, :, :],
                                ALU.mult).then_inc(s_kop, 1)
            link(V.tensor_tensor(xqk_gain[:, :], x_gain[:, 0, :], x_gain[:, 1, :], ALU.mult))

            def key_norms(i):
                head_norm("kxs", i, kxT, [xqk_gain[:, c:c + 1] for c in range(2)], 2, 9 + i)

            idb = ident[:, :].unsqueeze(1).to_broadcast([P, GH, P])
            for tb in range(TB):
                dve.wait_ge(s_lvl, tb + 1)
                V.tensor_tensor(TiT[:, tb, :, :], idb, ATl[0][:, tb, :, :], ALU.subtract).then_inc(s_T0, 1)
                b = bank_of(dve, f"X0_{tb}")[:, :].rearrange("p (h c) -> p h c", h=GH)
                read(V.tensor_tensor(Ti[:, tb, :, :], idb, b, ALU.subtract), f"X0_{tb}")
            for i in range(4):
                key_norms(i)
            for n in range(1, len(LEVELS)):
                for tb in range(TB):
                    if n < len(LEVELS) - 1:
                        b = bank_of(dve, f"Y{n}_{tb}")[:, :].rearrange("p (h c) -> p h c", h=GH)
                        dve.wait_ge(*free_of(f"X0_{tb}" if n == 1 else f"Y{n - 1}_{tb}"))
                        read(V.tensor_tensor(Ti[:, tb, :, :], Ti[:, tb, :, :], b, ALU.subtract), f"Y{n}_{tb}")
                    b = bank_of(dve, f"YT{n}_{tb}")[:, :].rearrange("p (h c) -> p h c", h=GH)
                    if n == 1:
                        dve.wait_ge(s_T0, tb + 1)
                    else:
                        dve.wait_ge(*free_of(f"YT{n - 1}_{tb}"))
                    read(V.tensor_tensor(TiT[:, tb, :, :], TiT[:, tb, :, :], b, ALU.subtract), f"YT{n}_{tb}")

            for c in range(4):
                tb, r0 = c // 2, CHUNK * (c % 2)
                b = bank_of(dve, f"vn{c}")
                read(V.tensor_copy(vnew[r0:r0 + CHUNK, tb, :], b[r0:r0 + CHUNK, :]), f"vn{c}")
                if c < 3:
                    b = bank_of(dve, f"S{c}")[:, :].rearrange("p (h d) -> p h d", h=GH)
                    if c:
                        dve.wait_ge(*free_of(f"S{c - 1}"))
                        link(V.tensor_tensor(Sd, St, expG[:, tb, :, r0 + CHUNK - 1:r0 + CHUNK].to_broadcast([P, GH, GD]),
                                             ALU.mult))
                        dve.wait_ge(*(full_of(f"go{tb}") if c % 2 else (s_os, c // 2 + 1)))
                        read(V.tensor_tensor(St, Sd, b, ALU.add), f"S{c}")
                    else:
                        read(V.tensor_copy(St, b), f"S{c}")
            for tb in range(TB):
                dve.wait_ge(s_gsq, 2 * tb + 1)
                V.tensor_reduce(grs[:, tb, :], gsq[:, 0, :].rearrange("p (h d) -> p h d", h=GH), AX.X, ALU.add).then_inc(s_gsq, 1)
                root_wait()
                link(V.reciprocal(grs[:, tb, :], grs[:, tb, :]))
                b = bank_of(dve, f"go{tb}")[:, :].rearrange("p (h d) -> p h d", h=GH)
                g = go[:, tb, :].rearrange("p (h d) -> p h d", h=GH)
                read(V.tensor_tensor(g, b, grs[:, tb, :].unsqueeze(2).to_broadcast([P, GH, GD]), ALU.mult), f"go{tb}")
                dve.wait_ge(*free_of(f"go{tb}"))
                V.tensor_tensor(go[:, tb, :], go[:, tb, :], zs[:, tb, :], ALU.mult).then_inc(s_go, 1)
            for tb in range(TB):
                b = bank_of(dve, f"gT{tb}")[:, :].rearrange("p (k t) -> p k t", k=4)
                read(V.tensor_scalar(mixT[:, 4:8, P * tb:P * tb + P], b, gout_gain[:, 0:1], None, ALU.mult), f"gT{tb}")
                dve.wait_ge(*free_of(f"gT{tb}"))

            def residual(name, banks=range(4)):
                for i in banks:
                    b = bank_of(dve, f"{name}{i}")
                    n0 = WIDE * (i // 2)
                    dst = xs[:, i % 2, n0:n0 + WIDE]
                    read(V.tensor_tensor(dst, dst, b[:, :], ALU.add), f"{name}{i}")
                for i in banks:
                    dve.wait_ge(*free_of(f"{name}{i}"))

            residual("wo")
            norm_rows(xs, hn, 0)
            turned("h2T", hT, 2)
            dve.wait_ge(*free_of("qs"))
            link(V.reciprocal(xqr[:, :, :], xqr[:, :, :]))
            link(V.tensor_scalar(xqr[:, :, :], xqr[:, :, :], XD ** -0.5, None, ALU.mult))

            def row_max(h):
                b = bank_of(dve, f"xS{h}")[:, :].rearrange("p (a t) -> p a t", a=2)
                link(V.tensor_reduce(xmx[:, h, :], b, AX.X, ALU.max))
                V.scalar_tensor_tensor(xmx[:, h, :], xmx[:, h, :], -1.0, xqr[:, :, h], ALU.mult, ALU.mult).then_inc(s_xm, 1)

            def over_sums(h):
                dve.wait_ge(s_xe, h + 1)
                dve.wait_ge(*free_of(f"xS{h}"))
                link(V.reciprocal(xsum[:, h, :], xsum[:, h, :]))
                pv = xP[:, h, :].rearrange("p (a t) -> p a t", a=2)
                V.tensor_tensor(pv, pv, xsum[:, h, :].unsqueeze(2).to_broadcast([P, 2, T]), ALU.mult).then_inc(s_xp, 1)

            row_max(0)
            row_max(1)
            over_sums(0)
            row_max(2)
            over_sums(1)
            row_max(3)
            over_sums(2)
            over_sums(3)

            residual("xo", range(3))
            norm_rows(xs, hn, 4, [0])
            turned("h3T", hT, 3, range(2))
            residual("xo", [3])
            norm_rows(xs, hn, 4, [1])
            turned("h3T", hT, 3, range(2, 4))

            for tb in range(TB):
                b = bank_of(dve, f"lg{tb}")
                L = lg[:, tb, :]
                read(V.tensor_tensor(L, b[:, 0:NE], brt[:, :], ALU.add), f"lg{tb}")
                dve.wait_ge(*free_of(f"lg{tb}"))
                link(V.max(top8[:, tb, :], L))
                link(V.tensor_scalar(rcol[:, tb, 3:4], top8[:, tb, 0:1], -1.0, None, ALU.mult))
                V.tensor_scalar(rt[:, tb, 0, :], L, top8[:, tb, TOPK - 1:TOPK], None, ALU.is_gt).then_inc(s_lg, 1)
                link(V.tensor_scalar(rt[:, tb, 1, :], L, top8[:, tb, TOPK - 1:TOPK], None, ALU.is_equal))
                dve.wait_ge(s_lg, tb + 1)
                link(V.tensor_reduce(rcol[:, tb, 0:1], rt[:, tb, 0, :], AX.X, ALU.add))
                link(V.tensor_scalar(rcol[:, tb, 1:2], rcol[:, tb, 0:1], -1.0, float(TOPK), ALU.mult, ALU.add))
                link(V.tensor_tensor_scan(rt[:, tb, 2, :], ones[:, 0:NE], rt[:, tb, 1, :], 0.0, ALU.mult, ALU.add))
                link(V.scalar_tensor_tensor(rt[:, tb, 1, :], rt[:, tb, 2, :], rcol[:, tb, 1:2], rt[:, tb, 1, :],
                                            ALU.is_le, ALU.mult))
                V.tensor_tensor(sel[:, tb, :], rt[:, tb, 0, :], rt[:, tb, 1, :], ALU.add).then_inc(s_sel, 1)
                dve.wait_ge(s_sel, tb + 1)
                dve.wait_ge(s_re, tb + 1)
                link(V.tensor_tensor(comb[:, tb, :], rt[:, tb, 3, :], sel[:, tb, :], ALU.mult))
                link(V.tensor_reduce(rcol[:, tb, 2:3], comb[:, tb, :], AX.X, ALU.add))
                link(V.reciprocal(rcol[:, tb, 2:3], rcol[:, tb, 2:3]))
                V.tensor_scalar(comb[:, tb, :], comb[:, tb, :], rcol[:, tb, 2:3], None, ALU.mult).then_inc(s_comb, 1)
            dve.wait_ge(s_comb, 2)
            for tb in range(TB):
                b = bank_of(dve, f"rank{tb}")
                read(V.tensor_tensor(posx[:, tb, 0:NE], b[:, 0:NE], sel[:, tb, :], ALU.mult), f"rank{tb}")
                dve.wait_ge(*free_of(f"rank{tb}"))

            def places(r):
                link(V.tensor_scalar(posx[:, :, NE * r:NE * r + NE], posx[:, :, 0:NE], -1.0 * SLOTS * r, None, ALU.add))
                link(V.tensor_copy(combx[:, :, NE * r:NE * r + NE], comb))

            sel4 = Sel.rearrange("p t (a s) -> p t a s", a=2)
            cw4 = CW.rearrange("p t (a s) -> p t a s", a=2)

            def select(j, first=False):
                def col(buf, tb, a):
                    return buf[:, tb, 2 * j + a:2 * j + a + 1] if isinstance(j, int) else buf[:, tb, bass.ds(2 * j + a, 1)]

                for tb in range(TB):
                    for a in range(2):
                        V.tensor_scalar(sel4[:, tb, a, :], slot_no[:, :], col(posx, tb, a), None,
                                        ALU.is_equal).then_inc(j_sel, 1)
                for tb in range(TB):
                    for a in range(2):
                        V.tensor_scalar(cw4[:, tb, a, :], slot_no[:, :], col(posx, tb, a), col(combx, tb, a),
                                        ALU.is_equal, ALU.mult).then_inc(j_sel, 1)

            def gathered(j):
                for a in range(2):
                    dve.wait_ge(j_ga, 2 * j + a + 1)
                    V.tensor_tensor(hgT[:, 4 * a:4 * a + 4, :], ps[6 + a][:, :].rearrange("p (k s) -> p k s", k=4),
                                    gains[:, 3, 4 * a:4 * a + 4].unsqueeze(2).to_broadcast([P, 4, P]), ALU.mult).then_inc(j_hg, 1)

            select(0)
            gathered(0)
            for r in range(1, ROUNDS + 1):
                places(r)
            residual("bd", range(2))

            def overflow():
                b = bank_of(dve, "cnt")
                read(V.tensor_reduce(flag_f[:, :], b[:, 0:NE], AX.X, ALU.max), "cnt")
                dve.wait_ge(*free_of("cnt"))
                link(V.tensor_scalar(flag_f[:, :], flag_f[:, :], float(SLOTS), None, ALU.is_gt))
                V.tensor_copy(flag[:, :], flag_f[:, :]).then_inc(s_flag, 1)

            def add(j, n, banks):
                for tb in range(TB):
                    dve.wait_ge(j_sc, 4 * j + 2 * n + tb + 1)
                    dst = xs[:, tb, WIDE * n:WIDE * n + WIDE]
                    V.tensor_tensor(dst, dst, ps[banks[tb]][:, :], ALU.add).then_inc(j_add, 1)

            def job(i, p, first=False, last=False):
                j = 2 * i + p
                for a in range(2):
                    if a == 0:
                        dve.wait_ge(j_gu, j + 1)
                    else:
                        dve.wait_ge(*gate_up_end(i, p))
                    V.tensor_scalar(gS[:, a, :], ps[a][:, :], LIMIT, None, ALU.min).then_inc(j_g, 1)
                    V.tensor_scalar(uS[:, a, :], ps[2 + a][:, :], LIMIT, -LIMIT, ALU.min, ALU.max).then_inc(j_u, 1)
                    dve.wait_ge(j_u, 2 * j + a + 1)
                    dve.wait_ge(j_g, 2 * j + a + 1)
                    V.scalar_tensor_tensor(uS[:, a, :], uS[:, a, :], 1.0, gS[:, a, :], ALU.add, ALU.mult).then_inc(j_t, 1)
                    dve.wait_ge(j_sg, 2 * j + a + 1)
                    dve.wait_ge(j_t, 2 * j + a + 1)
                    V.tensor_tensor(aS[:, a, :], uS[:, a, :], sS[:, a, :], ALU.mult).then_inc(j_a, 1)
                if first:
                    residual("bd", range(2, 4))
                    overflow()
                else:
                    add(j - 1, 0, (6, 7))
                    add(j - 1, 1, (4, 5))
                dve.wait_ge(j_ct, j + 1)
                V.tensor_copy(WT[:, :, :], ps[2][:, 0:T].rearrange("p (t s) -> p t s", t=TB)).then_inc(j_wt, 1)
                if last:
                    add(j, 0, (6, 7))
                    add(j, 1, (0, 1))
                else:
                    select(j + 1)
                    gathered(j + 1)

            def jobs(i0, i1):
                with dve.Fori(i0, i1) as i:
                    job(i, 1)
                    job(i + 1, 0)

            job(0, 0, first=True)
            jobs(0, PAIRS // 2 - 1)
            dve.wait_ge(s_flag, 1)
            more = dve.value_load(flag[0:1, 0:1], min_val=0, max_val=1)
            with dve.If(more > 0):
                jobs(PAIRS // 2 - 1, ROUNDS * PAIRS // 2 - 1)
                job(ROUNDS * PAIRS // 2 - 1, 1, last=True)
            with dve.Else():
                job(PAIRS // 2 - 1, 1, last=True)

        @block.tensor
        def _(pe):
            M = nc.tensor

            def turn_rows(src, name, ready, banks=range(4)):
                for i in banks:
                    q, tb = i % 2, i // 2
                    pe.wait_ge(s_hn, ready + tb)
                    b = into(pe, f"{name}{i}")
                    for k in range(4):
                        ins = M.transpose(b[:, P * k:P * k + P],
                                          src[:, tb, :].rearrange("p (d k) -> p k d", k=KD)[:, 4 * q + k, :], ident[:, :])
                    filled(ins, f"{name}{i}")

            def channel_banks(w, rhsT, name, i0=0, banks=range(2)):
                for i in banks:
                    b = into(pe, f"{name}{i0 + i}")
                    for c in range(2):
                        for k in range(KD):
                            ins = M.matmul(b[:, T * c:T * c + T], w[:, k, P * (2 * i + c):P * (2 * i + c) + P], rhsT[:, k, :],
                                           start=(k == 0), stop=(k == KD - 1))
                    filled(ins, f"{name}{i0 + i}")

            def token_bank(w, lhs, name, tb):
                b = into(pe, name)
                for k in range(KD):
                    ins = M.matmul(b[:, :], lhs[:, k, P * tb:P * tb + P], w[:, k, :], start=(k == 0), stop=(k == KD - 1))
                filled(ins, name)

            def evacuated(name):
                pe.wait_ge(*free_of(name))

            pe.wait_ge(s_ident, 1)
            for _ in range(WARM_UP):
                M.matmul(ps[7][:, 0:P], ident[:, :], ident[:, :], start=True, stop=True)
            turn_rows(hn, "xT", 1)
            pe.wait_ge(s_par2, 32)
            for i in range(4):
                evacuated(f"xT{i}")
            for tb in range(TB):
                b = into(pe, f"gate{tb}")
                for k in range(KD):
                    ins = M.matmul(b[:, 0:16], hT[:, k, P * tb:P * tb + P], wsm[:, k, :], start=(k == 0), stop=(k == KD - 1))
                filled(ins, f"gate{tb}")

            def sumsq(name, src, i, width):
                b = into(pe, f"{name}{i}")
                q = sq[:, 2 * (i % 2):2 * (i % 2) + 2, :].rearrange("p a t -> p (a t)")
                if width == 1:
                    M.matmul(b[:, 0:T], ones[:, :], q[:, 0:T], start=True, stop=False)
                    ins = M.matmul(b[:, 0:T], ones[:, :], q[:, T:2 * T], start=False, stop=True)
                else:
                    ins = M.matmul(b[:, :], src[:, :], q, start=True, stop=True)
                filled(ins, f"{name}{i}")

            channel_banks(pre_w(pe, 0), hT, "fq")
            turn_rows(mn, "mT", 3)
            pe.wait_ge(s_const, 1)
            for i in range(2):
                evacuated(f"fq{i}")
                sumsq("fqs", cones, i, 2)
            channel_banks(pre_w(pe, 1), hT, "fk")
            pe.wait_ge(s_nlf, 2)
            b = into(pe, "cumT0")
            filled(M.matmul(b[:, 0:FH], prefix[:, :], nlf[:, 0, :], start=True, stop=True), "cumT0")
            b = into(pe, "cumT1")
            M.matmul(b[:, 0:FH], ones[:, :], nlf[:, 0, :], start=True, stop=False)
            filled(M.matmul(b[:, 0:FH], prefix[:, :], nlf[:, 1, :], start=False, stop=True), "cumT1")
            for i in range(2):
                evacuated(f"fk{i}")
                sumsq("fks", cones, i, 2)
            w = pre_w(pe, 2)
            for tb in range(TB):
                token_bank(w, hT, f"fv{tb}", tb)
            for i in range(2):
                evacuated(f"fv{i}")
            pe.wait_ge(s_nrm, 4)

            def first_projection(i0, i1):
                w, b = pre_w(pe, 3), ps[turn["gr0"][0]]
                if i0 == 0:
                    into(pe, "gr0")
                for i in range(i0, i1):
                    c, k = divmod(i, KD)
                    ins = M.matmul(b[:, T * c:T * c + T], w[:, k, P * c:P * c + P], hT[:, k, :], start=(k == 0), stop=(k == KD - 1))
                if i1 == 2 * KD:
                    filled(ins, "gr0")

            def decay_sums(tb):
                b = into(pe, f"GS{tb}")
                M.matmul(b[:, 0:GH], cprefix[:, :], gg[:, tb, :], start=True, stop=True)
                filled(M.matmul(b[:, GH:2 * GH], cones[:, :], gg[:, tb, :], start=True, stop=True), f"GS{tb}")

            def decay_row(name, src, rhs):
                tb = int(name[-1])
                b = into(pe, name)
                for h in range(GH):
                    ins = M.matmul(b[:, P * h:P * h + P], src[:, tb, h:h + 1].to_broadcast([P, P]), rhs[:, :],
                                   start=True, stop=True)
                filled(ins, name)

            for h in range(FH + 2):
                if h < FH:
                    if h % 2 == 0:
                        b = into(pe, f"fcum{h // 2}")
                        for c in range(2):
                            row = [nlf[:, tb, h + c:h + c + 1].to_broadcast([P, P]) for tb in range(TB)]
                            M.matmul(b[:, T * c:T * c + P], row[0], prefix[:, :], start=True, stop=True)
                            M.matmul(b[:, T * c + P:T * c + T], row[0], ones[:, :], start=True, stop=False)
                            ins = M.matmul(b[:, T * c + P:T * c + T], row[1], prefix[:, :], start=False, stop=True)
                        filled(ins, f"fcum{h // 2}")
                    b = into(pe, f"fS{h}")
                    M.matmul(b[:, 0:P], fqz[:, h, 0:P], fkT[:, h // 2, 0:P], start=True, stop=True)
                    filled(M.matmul(b[:, P:3 * P], fqz[:, h, P:T], fkT[:, h // 2, :], start=True, stop=True), f"fS{h}")
                if 1 <= h <= FH:
                    g = h - 1
                    first_projection(2 * h - 2, 2 * h)
                    pe.wait_ge(s_fp, 2 * h)
                    b = into(pe, f"fPT{g}")
                    for i in range(3):
                        ins = M.transpose(b[:, P * i:P * i + P], fP[:, g % 2, P * i:P * i + P], ident[:, :])
                    filled(ins, f"fPT{g}")
                if h == FH + 1:
                    decay_sums(0)
                    decay_sums(1)
                    decay_row("GB0", gg, cprefix)
                    decay_row("bB0", beta, ident)
                if h >= 2:
                    g = h - 2
                    evacuated(f"fPT{g}")
                    if g == 0:
                        o0, o1 = into(pe, "fo0"), into(pe, "fo1")
                    pt, c0 = fPT[:, g % 2, :], FD * g
                    i0 = M.matmul(o0[:, c0:c0 + FD], pt[:, 0:P], fv[:, 0, c0:c0 + FD], start=True, stop=True)
                    M.matmul(o1[:, c0:c0 + FD], pt[:, P:2 * P], fv[:, 0, c0:c0 + FD], start=True, stop=False)
                    i1 = M.matmul(o1[:, c0:c0 + FD], pt[:, 2 * P:3 * P], fv[:, 1, c0:c0 + FD], start=False, stop=True)
                    if g < FH - 1:
                        i1.then_inc(s_pv, 1)
                    else:
                        filled(i0, "fo0")
                        filled(i1, "fo1")

            decay_row("GB1", gg, cprefix)
            decay_row("bB1", beta, ident)
            channel_banks(pre_w(pe, 3), hT, "gr", 0, [1])
            channel_banks(pre_w(pe, 4), hT, "gr", 2)
            w = pre_w(pe, 5)
            for half in range(2):
                channel_banks(w, hT, "gr", 4, [half])
                for i in (2 * half, 2 * half + 1):
                    pe.wait_ge(s_sq, i + 1)
                    sumsq("gs", ones, i, 2)
            w = pre_w(pe, 6)
            for tb in range(TB):
                token_bank(w, hT, f"z{tb}", tb)
            for tb in range(TB):
                pe.wait_ge(s_fo, tb + 1)
                b = into(pe, f"fT{tb}")
                for k in range(4):
                    ins = M.transpose(b[:, P * k:P * k + P], fo[:, tb, P * k:P * k + P], ident[:, :])
                filled(ins, f"fT{tb}")
            for i in range(4):
                evacuated(f"mT{i}")
            channel_banks(pre_w(pe, 7), mT, "kx", 0)
            def key_products(name, rhs):
                for tb in range(TB):
                    b = into(pe, f"{name}{tb}")
                    for h in range(GH):
                        ins = M.matmul(b[:, P * h:P * h + P], gk[:, h, P * tb:P * tb + P], rhs[:, h, P * tb:P * tb + P],
                                       start=True, stop=True)
                    filled(ins, f"{name}{tb}")

            pe.wait_ge(s_nrm, 8)
            key_products("kk", gk)
            pe.wait_ge(s_silu, 3)
            for tb in range(TB):
                for name, src in (("ktok", gk), ("vtok", gvT)):
                    b = into(pe, f"{name}{tb}")
                    for h in range(GH):
                        ins = M.transpose(b[:, P * h:P * h + P], src[:, h, P * tb:P * tb + P], ident[:, :])
                    filled(ins, f"{name}{tb}")
            key_products("qk", gq)
            for i in range(2):
                evacuated(f"kx{i}")
                sumsq("kxs", ones, i, 1)
            for tb in range(TB):
                pe.wait_ge(s_lvl, tb + 1)
                b = into(pe, f"X0_{tb}")
                for h in range(GH):
                    ins = M.transpose(b[:, P * h:P * h + P], ATl[0][:, tb, h, :], ident[:, :])
                filled(ins, f"X0_{tb}")
            channel_banks(pre_w(pe, 8), mT, "kx", 2)
            for i in range(2, 4):
                evacuated(f"kx{i}")
                sumsq("kxs", ones, i, 1)
            for n in range(1, len(LEVELS)):
                for tb in range(TB):
                    pe.wait_ge(s_lvl, 2 * n + tb + 1)
                    if n == 1:
                        pe.wait_ge(s_T0, tb + 1)
                        evacuated(f"X0_{tb}")
                    else:
                        evacuated(f"Y{n - 1}_{tb}")
                        evacuated(f"YT{n - 1}_{tb}")
                    b = into(pe, f"X{n}_{tb}")
                    for h in range(GH):
                        ins = M.matmul(b[:, P * h:P * h + P], ATl[n % 3][:, tb, h, :], Ti[:, tb, h, :], start=True, stop=True)
                    filled(ins, f"X{n}_{tb}")
                for tb in range(TB):
                    evacuated(f"X{n}_{tb}")
                    if n < len(LEVELS) - 1:
                        b = into(pe, f"Y{n}_{tb}")
                        for h in range(GH):
                            ins = M.matmul(b[:, P * h:P * h + P], TiT[:, tb, h, :], Xi[:, tb, h, :], start=True, stop=True)
                        filled(ins, f"Y{n}_{tb}")
                    b = into(pe, f"YT{n}_{tb}")
                    for h in range(GH):
                        ins = M.matmul(b[:, P * h:P * h + P], Xi[:, tb, h, :], TiT[:, tb, h, :], start=True, stop=True)
                    filled(ins, f"YT{n}_{tb}")
            for tb in range(TB):
                evacuated(f"YT{len(LEVELS) - 1}_{tb}")
            evacuated("ktok1")
            evacuated("vtok1")
            evacuated("vtok0")
            evacuated("qk1")
            evacuated("qk0")
            pe.wait_ge(s_kop, 4)
            for tb in range(TB):
                b = into(pe, f"w{tb}")
                for h in range(GH):
                    ins = M.matmul(b[:, P * h:P * h + P], kbn[:, tb, h, :], TiT[:, tb, h, :], start=True, stop=True)
                filled(ins, f"w{tb}")
            def values_part(c, tb, k0, k1):
                name = f"vx{2 * c + tb}"
                if k0 == 0:
                    into(pe, name)
                w = pre_w(pe, 9 if c == 0 else 12)
                b = ps[turn[name][0]]
                for k in range(k0, k1):
                    ins = M.matmul(b[:, :], mT[:, k, P * tb:P * tb + P], w[:, k, :], start=(k == 0), stop=(k == KD - 1))
                if k1 == KD:
                    filled(ins, name)

            go_b = {}
            for c in range(4):
                tb, r0 = c // 2, CHUNK * (c % 2)
                rows = slice(r0, r0 + CHUNK)
                if c == 1:
                    evacuated("w0")
                    evacuated("w1")
                if c:
                    evacuated(f"S{c - 1}")
                b = into(pe, f"vn{c}")
                for h in range(GH):
                    o = b[rows, P * h:P * h + P]
                    ins = M.matmul(o, TiT[:, tb, h, rows], vb[:, tb, h, :], start=True, stop=(c == 0))
                    if c:
                        ins = M.matmul(o, wTn[:, tb, h, rows], St[:, h, :], start=False, stop=True)
                filled(ins, f"vn{c}")
                values_part(0, c // 2, 4 * (c % 2), 4 * (c % 2) + 2)
                evacuated(f"vn{c}")
                if c < 3:
                    b = into(pe, f"S{c}")
                    for h in range(GH):
                        ins = M.matmul(b[:, P * h:P * h + P], kd[rows, tb, h, :], vnew[rows, tb, P * h:P * h + P], start=True, stop=True)
                    filled(ins, f"S{c}")
                if c % 2 == 0:
                    go_b[tb] = into(pe, f"go{tb}")
                for h in range(GH):
                    o = go_b[tb][rows, P * h:P * h + P]
                    if c:
                        M.matmul(o, qd[:, h, P * tb + r0:P * tb + r0 + CHUNK], St[:, h, :], start=True, stop=False)
                    ins = M.matmul(o, qkT[rows, tb, h, rows], vnew[rows, tb, P * h:P * h + P], start=(c == 0), stop=True)
                if c % 2:
                    filled(ins, f"go{tb}")
                else:
                    ins.then_inc(s_os, 1)
                values_part(0, c // 2, 4 * (c % 2) + 2, 4 * (c % 2) + 4)
            wo = []

            def output_part(i, half):
                c, tb = i // 2, i % 2
                if half == 0:
                    if tb == 0:
                        wo.append(pre_w(pe, 10 + c))
                    into(pe, f"wo{i}")
                b = ps[turn[f"wo{i}"][0]]
                for k in range(4 * half, 4 * half + 4):
                    ins = M.matmul(b[:, :], mixT[:, k, P * tb:P * tb + P], wo[c][:, k, :], start=(k == 0), stop=(k == KD - 1))
                if half:
                    filled(ins, f"wo{i}")

            evacuated("fT0")
            evacuated("fT1")
            output_part(0, 0)
            output_part(1, 0)
            for tb in range(TB):
                pe.wait_ge(s_go, tb + 1)
                b = into(pe, f"gT{tb}")
                for k in range(4):
                    ins = M.transpose(b[:, P * k:P * k + P], go[:, tb, P * k:P * k + P], ident[:, :])
                filled(ins, f"gT{tb}")
            output_part(2, 0)
            output_part(3, 0)
            for i in range(4):
                evacuated(f"gT{i % 2}")
                output_part(i, 1)
            values_part(1, 0, 0, KD)
            values_part(1, 1, 0, KD // 2)
            turn_rows(hn, "h2T", 5)
            for i in range(4):
                evacuated(f"h2T{i}")
            def query_sums(h):
                evacuated(f"qx{h}")
                b = into(pe, "qs") if h == 0 else ps[turn["qs"][0]]
                for tb in range(TB):
                    n = tb * XH + h
                    for c in range(2):
                        ins = M.matmul(b[:, n:n + 1], sq[:, 2 * (h % 2) + c, P * tb:P * tb + P], ones[:, 0:1],
                                       start=(c == 0), stop=(c == 1))
                if h < XH - 1:
                    ins.then_inc(s_qs, 1)
                else:
                    filled(ins, "qs")

            channel_banks(pre_w(pe, 13), hT, "qx")
            w = pre_w(pe, 14)
            channel_banks(w, hT, "qx", 2, [0])
            query_sums(0)
            query_sums(1)
            channel_banks(w, hT, "qx", 2, [1])
            def scores(h):
                evacuated(f"qx{h}")
                b = into(pe, f"xS{h}")
                for qb in range(2):
                    for c in range(2):
                        ins = M.matmul(b[:, T * qb:T * qb + T], qxT[:, 2 * h + c, P * qb:P * qb + P], kxT[:, 2 * h + c, :],
                                       start=(c == 0), stop=(c == 1))
                filled(ins, f"xS{h}")

            def turn_probs(h):
                pe.wait_ge(s_xp, h + 1)
                b = into(pe, f"xPT{h}")
                for mb in range(2):
                    for qb in range(2):
                        ins = M.transpose(b[:, T * mb + P * qb:T * mb + P * qb + P],
                                          xP[:, h, T * qb + P * mb:T * qb + P * mb + P], ident[:, :])
                filled(ins, f"xPT{h}")

            def weighted_values(h):
                evacuated(f"xPT{h}")
                b = into(pe, f"xO{h}")
                for c in range(2):
                    for mb in range(2):
                        ins = M.matmul(b[:, T * c:T * c + T], vx[:, mb, XD * h + P * c:XD * h + P * c + P],
                                       xPT[:, h % 2, T * mb:T * mb + T], start=(mb == 0), stop=(mb == 1))
                filled(ins, f"xO{h}")

            pe.wait_ge(s_nrm, 12)
            query_sums(2)
            scores(0)
            query_sums(3)
            scores(1)
            scores(2)
            values_part(1, 1, KD // 2, KD)
            turn_probs(0)
            scores(3)
            turn_probs(1)
            evacuated("vx2")
            evacuated("vx3")
            weighted_values(0)
            turn_probs(2)
            weighted_values(1)
            turn_probs(3)
            weighted_values(2)
            weighted_values(3)
            for g in range(XH):
                evacuated(f"xO{g}")
            w = pre_w(pe, 15)
            token_bank(w, mixT, "xo0", 0)
            token_bank(w, mixT, "xo1", 1)
            w = pre_w(pe, 16)
            token_bank(w, mixT, "xo2", 0)
            b = into(pe, "xo3")
            for k in range(KD):
                if k == KD // 2:
                    turn_rows(hn, "h3T", 7, range(2))
                ins = M.matmul(b[:, :], mixT[:, k, P:T], w[:, k, :], start=(k == 0), stop=(k == KD - 1))
            filled(ins, "xo3")
            def job_biases(src, banks=range(4)):
                for b in banks:
                    ins = M.matmul(ps[b][:, :], pairsel[:, :], src[:, WIDE * b:WIDE * b + WIDE], start=True, stop=False)
                return ins

            pe.wait_ge(s_par, 16 * 17)
            pe.wait_ge(s_bgu, 16)
            for tb in range(TB):
                if tb:
                    evacuated("xo0")
                    job_biases(bgu0, [0])
                    evacuated("xo1")
                    job_biases(bgu0, [1])
                    turn_rows(hn, "h3T", 7, range(2, 4))
                    evacuated("xo2")
                    job_biases(bgu0, [2])
                for i in (2 * tb, 2 * tb + 1):
                    evacuated(f"h3T{i}")
                b = into(pe, f"lg{tb}")
                for k in range(KD):
                    ins = M.matmul(b[:, 0:NE], hT[:, k, P * tb:P * tb + P], wr[:, k, :], start=(k == 0), stop=(k == KD - 1))
                filled(ins, f"lg{tb}")
            evacuated("xo3")
            job_biases(bgu0, [3]).then_inc(j_bias, 1)
            pe.wait_ge(s_sel, 1)
            b = into(pe, "rank0")
            filled(M.matmul(b[:, 0:NE], prefix[:, :], sel[:, 0, :], start=True, stop=True), "rank0")
            pe.wait_ge(s_sel, 2)
            b = into(pe, "rank1")
            M.matmul(b[:, 0:NE], ones[:, :], sel[:, 0, :], start=True, stop=False)
            filled(M.matmul(b[:, 0:NE], prefix[:, :], sel[:, 1, :], start=False, stop=True), "rank1")
            def turn_weights():
                pe.wait_ge(s_comb, 2)
                b = into(pe, "cT")
                for tb in range(TB):
                    ins = M.transpose(b[0:NE, P * tb:P * tb + P], comb[:, tb, :], ident[:, :])
                filled(ins, "cT")

            def down_biases(*banks):
                for i in banks:
                    b = into(pe, f"bd{i}")
                    filled(M.matmul(b[:, :], combT[:, P * (i % 2):P * (i % 2) + P], bdn[:, WIDE * (i // 2):WIDE * (i // 2) + WIDE],
                                    start=True, stop=True), f"bd{i}")

            rows_k = hn[:, :, :].rearrange("p t (d k) -> p t k d", k=KD)

            def gather(j, halves=range(2)):
                pe.wait_ge(j_sel, 8 * j + 4)
                for a in halves:
                    for q in range(4):
                        for tb in range(TB):
                            ins = M.matmul(ps[6 + a][:, P * q:P * q + P], rows_k[:, tb, 4 * a + q, :], Sel[:, tb, :],
                                           start=(tb == 0), stop=(tb == 1))
                    ins.then_inc(j_ga, 1)

            def scatter(n, banks):
                for tb in range(TB):
                    M.matmul(ps[banks[tb]][:, :], WT[:, tb, :], yS[:, n, :], start=True, stop=True).then_inc(j_sc, 1)

            def tiles(i, p, ms, k):
                w = []
                for m in ms:
                    s = slot_of(p, m)
                    before = pre_count[s] + fills_before(i, p, m)
                    pe.wait_ge(landed[s], 16 * (before + 1))
                    w.append(slot(s).rearrange("p (k n) -> p k n", k=k))
                return w

            def job(i, p, first=False, last=False):
                j = 2 * i + p
                if first:
                    pe.wait_ge(j_hg, 1)
                else:
                    pe.wait_ge(j_hg, 2 * j + 2)
                    pe.wait_ge(j_g, 2 * j)
                    pe.wait_ge(j_u, 2 * j)
                    pe.wait_ge(j_wt, j)
                    pe.wait_ge(s_bgu, 16 * j + 16)
                    job_biases(bgu).then_inc(j_bias, 1)
                for q in range(4):
                    if first and q == 1:
                        evacuated("h3T3")
                        gather(0, [1])
                        down_biases(1)
                    if first and q == 2:
                        pe.wait_ge(j_hg, 2)
                    w = tiles(i, p, (2 * q, 2 * q + 1), 2)
                    order = [(kk, b) for kk in range(2) for b in range(4)] if q < 3 else \
                            [(kk, b) for bs in ((0, 2), (1, 3)) for kk in range(2) for b in bs]
                    for kk, b in order:
                        k = 2 * q + kk
                        for a in range(2):
                            r = slice(SLOTS * a, SLOTS * a + SLOTS)
                            ins = M.matmul(ps[b][r, :], hgT[:, k, r], w[a][:, kk, WIDE * b:WIDE * b + WIDE],
                                           start=False, stop=(k == KD - 1))
                            if kk == 1 and b == 3:
                                ins.then_inc(spent[slot_of(p, 2 * q + a)], 1)
                            elif k == KD - 1 and b == 2 and a == 1:
                                ins.then_inc(j_gu, 1)
                if first:
                    down_biases(2, 3)
                    b = into(pe, "cnt")
                    M.matmul(b[:, 0:NE], ones[:, :], sel[:, 0, :], start=True, stop=False)
                    filled(M.matmul(b[:, 0:NE], ones[:, :], sel[:, 1, :], start=False, stop=True), "cnt")
                else:
                    pe.wait_ge(j_y, 2 * j)
                    for n in range(2):
                        scatter(n, ((6, 7), (4, 5))[n])
                pe.wait_ge(j_u, 2 * j + 1)
                pe.wait_ge(j_sel, 8 * j + 8)
                for tb in range(TB):
                    ins = M.transpose(ps[2][:, P * tb:P * tb + P], CW[:, tb, :], ident[:, :])
                ins.then_inc(j_ct, 1)
                for a in range(2):
                    pe.wait_ge(j_a, 2 * j + a + 1)
                    for k in range(4):
                        ins = M.transpose(ps[a][:, P * k:P * k + P], aS[:, a, P * k:P * k + P], ident[:, :])
                    ins.then_inc(j_T, 1)
                pe.wait_ge(j_aT, 2 * j + 2)
                if first:
                    for b in range(2):
                        evacuated(f"bd{2 + b}")
                else:
                    pe.wait_ge(j_add, 4 * j)
                for q in range(2):
                    w = tiles(i, p, (8 + 2 * q, 9 + 2 * q), 4)
                    order = [(kk, b) for kk in range(4) for b in range(2)] if q == 0 else \
                            [(kk, b) for b in range(2) for kk in range(4)]
                    for kk, b in order:
                        k = 4 * q + kk
                        for a in range(2):
                            r = slice(SLOTS * a, SLOTS * a + SLOTS)
                            ins = M.matmul(ps[4 + b][r, :], actT[:, k, r], w[a][:, kk, WIDE * b:WIDE * b + WIDE],
                                           start=(k == 0), stop=(k == KF - 1))
                            if kk == 3 and b == 1:
                                ins.then_inc(spent[slot_of(p, 8 + 2 * q + a)], 1)
                            elif k == KF - 1 and b == 0 and a == 1:
                                ins.then_inc(j_D, 1)
                    if q == 0 and not last:
                        if first:
                            evacuated("cnt")
                        gather(j + 1)
                if last:
                    pe.wait_ge(j_wt, j + 1)
                    for n in range(2):
                        pe.wait_ge(j_y, 2 * j + n + 1)
                        scatter(n, ((6, 7), (0, 1))[n])

            def jobs(i0, i1):
                with pe.Fori(i0, i1) as i:
                    job(i, 1)
                    job(i + 1, 0)

            turn_weights()
            evacuated("h3T2")
            gather(0, [0])
            pe.wait_ge(s_bdn, 16)
            evacuated("cT")
            down_biases(0)
            job(0, 0, first=True)
            jobs(0, PAIRS // 2 - 1)
            pe.wait_ge(s_flag, 1)
            more = pe.value_load(flag[0:1, 0:1], min_val=0, max_val=1)
            with pe.If(more > 0):
                jobs(PAIRS // 2 - 1, ROUNDS * PAIRS // 2 - 1)
                job(ROUNDS * PAIRS // 2 - 1, 1, last=True)
            with pe.Else():
                job(PAIRS // 2 - 1, 1, last=True)


_INS = ["x", "mem", "mix_norm", "w_in", "b_forget", "fox_q_gain", "fox_k_gain", "fox_out_gain",
        "gdn_conv_w", "gdn_a_log", "gdn_dt_bias", "gdn_out_gain", "w_out",
        "xattn_norm", "mem_norm", "w_xq", "w_xkv", "xq_gain", "xk_gain", "w_xo",
        "moe_norm", "w_router", "b_router", "w_gate_up", "b_gate_up", "w_down", "b_down"]


def kernel(**inputs):
    import numpy as _np
    import concourse.bacc as _bacc
    from concourse import mybir as _mybir
    from concourse.bass_utils import run_bass_kernel_spmd as _run

    nc = _bacc.Bacc("TRN2", target_bir_lowering=False, num_devices=1)
    arrays, args = {}, []
    for name in _INS:
        a = _np.ascontiguousarray(inputs[name])
        arrays[f"in_{name}_dram"] = a
        args.append(nc.dram_tensor(f"in_{name}_dram", a.shape, _mybir.dt.from_np(a.dtype), kind="ExternalInput").ap())
    o = nc.dram_tensor("out_0_dram", (1, T, D), F32, kind="ExternalOutput").ap()
    layer_kernel(nc, *args, o)
    r = _run(nc, [arrays], core_ids=[0])
    return r.results[0]["out_0_dram"]
```
